# Optimizing a Trainium2 kernel written in Bass

```python
import jax, jax.numpy as jnp
from jax import lax
import numpy as np

D_MODEL = 1024
BATCH = 1
SEQ = 512
DEPTH = 2

GRID_W = 64
CTX_LEN = 256
N_MIXERS = 2
N_SUB = 3
N_MOD = 3
D_FF = 2816
RMS_EPS = 1e-6
D_RNN = 1024
RG_BLOCKS = 8
RG_BW = D_RNN // RG_BLOCKS
CONV_W = 4
CONV_PAD_L = 2
CONV_PAD_R = CONV_W - 1 - CONV_PAD_L
RG_C = 8.0
MLA_HEADS = 8
Q_LORA = 512
KV_LORA = 256
NOPE = 128
ROPE = 64
V_DIM = 128
ROPE_BASE = 10000.0
Q_BLOCK = 128
ATTN_SCALE = (NOPE + ROPE) ** -0.5

kernel_name = "hybrid_rglru_mla_macaron_dit"

def rms_norm(x, g):
    xf = x.astype(jnp.float32)
    y = xf * lax.rsqrt(jnp.mean(xf * xf, axis=-1, keepdims=True) + RMS_EPS)
    return (y * g.astype(jnp.float32)).astype(x.dtype)

def modulate_in(x, g, m):
    return rms_norm(x, g) * (1 + m[:, None, 1]) + m[:, None, 0]

def gated_residual(x, y, g, m, weight):
    return x + weight * m[:, None, 2] * rms_norm(y, g)

def swiglu(h, w_in, w_out):
    a, b = jnp.split(h @ w_in, 2, axis=-1)
    return (jax.nn.silu(a) * b) @ w_out

def half_ffn_sublayer(x, m, g_pre, g_post, w_in, w_out):
    return gated_residual(x, swiglu(modulate_in(x, g_pre, m), w_in, w_out), g_post, m, 0.5)

def centred_dwconv(u, w, b):
    L = u.shape[1]
    up = jnp.pad(u, ((0, 0), (CONV_PAD_L, CONV_PAD_R), (0, 0)))
    out = b
    for k in range(CONV_W):
        out = out + up[:, k:k + L] * w[k]
    return out

def rglru_coeffs(u, gate_w, gate_b, lam):
    B, L, _ = u.shape
    ub = u.reshape(B, L, RG_BLOCKS, RG_BW)
    g = jnp.einsum("blnj,gnjk->gblnk", ub, gate_w.astype(jnp.float32)).reshape(2, B, L, D_RNN)
    g = jax.nn.sigmoid(g + gate_b.astype(jnp.float32)[:, None, None, :])
    r, i = g[0], g[1]
    log_a = -RG_C * r * jax.nn.softplus(-lam.astype(jnp.float32))
    a = jnp.exp(log_a)
    return a, jnp.sqrt(-jnp.expm1(2.0 * log_a)) * (i * u)

def linear_scan(a, b, h0, reverse):
    first = a.shape[1] - 1 if reverse else 0
    b = b.at[:, first].add(a[:, first] * h0)

    def combine(e1, e2):
        a1, b1 = e1
        a2, b2 = e2
        return a1 * a2, a2 * b1 + b2

    _, h = lax.associative_scan(combine, (a, b), reverse=reverse, axis=1)
    return h

def rglru_mixer(hc, hl, params, need_ctx):
    w_in, conv_w, conv_b, gate_w, gate_b, lam, w_out = params

    def branches(h):
        y, u = jnp.split(h @ w_in, 2, axis=-1)
        return jax.nn.gelu(y), centred_dwconv(u, conv_w, conv_b).astype(jnp.float32)

    yc, uc = branches(hc)
    yl, ul = branches(hl)
    h0 = jnp.zeros((hc.shape[0], D_RNN), jnp.float32)
    ctx_dirs, lat_dirs = [], []
    for d, reverse in enumerate((False, True)):
        a_c, b_c = rglru_coeffs(uc, gate_w[d], gate_b[d], lam[d])
        h_c = linear_scan(a_c, b_c, h0, reverse)
        h_last = h_c[:, 0] if reverse else h_c[:, -1]
        a_l, b_l = rglru_coeffs(ul, gate_w[d], gate_b[d], lam[d])
        lat_dirs.append(linear_scan(a_l, b_l, h_last, reverse))
        ctx_dirs.append(h_c)
    out_l = ((lat_dirs[0] + lat_dirs[1]).astype(hl.dtype) * yl) @ w_out
    out_c = None
    if need_ctx:
        out_c = ((ctx_dirs[0] + ctx_dirs[1]).astype(hc.dtype) * yc) @ w_out
    return out_c, out_l

def axial_rope(t, rows, cols):
    half = ROPE // 2
    quarter = half // 2
    inv_freq = ROPE_BASE ** (-jnp.arange(quarter, dtype=jnp.float32) / quarter)
    tf = t.astype(jnp.float32)
    bshape = (1, t.shape[1]) + (1,) * (t.ndim - 3) + (quarter,)

    def rot(v, pos):
        ang = (pos.astype(jnp.float32)[:, None] * inv_freq).reshape(bshape)
        cos, sin = jnp.cos(ang), jnp.sin(ang)
        v1, v2 = v[..., :quarter], v[..., quarter:]
        return jnp.concatenate([v1 * cos - v2 * sin, v1 * sin + v2 * cos], axis=-1)

    return jnp.concatenate([rot(tf[..., :half], rows), rot(tf[..., half:], cols)], axis=-1).astype(t.dtype)

def mla_project(h, w_a, q_norm, kv_norm, w_qb, w_kvb):
    B, L, _ = h.shape
    c_q, c_kv, k_rope = jnp.split(h @ w_a, [Q_LORA, Q_LORA + KV_LORA], axis=-1)
    q = (rms_norm(c_q, q_norm) @ w_qb).reshape(B, L, MLA_HEADS, NOPE + ROPE)
    kv = (rms_norm(c_kv, kv_norm) @ w_kvb).reshape(B, L, MLA_HEADS, NOPE + V_DIM)
    return q[..., :NOPE], q[..., NOPE:], kv[..., :NOPE], k_rope, kv[..., NOPE:]

def mla_attention(q_nope, q_rope, k_nope, k_rope, v):
    B, L, H, _ = q_nope.shape
    nb = L // Q_BLOCK

    def to_blocks(q):
        return q.reshape(B, nb, Q_BLOCK, H, q.shape[-1]).swapaxes(0, 1)

    def attend(blk):
        qn, qr = blk
        s = (jnp.einsum("bqhd,bkhd->bhqk", qn, k_nope, preferred_element_type=jnp.float32)
             + jnp.einsum("bqhr,bkr->bhqk", qr, k_rope, preferred_element_type=jnp.float32)) * ATTN_SCALE
        p = jax.nn.softmax(s, axis=-1).astype(v.dtype)
        return jnp.einsum("bhqk,bkhd->bqhd", p, v)

    o = lax.map(attend, (to_blocks(q_nope), to_blocks(q_rope)))
    return o.swapaxes(0, 1).reshape(B, L, H * V_DIM)

def mla_mixer(hc, hl, params, need_ctx):
    w_a, q_norm, kv_norm, w_qb, w_kvb, w_o = params
    L = hl.shape[1]
    n_rows = L // GRID_W
    rows = jnp.repeat(jnp.arange(n_rows, dtype=jnp.int32), GRID_W)
    cols = jnp.tile(jnp.arange(GRID_W, dtype=jnp.int32), n_rows)
    qn_l, qr_l, kn_l, kr_l, v_l = mla_project(hl, w_a, q_norm, kv_norm, w_qb, w_kvb)
    qr_l = axial_rope(qr_l, rows, cols)
    kr_l = axial_rope(kr_l, rows, cols)
    qn_c, qr_c, kn_c, kr_c, v_c = mla_project(hc, w_a, q_norm, kv_norm, w_qb, w_kvb)
    out_l = mla_attention(qn_l, qr_l,
                          jnp.concatenate([kn_c, kn_l], axis=1),
                          jnp.concatenate([kr_c, kr_l], axis=1),
                          jnp.concatenate([v_c, v_l], axis=1)) @ w_o
    out_c = None
    if need_ctx:
        out_c = mla_attention(qn_c, qr_c, kn_c, kr_c, v_c) @ w_o
    return out_c, out_l

def hybrid_layer(xc, xl, mod_c, mod_l, norm_g, ffn_w_in, ffn_w_out, mixer, mixer_params, last):
    xc = half_ffn_sublayer(xc, mod_c[:, 0], norm_g[0], norm_g[1], ffn_w_in[0], ffn_w_out[0])
    xl = half_ffn_sublayer(xl, mod_l[:, 0], norm_g[0], norm_g[1], ffn_w_in[0], ffn_w_out[0])
    out_c, out_l = mixer(modulate_in(xc, norm_g[2], mod_c[:, 1]),
                         modulate_in(xl, norm_g[2], mod_l[:, 1]), mixer_params, not last)
    xl = gated_residual(xl, out_l, norm_g[3], mod_l[:, 1], 1.0)
    xl = half_ffn_sublayer(xl, mod_l[:, 2], norm_g[4], norm_g[5], ffn_w_in[1], ffn_w_out[1])
    if not last:
        xc = gated_residual(xc, out_c, norm_g[3], mod_c[:, 1], 1.0)
        xc = half_ffn_sublayer(xc, mod_c[:, 2], norm_g[4], norm_g[5], ffn_w_in[1], ffn_w_out[1])
    return xc, xl

def setup_inputs(seed: int = 0) -> dict:
    key = jax.random.key(seed)
    ks = iter(jax.random.split(key, 64))

    def nrm(shape, scale):
        return jax.random.normal(next(ks), shape, jnp.float32) * scale

    d = D_MODEL
    inp = {
        "x": nrm((BATCH, SEQ, d), 1.0),
        "c": nrm((BATCH, d), 1.0),
        "ctx": nrm((BATCH, CTX_LEN, d), 1.0),
        "c_ctx": nrm((d,), 1.0),
    }
    for i in range(DEPTH):
        p = "l%d_" % i
        inp[p + "mod_w"] = nrm((d, N_SUB * N_MOD * d), 0.5 * d ** -0.5)
        inp[p + "mod_b"] = nrm((N_SUB * N_MOD * d,), 0.02)
        inp[p + "norm_g"] = 1.0 + nrm((2 * N_SUB, d), 0.05)
        inp[p + "ffn_w_in"] = nrm((2, d, 2 * D_FF), d ** -0.5)
        inp[p + "ffn_w_out"] = nrm((2, D_FF, d), D_FF ** -0.5)
        if i % N_MIXERS == 0:
            inp[p + "rg_w_in"] = nrm((d, 2 * D_RNN), d ** -0.5)
            inp[p + "rg_conv_w"] = nrm((CONV_W, D_RNN), CONV_W ** -0.5)
            inp[p + "rg_conv_b"] = nrm((D_RNN,), 0.02)
            inp[p + "rg_gate_w"] = nrm((2, 2, RG_BLOCKS, RG_BW, RG_BW), RG_BW ** -0.5)
            inp[p + "rg_gate_b"] = nrm((2, 2, D_RNN), 0.1)
            a_c = jax.random.uniform(next(ks), (2, D_RNN), jnp.float32, minval=0.9, maxval=0.999)
            a0 = a_c ** (1.0 / RG_C)
            inp[p + "rg_lambda"] = jnp.log(a0) - jnp.log1p(-a0)
            inp[p + "rg_w_out"] = nrm((D_RNN, d), D_RNN ** -0.5)
        else:
            inp[p + "mla_w_a"] = nrm((d, Q_LORA + KV_LORA + ROPE), d ** -0.5)
            inp[p + "mla_q_norm"] = 1.0 + nrm((Q_LORA,), 0.05)
            inp[p + "mla_kv_norm"] = 1.0 + nrm((KV_LORA,), 0.05)
            inp[p + "mla_w_qb"] = nrm((Q_LORA, MLA_HEADS * (NOPE + ROPE)), Q_LORA ** -0.5)
            inp[p + "mla_w_kvb"] = nrm((KV_LORA, MLA_HEADS * (NOPE + V_DIM)), KV_LORA ** -0.5)
            inp[p + "mla_w_o"] = nrm((MLA_HEADS * V_DIM, d), (MLA_HEADS * V_DIM) ** -0.5)
    return inp

def reference(x, c, ctx, c_ctx,
              l0_mod_w, l0_mod_b, l0_norm_g, l0_ffn_w_in, l0_ffn_w_out,
              l0_rg_w_in, l0_rg_conv_w, l0_rg_conv_b, l0_rg_gate_w, l0_rg_gate_b, l0_rg_lambda, l0_rg_w_out,
              l1_mod_w, l1_mod_b, l1_norm_g, l1_ffn_w_in, l1_ffn_w_out,
              l1_mla_w_a, l1_mla_q_norm, l1_mla_kv_norm, l1_mla_w_qb, l1_mla_w_kvb, l1_mla_w_o):
    layers = (
        (l0_mod_w, l0_mod_b, l0_norm_g, l0_ffn_w_in, l0_ffn_w_out,
         (l0_rg_w_in, l0_rg_conv_w, l0_rg_conv_b, l0_rg_gate_w, l0_rg_gate_b, l0_rg_lambda, l0_rg_w_out)),
        (l1_mod_w, l1_mod_b, l1_norm_g, l1_ffn_w_in, l1_ffn_w_out,
         (l1_mla_w_a, l1_mla_q_norm, l1_mla_kv_norm, l1_mla_w_qb, l1_mla_w_kvb, l1_mla_w_o)),
    )
    mixers = (rglru_mixer, mla_mixer)
    xc, xl = ctx, x
    for i in range(DEPTH):
        mod_w, mod_b, norm_g, ffn_w_in, ffn_w_out, mixer_params = layers[i]
        mod_l = (jax.nn.silu(c) @ mod_w + mod_b).reshape(c.shape[0], N_SUB, N_MOD, -1)
        mod_c = (jax.nn.silu(c_ctx) @ mod_w + mod_b).reshape(1, N_SUB, N_MOD, -1)
        xc, xl = hybrid_layer(xc, xl, mod_c, mod_l, norm_g, ffn_w_in, ffn_w_out,
                              mixers[i % N_MIXERS], mixer_params, i == DEPTH - 1)
    return xl


_drawn_inputs = setup_inputs


def setup_inputs(seed=0):
    import zlib

    import numpy as np

    out = dict(_drawn_inputs(seed))
    spreads = {}
    factors = {'l0_rg_conv_b': 2.705,
     'l0_rg_gate_b': 6.062,
     'l1_mla_q_norm': 8.0,
     'l1_mla_kv_norm': 3.979}
    for name, (base, spread) in spreads.items():
        noise = np.random.default_rng([zlib.crc32(name.encode()), seed]).standard_normal(out[name].shape)
        drawn = base * np.exp(spread * noise) if base else spread * noise
        out[name] = __import__('jax').numpy.asarray(drawn.astype(out[name].dtype))
    for name, factor in factors.items():
        out[name] = (out[name] * factor).astype(out[name].dtype)
    return out
```

```python
import numpy as np
import concourse.bass as bass
from concourse import mybir
from contextlib import ExitStack

F32 = mybir.dt.float32
F32R = mybir.dt.float32r
ALU = mybir.AluOpType
ACT = mybir.ActivationFunctionType
AX = mybir.AxisListType

P = 128
D = 1024
KT = D // P
CTX, LAT = 256, 512
TOK = CTX + LAT
DFF = 2816
FT = DFF // P
CHUNKS = (8, 8, FT - 16)
HALVES = ((0, TOK // 2), (TOK // 2, TOK))
LATENT = ((CTX, TOK),)
EPS = 1e-6
NSLOT = 4
NRAW = 4
MOD_W = 512
MOD_CHUNKS = 2 * 9 * D // MOD_W
MOD_FIRST = 4
HEADS = 8
NOPE, ROPE, VD = 128, 64, 128
QL, KVL = 512, 256
QKD = NOPE + ROPE
SCALE = float(QKD) ** -0.5
QT = LAT // P
CKT = TOK // P
RG_C = 8.0
CONV = 4

VEC = {}
_at = 0
for _name, _n in (("cond", 16), ("norm_g", 96), ("mod_b", 144), ("conv_w", 32), ("conv_b", 8), ("gate_b", 32),
                  ("lam", 16), ("q_norm", 4), ("kv_norm", 2)):
    VEC[_name] = _at
    _at += _n
NVEC = _at


class Stage:

    def __init__(self, kind, layer, sub, halves, group0, in0, out0, mod0):
        self.kind, self.layer, self.sub, self.halves = kind, layer, sub, halves
        self.group0, self.in0, self.out0, self.mod0 = group0, in0, out0, mod0
        self.nh = len(halves)


def plan():
    stages, g, i, o, mod = [], 0, 0, 0, MOD_FIRST
    for kind, layer, sub, halves in (("ffn", 0, 0, HALVES), ("rg", 0, 1, HALVES), ("ffn", 0, 2, HALVES),
                                     ("ffn", 1, 0, HALVES), ("mla", 1, 1, LATENT), ("ffn", 1, 2, LATENT)):
        stages.append(Stage(kind, layer, sub, halves, g, i, o, mod))
        nh = len(halves)
        if kind == "ffn":
            g += FT // 2 + 2 * len(CHUNKS)
            i += FT * nh
            o += KT * nh * len(CHUNKS)
            if layer == 0:
                mod += 16
        elif kind == "rg":
            g += KT // 2 + 1 + 2
            i += KT * nh
            o += KT * nh
        else:
            g += 2 + HEADS // 2 + 2
            o += KT * nh
    return stages, g


STAGES, GROUPS = plan()


class Tail:

    def __init__(self, n, stage, pre, squares, stats, posts, pres):
        self.n, self.stage, self.pre = n, stage, pre
        two = stage is None or stage.nh == 2
        self.halves = HALVES if two else LATENT
        if stage is None:
            self.order = [("pre", 0), ("pre", 1)]
        else:
            nh = stage.nh
            e = [("E", h, 4 * g + q) for g in range(2) for h in range(nh) for q in range(4)]
            if nh == 2:
                self.order = e[:12] + [("post", 0)] + e[12:14] + [("pre", 0)] + e[14:] + [("post", 1), ("pre", 1)]
            else:
                self.order = e + [("post", 0), ("pre", 0)]
            if not pre:
                self.order = [x for x in self.order if x[0] != "pre"]
        self.square, self.stat, self.post, self.pre_no = {}, {}, {}, {}
        for x in self.order:
            if x[0] == "E":
                squares += 1
                self.square[x] = squares
            elif x[0] == "post":
                stats += 1
                self.stat[x] = stats
                self.post[x[1]] = posts
                posts += 1
                if pre:
                    for m in range(KT):
                        squares += 1
                        self.square[("post", x[1], m)] = squares
            else:
                if stage is None:
                    for m in range(KT):
                        squares += 1
                        self.square[("post", x[1], m)] = squares
                stats += 1
                self.stat[x] = stats
                self.pre_no[x[1]] = pres
                pres += 1
        self.end = squares, stats, posts, pres


def tails():
    out = [Tail(0, None, True, 0, 0, 0, 0)]
    for n, s in enumerate(STAGES):
        out.append(Tail(n + 1, s, n < len(STAGES) - 1, *out[-1].end))
    return out


TAILS = tails()
MLA_TAIL = 5


def segments(c0, c1):
    out = []
    if c0 < CTX:
        out.append((1, c0, min(c1, CTX)))
    if c1 > CTX:
        out.append((0, max(c0, CTX), c1))
    return out


def build(nc, io):
    ctx = ExitStack()
    with ctx:
        KB = 1024
        X_AT, H_AT, G_AT, Y_AT = 0, 24 * KB, 72 * KB, 120 * KB
        W_AT, RAW_AT, MISC_AT = 144 * KB, 176 * KB, 192 * KB
        base = ((nc.sbuf_base + 63) // 64) * 64

        def at(name, offset, shape, dt=F32):
            return nc.alloc_sbuf_tensor_at(name, [P, *shape], dt, offset=base + offset)

        def sem(name):
            return ctx.enter_context(nc.semaphore(name))

        x_res = at("x_res", X_AT, [KT, TOK])
        h_in = at("h_in", H_AT, [2, KT, TOK], F32R)
        g_act = at("g_act", G_AT, [2, KT, TOK], F32R)
        y_acc = at("y_acc", Y_AT, [KT, TOK])
        w_slot = at("w_slot", W_AT, [NSLOT, 2, KT, P], F32R)
        raw = at("raw", RAW_AT, [NSLOT, KT, P])
        mod_raw = at("mod_raw", MISC_AT, [2, 2, MOD_W])
        mod_acc = at("mod_acc", MISC_AT + 8 * KB, [2, MOD_W])
        act_tmp = at("act_tmp", MISC_AT + 12 * KB, [2, 512])
        dve_tmp = at("dve_tmp", MISC_AT + 16 * KB, [2, 512])
        sum_sq = at("sum_sq", MISC_AT + 20 * KB, [TOK])
        rstd = at("rstd", MISC_AT + 23 * KB, [512])
        small_at = [MISC_AT + 25 * KB]

        def small(name, *shape):
            offset = small_at[0]
            small_at[0] += (4 * int(np.prod(shape)) + 31) // 32 * 32
            return at(name, offset, shape)

        vecs = small("vecs", NVEC)
        mods = small("mods", 2, 2 * 72)
        cond = small("cond", 16)
        post_gain = small("post_gain", 2, KT)
        pre_gain = small("pre_gain", 2, KT)
        decay = small("decay", 2, 16)
        eps_col = small("eps_col", 1)
        soft_max = small("soft_max", 2, 4)
        soft = small("soft", 6, 16)
        ones = small("ones", P)
        ident = small("ident", P)
        assert base + small_at[0] <= nc.sbuf_usable_end

        mod_first = [at("mod_first", G_AT, [3, KT, MOD_W])[:, n] for n in range(3)] + [
            at("mod_fourth", Y_AT, [1, KT, MOD_W])[:, 0]]

        rg_yu = at("rg_yu", G_AT, [2, KT, TOK])
        rg_uc = at("rg_uc", Y_AT, [KT, TOK])
        rg_m = g_act
        rg_split = at("rg_split", H_AT, [2, 2, TOK], F32R)
        rg_work = at("rg_work", H_AT + 12 * KB, [2, 2, 3, TOK])

        cq_raw = at("cq_raw", G_AT + 16 * KB, [4, LAT])
        ckv_raw = at("ckv_raw", G_AT + 24 * KB, [2, TOK])
        kr_raw = at("kr_raw", G_AT + 30 * KB, [TOK])
        kr_swap = at("kr_swap", G_AT + 33 * KB, [LAT])
        mla_sq = at("mla_sq", G_AT + 35 * KB, [2, LAT])
        cq_n = at("cq_n", G_AT, [2, 4, LAT], F32R)
        att_o = at("att_o", G_AT + 16 * KB, [2, HEADS, LAT], F32R)
        ckv_n = at("ckv_n", Y_AT, [2, 2, TOK], F32R)
        kr_n = at("kr_n", Y_AT + 12 * KB, [2, TOK], F32R)
        k_head = [at("k_head0", Y_AT + 18 * KB, [2, TOK], F32R), at("k_head1", H_AT + 40 * KB, [2, TOK], F32R)]
        v_pair = at("v_pair", H_AT, [2, CKT, 2 * VD], F32R)
        p_turned = at("p_turned", H_AT + 12 * KB, [2, CKT, LAT], F32R)
        q_head = [[at("q_head0h", H_AT + 36 * KB, [LAT], F32R), at("q_head0l", H_AT + 38 * KB, [LAT], F32R)],
                  [at("q_head1h", H_AT + 46 * KB, [LAT], F32R), at("q_head1l", MISC_AT + 18 * KB, [LAT], F32R)]]
        p_soft = at("p_soft", MISC_AT + 12 * KB, [2, TOK])
        cos_t = at("cos_t", MISC_AT, [LAT])
        sin_t = at("sin_t", MISC_AT + 2 * KB, [LAT])
        qr_pair = at("qr_pair", MISC_AT + 4 * KB, [2, LAT], F32R)
        rot_tmp = at("rot_tmp", MISC_AT + 8 * KB, [2, LAT])

        ps = ctx.enter_context(nc.psum_tensor("ps", [P, 8, 512], F32))
        STAT, MODB = 7, 7

        vec_in = sem("vec_in")
        x_in = sem("x_in")
        mod0_in = [sem(f"mod0_in{n}") for n in range(4)]
        raw_in = [sem(f"raw_in{n}") for n in range(NSLOT)]
        w_hi = sem("w_hi")
        w_lo = sem("w_lo")
        modp_in = [sem(f"modp_in{n}") for n in range(2)]
        modp_free = sem("modp_free")
        mod_step = sem("mod_step")
        mod_sum = sem("mod_sum")
        mod_done = sem("mod_done")
        consts = sem("consts")
        mod_sum0 = sem("mod_sum0")
        cond_done = sem("cond_done")
        in_ready = sem("in_ready")
        pair_act = sem("pair_act")
        in_free = sem("in_free")
        g_hi = sem("g_hi")
        g_free = sem("g_free")
        out_ready = sem("out_ready")
        out_free = sem("out_free")
        sq_done = sem("sq_done")
        ss_added = sem("ss_added")
        ss_zero = sem("ss_zero")
        stat_ready = sem("stat_ready")
        ln_done = sem("ln_done")
        rs_ready = sem("rs_ready")
        gain_done = sem("gain_done")
        y_normed = sem("y_normed")
        x_upd = sem("x_upd")
        x_normed = sem("x_normed")
        h_f32 = sem("h_f32")
        h_hi = sem("h_hi")
        h_lo = sem("h_lo")
        soft_step = sem("soft_step")
        soft_exp = sem("soft_exp")
        conv_step = sem("conv_step")
        uc_hi, uc_lo = sem("uc_hi"), sem("uc_lo")
        gate_ready = sem("gate_ready")
        sig_done = sem("sig_done")
        expd = sem("expd")
        coef_done = sem("coef_done")
        iu_done = sem("iu_done")
        rg_step = sem("rg_step")
        m_hi, m_lo = sem("m_hi"), sem("m_lo")
        rope_in = sem("rope_in")
        lat_ready = sem("lat_ready")
        lat_read = sem("lat_read")
        lat_sq, lat_step = sem("lat_sq"), sem("lat_step")
        lat_sum, lat_ln, lat_rs = sem("lat_sum"), sem("lat_ln"), sem("lat_rs")
        lat_hi, lat_lo = sem("lat_hi"), sem("lat_lo")
        kr_step = sem("kr_step")
        prj_ready, prj_hi, prj_free = sem("prj_ready"), sem("prj_hi"), sem("prj_free")
        qr_step = sem("qr_step")
        s_ready, s_max, s_exp, p_ready = sem("s_ready"), sem("s_max"), sem("s_exp"), sem("p_ready")
        p_rcp = sem("p_rcp")
        t_ready, t_hi, t_free = sem("t_ready"), sem("t_hi"), sem("t_free")
        o_ready, o_hi, o_free = sem("o_ready"), sem("o_hi"), sem("o_free")
        out_sent = sem("out_sent")

        units, mod_pieces, mod_start, x_t, vec_d, rope_d, out_d = io
        block = ctx.enter_context(nc.Block())

        def mod_at(layer, sub, what):
            return layer * 72 + (sub * 3 + what) * KT

        def gain_at(layer, row):
            return VEC["norm_g"] + (layer * 6 + row) * KT

        def wait_pos(eng, s, value):
            if value > 0:
                eng.wait_ge(s, value)

        def phases(st):
            if st.kind == "ffn":
                out, g, i, o = [], st.group0, st.in0, st.out0
                for c, tiles in enumerate(CHUNKS):
                    out.append(("in", c, g, tiles // 2, i))
                    g += tiles // 2
                    i += tiles * st.nh
                    out.append(("out", c, g, 2, o))
                    g += 2
                    o += KT * st.nh
                return out
            if st.kind == "rg":
                g = st.group0
                return [("in", 0, g, KT // 2, st.in0), ("gates", 0, g + KT // 2, 1, 0),
                        ("out", 0, g + KT // 2 + 1, 2, st.out0)]
            g = st.group0
            return [("latent", 0, g, 2, 0), ("heads", 0, g + 2, HEADS // 2, 0),
                    ("out", 0, g + 2 + HEADS // 2, 2, st.out0)]

        def last_out(st):
            return phases(st)[-1]

        def has_mods(st, ph):
            return st.kind == "ffn" and st.layer == 0 and ph[0] == "in" and ph[1] < 2

        def mod_chunk0(st, ph):
            return st.mod0 - MOD_FIRST + 8 * ph[1]

        BANKS = {2: (4, 5, 6, 4, 5, 6, 4, 5), 1: (4, 5, 6, 5)}
        BACK = {2: (2, 2, 3, 3, 3, 3, 3, 3), 1: (3, 2, 3, 2)}

        CONV_STEPS, RG_STEPS = 7, 9

        def out_item(st, x):
            _, h, m = x
            return last_out(st)[4] + (m // 4) * 4 * st.nh + 4 * h + m % 4

        def latent_norms():
            out = []
            for h in range(2):
                c0, c1 = HALVES[h]
                out.append(([(ckv_raw[:, t, c0:c1], 3 * h + t + 1) for t in range(2)], VEC["kv_norm"], c1 - c0, KVL))
            out.append(([(cq_raw[:, t], 7 + t + 1) for t in range(4)], VEC["q_norm"], LAT, QL))
            return out

        def rg_pool(m, split_lo, g):
            pool = nc.gpsimd
            if m == 0:
                rg_split_lo(0)
            if m + 1 < KT:
                rg_split_lo(m + 1)
            for d in range(2):
                pool.wait_ge(sig_done, 2 * m + d + 1)
                gate = rg_work[:, m % 2, d, 1]
                pool.tensor_tensor(gate, gate, rg_uc[:, m], ALU.mult).then_inc(iu_done, 1)
            if m % 2 == 1:
                split_lo(g + 1, m // 2)
            pool.wait_ge(m_hi, m + 1)
            pool.tensor_tensor(rg_m[:, 1, m], rg_work[:, m % 2, 0, 0], rg_m[:, 0, m].bitcast(F32),
                               ALU.subtract).then_inc(m_lo, 1)

        def rg_split_lo(m):
            pool = nc.gpsimd
            pool.wait_ge(uc_hi, m + 1)
            pool.tensor_tensor(rg_split[:, m % 2, 1], rg_uc[:, m], rg_split[:, m % 2, 0].bitcast(F32),
                               ALU.subtract).then_inc(uc_lo, 1)

        def latent_splits():
            out = []
            for h in range(2):
                c0, c1 = HALVES[h]
                for t in range(2):
                    out.append((ckv_n[:, :, t, c0:c1], ckv_raw[:, t, c0:c1]))
            for t in range(4):
                out.append((cq_n[:, :, t], cq_raw[:, t]))
            return out

        def mla_latent_pool(split_lo, g):
            pool = nc.gpsimd
            for q in range(NSLOT):
                split_lo(g + 1, q)
            pool.wait_ge(lat_hi, 1)
            pool.tensor_tensor(kr_n[:, 1], kr_raw[:], kr_n[:, 0].bitcast(F32), ALU.subtract).then_inc(lat_lo, 1)
            for n, (dst, src) in enumerate(latent_splits()):
                if n == 4:
                    for q in range(NSLOT):
                        split_lo(g + 2, q)
                pool.wait_ge(lat_hi, n + 2)
                pool.tensor_tensor(dst[:, 1], src, dst[:, 0].bitcast(F32), ALU.subtract).then_inc(lat_lo, 1)

        @block.sync
        def _(sp):
            sp.dma_start(vecs[:], vec_d).then_inc(vec_in, 16)
            sp.dma_start(x_res[:], x_t).then_inc(x_in, 16)
            for c in range(MOD_FIRST):
                sp.dma_start(mod_first[c], mod_start[c]).then_inc(mod0_in[c], 16)

            def load_units(group):
                for q in range(NSLOT):
                    if not (isinstance(group, int) and group == 0):
                        sp.wait_ge(w_lo, (group - 1) * NSLOT + q + 1)
                    sp.dma_start(raw[:, q], units[bass.ds(group * NSLOT + q, 1)]).then_inc(raw_in[q], 16)

            load_units(0)
            for st in STAGES:
                for ph in phases(st):
                    kind, c, g, count, _ = ph
                    if kind == "latent":
                        sp.wait_ge(mod_done, MOD_CHUNKS - MOD_FIRST + 1)
                        for dst, src in zip((cos_t, sin_t, ident), rope_d):
                            sp.dma_start(dst[:], src).then_inc(rope_in, 16)
                    last = g + count == GROUPS
                    n = count - last
                    with sp.Fori(0, n) as i:
                        load_units(g + 1 + i)
                        if has_mods(st, ph):
                            for j in range(8):
                                piece = 4 * mod_chunk0(st, ph) + 8 * i + j
                                sp.wait_ge(modp_free, piece + 1)
                                sp.dma_start(mod_raw[:, j % 2], mod_pieces[bass.ds(piece, 1)]).then_inc(modp_in[j % 2], 16)
            st = STAGES[-1]
            tail = TAILS[len(STAGES)]
            n = 0
            for h in range(st.nh):
                c0, c1 = st.halves[h]
                for m in range(KT):
                    sp.wait_ge(x_upd, KT * tail.post[h] + m + 1)
                    sp.dma_start(out_d[m, :, c0 - (TOK - out_d.shape[2]):c1 - (TOK - out_d.shape[2])],
                                 x_res[:, m, c0:c1]).then_inc(out_sent, 16)
                    n += 16
            sp.wait_ge(out_sent, n)

        @block.gpsimd
        def _(pool):
            nc.gpsimd.memset(ones[:], 1.0).then_inc(consts, 1)
            nc.gpsimd.memset(eps_col[:], EPS).then_inc(consts, 1)
            nc.gpsimd.memset(sum_sq[:], 0.0).then_inc(ss_zero, 1)

            def split_lo(group, q):
                pool.wait_ge(w_hi, group * NSLOT + q + 1)
                nc.gpsimd.tensor_tensor(w_slot[:, q, 1], raw[:, q], w_slot[:, q, 0].bitcast(F32),
                                        ALU.subtract).then_inc(w_lo, 1)

            def add_square(number, c0, c1):
                pool.wait_ge(sq_done, number)
                wait_pos(pool, ss_added, number - 1)
                nc.gpsimd.tensor_tensor(sum_sq[:, c0:c1], sum_sq[:, c0:c1], act_tmp[:, (number - 1) % 2, :c1 - c0],
                                        ALU.add).then_inc(ss_added, 1)

            def clear_sums(stat, c0, c1):
                pool.wait_ge(stat_ready, stat)
                nc.gpsimd.memset(sum_sq[:, c0:c1], 0.0).then_inc(ss_zero, 1)
                pool.wait_ge(ss_zero, stat + 1)

            def tail_steps(tail):
                if tail.n == 0:
                    pool.wait_ge(ss_zero, 1)
                nxt = (tail.stage.group0 if tail.stage else 0)
                for x in tail.order:
                    h = x[1]
                    c0, c1 = tail.halves[h]
                    if x[0] == "E":
                        add_square(tail.square[x], c0, c1)
                        nh, q = len(tail.halves), x[2] % 4
                        if h == nh - 1:
                            group = last_out(tail.stage)[2] + x[2] // 4 + 1
                            if group < GROUPS:
                                split_lo(group, q)
                    elif x[0] == "post":
                        if tail.pre:
                            clear_sums(tail.stat[x], c0, c1)
                            for m in range(KT):
                                add_square(tail.square[("post", h, m)], c0, c1)
                    else:
                        if tail.stage is None:
                            for m in range(KT):
                                add_square(tail.square[("post", h, m)], c0, c1)
                        clear_sums(tail.stat[x], c0, c1)
                        for m in range(KT):
                            k = KT * tail.pre_no[h] + m
                            pool.wait_ge(h_hi, k + 1)
                            nc.gpsimd.tensor_tensor(h_in[:, 1, m, c0:c1], dve_tmp[:, m % 2, :c1 - c0],
                                                    h_in[:, 0, m, c0:c1].bitcast(F32), ALU.subtract).then_inc(h_lo, 1)

            g_items = 0
            for q in range(NSLOT):
                split_lo(0, q)
            tail_steps(TAILS[0])
            for n, st in enumerate(STAGES):
                for ph in phases(st):
                    kind, c, g, count, item0 = ph
                    per = 2 * st.nh
                    if kind == "in" and st.kind == "ffn":
                        with pool.Fori(0, count) as i:
                            for x in range(per):
                                t, (c0, c1) = x % 2, st.halves[x // 2]
                                pool.wait_ge(g_hi, g_items + per * i + x + 1)
                                dst = g_act[:, :, bass.ds(2 * i + t, 1), c0:c1]
                                nc.gpsimd.tensor_tensor(dst[:, 1], dve_tmp[:, x % 2:x % 2 + 1, :c1 - c0], dst[:, 0].bitcast(F32),
                                                        ALU.subtract).then_inc(g_free, 1)
                                for q in ((0, 1), (2, 3))[x % 2] if x >= per - 2 else ():
                                    split_lo(g + i + 1, q)
                        g_items += per * count
                    elif kind == "in":
                        with pool.Fori(0, count) as i:
                            for q in range(NSLOT):
                                split_lo(g + i + 1, q)
                    elif kind == "gates":
                        for m in range(KT):
                            rg_pool(m, split_lo, g)
                    elif kind == "latent":
                        mla_latent_pool(split_lo, g)
                    elif kind == "heads":
                        with pool.Fori(0, count) as i:
                            for q in range(NSLOT):
                                split_lo(g + i + 1, q)
                    elif ph != last_out(st):
                        with pool.Fori(0, count) as i:
                            for q in range(NSLOT):
                                split_lo(g + i + 1, q)
                tail_steps(TAILS[n + 1])

        PAIR = [("S", 0), ("S", 1), ("T", 0), ("S", 2), ("T", 1), ("S", 3), ("T", 2), ("S", 4), ("T", 3), ("S", 5),
                ("V", 0), ("T", 4), ("S", 6), ("T", 5), ("S", 7), ("T", 6), ("T", 7), ("V", 1)]
        PROJ = ([("qr", 0, 0)] + [x for h in range(2) for x in (("q", h, 0), ("k", h, 0), ("k", h, 1))]
                + [("v", t, 0) for t in range(CKT)])

        def proj_dst(kind, n, half):
            if kind == "q":
                return q_head[n][0][:], q_head[n][1][:]
            if kind == "k":
                c0, c1 = HALVES[half]
                return k_head[n][:, 0, c0:c1], k_head[n][:, 1, c0:c1]
            return v_pair[:, 0, n], v_pair[:, 1, n]

        def turned(u):
            src = ps[:, 4:6, :3 * P].rearrange("p b (t q) -> p b t q", t=3)
            c = (u % QT) * P
            dst = [p_turned[:, n, :, c:c + P].rearrange("p (b t) q -> p b t q", b=2) for n in range(2)]
            return src, dst

        @block.scalar
        def _(act):
            def split_hi(group, q):
                act.wait_ge(raw_in[q], 16 * (group + 1))
                nc.scalar.activation(w_slot[:, q, 0], raw[:, q], ACT.Copy).then_inc(w_hi, 1)

            def square(number, src, n):
                wait_pos(act, ss_added, number - 2)
                nc.scalar.activation(act_tmp[:, (number - 1) % 2, :n], src, ACT.Square).then_inc(sq_done, 1)

            def rsqrt_mean(stat, n):
                act.wait_ge(stat_ready, stat)
                nc.scalar.activation(rstd[:, :n], ps[:, STAT, :n], ACT.Ln, bias=eps_col[:], scale=1.0 / D).then_inc(ln_done, 1)
                act.wait_ge(ln_done, stat)
                nc.scalar.activation(rstd[:, :n], rstd[:, :n], ACT.Exp, scale=-0.5).then_inc(rs_ready, 1)

            def tail_steps(tail):
                st = tail.stage
                if st is not None and st.kind == "ffn":
                    act.wait_ge(in_free, 2 + st.in0 + FT * st.nh)
                for x in tail.order:
                    h = x[1]
                    c0, c1 = tail.halves[h]
                    n = c1 - c0
                    if x[0] == "E":
                        item = out_item(st, x)
                        act.wait_ge(out_free, 3 + item + 1)
                        square(tail.square[x], y_acc[:, x[2], c0:c1], n)
                        if h == st.nh - 1:
                            group = last_out(st)[2] + x[2] // 4 + 1
                            if group < GROUPS:
                                split_hi(group, x[2] % 4)
                    elif x[0] == "post":
                        rsqrt_mean(tail.stat[x], n)
                        if tail.pre:
                            for m in range(KT):
                                act.wait_ge(x_upd, KT * tail.post[h] + m + 1)
                                square(tail.square[("post", h, m)], x_res[:, m, c0:c1], n)
                    else:
                        if st is None:
                            act.wait_ge(x_in, 16)
                            for m in range(KT):
                                square(tail.square[("post", h, m)], x_res[:, m, c0:c1], n)
                        rsqrt_mean(tail.stat[x], n)
                        for m in range(KT):
                            k = KT * tail.pre_no[h] + m
                            act.wait_ge(h_f32, k + 1)
                            nc.scalar.activation(h_in[:, 0, m, c0:c1], dve_tmp[:, m % 2, :n], ACT.Copy).then_inc(h_hi, 1)

            def ffn_in(st, g, count, item0, g0):
                per = 2 * st.nh
                with act.Fori(0, count) as i:
                    for x in range(per):
                        t, (c0, c1) = x % 2, st.halves[x // 2]
                        item = item0 + per * i + x
                        act.wait_ge(in_ready, item + 1)
                        act.wait_ge(in_free, item + 1)
                        nc.scalar.activation(act_tmp[:, t, :c1 - c0], ps[:, 2 * t, :c1 - c0], ACT.Silu).then_inc(pair_act, 1)
                        act.wait_ge(in_free, item + 3)
                        nc.scalar.activation(g_act[:, 0, bass.ds(2 * i + t, 1), c0:c1], dve_tmp[:, t:t + 1, :c1 - c0],
                                             ACT.Copy).then_inc(g_hi, 1)
                        for q in ((0, 1), (2, 3))[x % 2] if x >= per - 2 else ():
                            split_hi(g + i + 1, q)

            def out_loop(st, g, count, item0):
                nh = st.nh
                with act.Fori(0, count) as i:
                    for q in range(NSLOT):
                        act.wait_ge(out_ready, item0 + 4 * nh * i + 4 * (nh - 1) + q + 1)
                        split_hi(g + i + 1, q)

            def rg(st, ph):
                kind, c, g, count, item0 = ph
                if kind == "in":
                    with act.Fori(0, count) as i:
                        for x in range(4):
                            t, (c0, c1) = x % 2, st.halves[x // 2]
                            act.wait_ge(in_ready, item0 + 4 * i + x + 1)
                            nc.scalar.activation(rg_yu[:, 0, bass.ds(2 * i + t, 1), c0:c1], ps[:, 2 * t:2 * t + 1, :c1 - c0],
                                                 ACT.Gelu_apprx_tanh).then_inc(pair_act, 1)
                            for q in ((0, 1), (2, 3))[t] if x >= 2 else ():
                                split_hi(g + i + 1, q)
                elif kind == "gates":
                    def uc_split(m):
                        act.wait_ge(conv_step, CONV_STEPS * (m + 1))
                        if m >= 2:
                            act.wait_ge(gate_ready, 2 * (m - 1))
                        nc.scalar.activation(rg_split[:, m % 2, 0], rg_uc[:, m], ACT.Copy).then_inc(uc_hi, 1)

                    uc_split(0)
                    for m in range(KT):
                        if m + 1 < KT:
                            uc_split(m + 1)
                        if m >= 2:
                            act.wait_ge(m_lo, m - 1)
                        for d in range(2):
                            act.wait_ge(gate_ready, 2 * m + d + 1)
                            for k in range(2):
                                col = VEC["gate_b"] + (d * 2 + k) * KT + m
                                ins = nc.scalar.activation(
                                    rg_work[:, m % 2, d, k].rearrange("p (h c) -> p h c", h=2),
                                    ps[:, 4 * d + 2 * k:4 * d + 2 * k + 2, :TOK // 2], ACT.Sigmoid,
                                    bias=vecs[:, col:col + 1])
                            ins.then_inc(sig_done, 1)
                        if m % 2 == 1:
                            split_hi(g + 1, m // 2)
                        act.wait_ge(sig_done, 2 * m + 2)
                        for d in range(2):
                            w = rg_work[:, m % 2, d]
                            col = d * KT + m
                            nc.scalar.activation(w[:, 2], w[:, 0], ACT.Exp, scale=decay[:, 0, col:col + 1]).then_inc(expd, 1)
                        for d in range(2):
                            w = rg_work[:, m % 2, d]
                            col = d * KT + m
                            nc.scalar.activation(w[:, 0], w[:, 0], ACT.Tanh, scale=decay[:, 1, col:col + 1]).then_inc(expd, 1)
                        for d in range(2):
                            act.wait_ge(expd, 4 * m + 3 + d)
                            w = rg_work[:, m % 2, d]
                            nc.scalar.activation(w[:, 0], w[:, 0], ACT.Sqrt).then_inc(coef_done, 1)
                        act.wait_ge(rg_step, RG_STEPS * (m + 1))
                        nc.scalar.activation(rg_m[:, 0, m], rg_work[:, m % 2, 0, 0], ACT.Copy).then_inc(m_hi, 1)

            def mla(st, ph):
                kind, c, g, count, _ = ph
                if kind == "latent":
                    for q in range(NSLOT):
                        act.wait_ge(lat_ready, q + 4)
                        split_hi(g + 1, q)
                    sums = 0
                    norms = latent_norms()
                    for n, (src, gains, cols, size) in enumerate(norms):
                        for x in src:
                            sums += 1
                            act.wait_ge(lat_read, x[1])
                            wait_pos(act, lat_sum, sums - 2)
                            nc.scalar.activation(mla_sq[:, (sums - 1) % 2, :cols], x[0], ACT.Square).then_inc(lat_sq, 1)
                        if n == 0:
                            act.wait_ge(kr_step, 3)
                            act.wait_ge(lat_read, 6)
                            nc.scalar.activation(kr_n[:, 0], kr_raw[:], ACT.Copy).then_inc(lat_hi, 1)
                        if n == 2:
                            for q in range(NSLOT):
                                act.wait_ge(lat_ready, 8 + q)
                                split_hi(g + 2, q)
                        act.wait_ge(lat_sum, sums)
                        nc.scalar.activation(rstd[:, :cols], ps[:, 6, :cols], ACT.Ln, bias=eps_col[:],
                                             scale=1.0 / size).then_inc(lat_ln, 1)
                        act.wait_ge(lat_ln, n + 1)
                        nc.scalar.activation(rstd[:, :cols], rstd[:, :cols], ACT.Exp, scale=-0.5).then_inc(lat_rs, 1)
                        for k, x in enumerate(src):
                            act.wait_ge(lat_step, sums - len(src) + k + 1)
                            dst = latent_splits()[sums - len(src) + k][0]
                            nc.scalar.activation(dst[:, 0], x[0], ACT.Copy).then_inc(lat_hi, 1)
                    return
                with act.Fori(0, count) as i:
                    for n, (what, a, half) in enumerate(PROJ):
                        if what == "qr":
                            act.wait_ge(qr_step, 4 * i + 4)
                            nc.scalar.activation(qr_pair[:, 0], rot_tmp[:, 0], ACT.Copy).then_inc(prj_hi, 1)
                            continue
                        width = {"q": LAT, "k": TOK // 2, "v": 2 * VD}[what]
                        act.wait_ge(prj_ready, len(PROJ) * i + n + 1)
                        nc.scalar.activation(proj_dst(what, a, half)[0], ps[:, n % 4, :width], ACT.Copy).then_inc(prj_hi, 1)
                    for q in range(NSLOT):
                        split_hi(g + i + 1, q)
                    for what, u in PAIR:
                        if what == "S":
                            act.wait_ge(t_ready, 8 * i + u + 1)
                            act.wait_ge(s_max, 16 * i + 2 * u + 2)
                            nc.scalar.activation(p_soft[:, u % 2].rearrange("p (b c) -> p b c", b=2),
                                                 ps[:, 2 * (u % 2):2 * (u % 2) + 2, :TOK // 2], ACT.Exp,
                                                 bias=soft_max[:, u % 2, 1:2], scale=SCALE,
                                                 accum_out=soft_max[:, u % 2, 2:3]).then_inc(s_exp, 1)
                        elif what == "T":
                            act.wait_ge(t_ready, 8 * i + u + 3)
                            src, dst = turned(u)
                            nc.scalar.activation(dst[0], src, ACT.Copy).then_inc(t_hi, 1)
                        else:
                            act.wait_ge(o_ready, 2 * i + u + 1)
                            nc.scalar.activation(att_o[:, 0, bass.ds(2 * i + u, 1)], ps[:, 6:7, :LAT], ACT.Copy).then_inc(o_hi, 1)

            act.wait_ge(vec_in, 16)
            nc.scalar.activation(cond[:], vecs[:, VEC["cond"]:VEC["cond"] + 16], ACT.Silu).then_inc(cond_done, 1)
            act.wait_ge(soft_step, 1)
            nc.scalar.activation(soft[:, 1], soft[:, 0], ACT.Exp).then_inc(soft_exp, 1)
            act.wait_ge(consts, 2)
            for q in range(NSLOT):
                split_hi(0, q)
            tail_steps(TAILS[0])
            g_items = 0
            for n, st in enumerate(STAGES):
                if st.kind == "ffn":
                    wait_pos(act, ss_added, TAILS[n].end[0])
                for ph in phases(st):
                    kind, c, g, count, item0 = ph
                    if st.kind == "rg" and kind != "out":
                        rg(st, ph)
                    elif st.kind == "mla" and kind != "out":
                        mla(st, ph)
                    elif kind == "in":
                        ffn_in(st, g, count, item0, g_items)
                        g_items += 2 * st.nh * count
                    elif ph != last_out(st):
                        out_loop(st, g, count, item0)
                tail_steps(TAILS[n + 1])

        @block.vector
        def _(dve):
            v = nc.vector
            dve.sem_inc(in_free, 2)
            dve.sem_inc(out_free, 3)
            dve.sem_inc(g_free, 2)
            dve.sem_inc(modp_free, 2)
            dve.sem_inc(t_ready, 2)
            dve.sem_inc(s_exp, 2)
            dve.sem_inc(t_free, 1)
            dve.sem_inc(o_free, 1)
            soft_n = [0]

            def soft_link(ins):
                soft_n[0] += 1
                ins.then_inc(soft_step, 1)
                dve.wait_ge(soft_step, soft_n[0])

            def softplus():
                z, e, s, s2, acc = (soft[:, n] for n in range(5))
                lam = vecs[:, VEC["lam"]:VEC["lam"] + 16]
                v.tensor_scalar(acc, lam, -1.0, None, ALU.mult).then_inc(soft_exp, 1)
                dve.wait_ge(soft_exp, 1)
                soft_link(v.tensor_tensor(z, lam, acc, ALU.min))
                dve.wait_ge(soft_exp, 2)
                soft_link(v.tensor_scalar(s, e, 2.0, None, ALU.add))
                soft_link(v.reciprocal(s, s))
                soft_link(v.tensor_tensor(s, s, e, ALU.mult))
                soft_link(v.tensor_tensor(s2, s, s, ALU.mult))
                soft_link(v.tensor_scalar(e, s2, 1.0 / 15, 1.0 / 13, ALU.mult, ALU.add))
                for k in (11, 9, 7, 5, 3, 1):
                    soft_link(v.tensor_tensor(e, e, s2, ALU.mult))
                    soft_link(v.tensor_scalar(e, e, 1.0 / k, None, ALU.add))
                soft_link(v.tensor_tensor(e, e, s, ALU.mult))
                soft_link(v.tensor_scalar(acc, acc, 0.0, None, ALU.max))
                soft_link(v.scalar_tensor_tensor(e, e, 2.0, acc, ALU.mult, ALU.add))
                soft_link(v.tensor_scalar(decay[:, 0], e, -RG_C, None, ALU.mult))
                soft_link(v.tensor_scalar(decay[:, 1], e, RG_C / 2, None, ALU.mult))

            gains = [0]

            def gain_link(ins):
                gains[0] += 1
                ins.then_inc(gain_done, 1)

            def make_gains(tail):
                st = tail.stage
                if st is not None:
                    w = 0.5 if st.kind == "ffn" else 1.0
                    a, b = mod_at(st.layer, st.sub, 2), gain_at(st.layer, 2 * st.sub + 1)
                    for k in range(2):
                        gain_link(v.scalar_tensor_tensor(post_gain[:, k], mods[:, k, a:a + KT], w, vecs[:, b:b + KT],
                                                         ALU.mult, ALU.mult))
                if tail.pre:
                    nx = STAGES[tail.n]
                    a, b = mod_at(nx.layer, nx.sub, 1), gain_at(nx.layer, 2 * nx.sub)
                    for k in range(2):
                        gain_link(v.scalar_tensor_tensor(pre_gain[:, k], mods[:, k, a:a + KT], 1.0, vecs[:, b:b + KT],
                                                         ALU.add, ALU.mult))
                dve.wait_ge(gain_done, gains[0])

            def evict(item, dst, bank, n, first):
                dve.wait_ge(out_ready, item + 1)
                if first:
                    v.tensor_copy(dst, bank).then_inc(out_free, 1)
                else:
                    v.tensor_tensor(dst, bank, dst, ALU.add).then_inc(out_free, 1)

            def tail_steps(tail):
                st = tail.stage
                make_gains(tail)
                if st is not None and st.kind == "ffn":
                    dve.wait_ge(g_free, 2 + g_total[0])
                if st is not None:
                    first = st.kind != "ffn"
                for x in tail.order:
                    h = x[1]
                    c0, c1 = tail.halves[h]
                    n = c1 - c0
                    segs = segments(c0, c1)
                    if x[0] == "E":
                        nh = st.nh
                        bank = BANKS[nh][4 * h + x[2] % 4]
                        evict(out_item(st, x), y_acc[:, x[2], c0:c1], ps[:, bank, :n], n, first)
                    elif x[0] == "post":
                        no = KT * tail.post[h]
                        wait_pos(dve, h_lo, KT * pres_done[0])
                        dve.wait_ge(rs_ready, tail.stat[x])

                        def normed(m):
                            if m >= 2:
                                dve.wait_ge(x_upd, no + m - 1)
                            v.tensor_tensor(dve_tmp[:, m % 2, :n], y_acc[:, m, c0:c1], rstd[:, :n],
                                            ALU.mult).then_inc(y_normed, 1)

                        normed(0)
                        for m in range(KT):
                            if m + 1 < KT:
                                normed(m + 1)
                            dve.wait_ge(y_normed, no + m + 1)
                            for k, a, b in segs:
                                ins = v.scalar_tensor_tensor(x_res[:, m, a:b], dve_tmp[:, m % 2, a - c0:b - c0],
                                                             post_gain[:, k, m:m + 1], x_res[:, m, a:b], ALU.mult, ALU.add)
                            ins.then_inc(x_upd, 1)
                    else:
                        nx = STAGES[tail.n]
                        shift = mod_at(nx.layer, nx.sub, 0)
                        no = KT * tail.pre_no[h]
                        dve.wait_ge(rs_ready, tail.stat[x])
                        if st is None:
                            dve.wait_ge(x_in, 16)
                        for m in range(KT):
                            wait_pos(dve, h_lo, no + m - 1)
                            tmp = dve_tmp[:, m % 2, :n]
                            v.tensor_tensor(tmp, x_res[:, m, c0:c1], rstd[:, :n], ALU.mult).then_inc(x_normed, 1)
                            dve.wait_ge(x_normed, no + m + 1)
                            for k, a, b in segs:
                                part = dve_tmp[:, m % 2, a - c0:b - c0]
                                ins = v.tensor_scalar(part, part, pre_gain[:, k, m:m + 1],
                                                      mods[:, k, shift + m:shift + m + 1], ALU.mult, ALU.add)
                            ins.then_inc(h_f32, 1)
                        pres_done[0] = tail.pre_no[h] + 1

            def mod_part(j, chunk, step0):
                for b in range(2):
                    dve.wait_ge(modp_in[b], 16 * (2 * chunk + j + 1))
                    for kk in range(2):
                        k = 4 * j + 2 * b + kk
                        for c in range(2):
                            step = step0 + 8 * j + 4 * b + 2 * kk + c
                            if k == 0:
                                ins = v.tensor_scalar(mod_acc[:, c], mod_raw[:, b, kk], cond[:, 2 * k + c:2 * k + c + 1],
                                                      None, ALU.mult)
                            else:
                                dve.wait_ge(mod_step, step - 1)
                                ins = v.scalar_tensor_tensor(mod_acc[:, c], mod_raw[:, b, kk],
                                                             cond[:, 2 * k + c:2 * k + c + 1], mod_acc[:, c],
                                                             ALU.mult, ALU.add)
                            ins.then_inc(mod_step, 1)
                    dve.wait_ge(mod_step, step + 1)
                    dve.sem_inc(modp_free, 1)

            def mod_finish(chunk):
                dve.wait_ge(mod_sum, chunk + 1)
                per = MOD_W // P
                col = (MOD_FIRST + chunk) * per
                bias = vecs[:, bass.ds(VEC["mod_b"] + col, per)]
                for c in range(2):
                    ins = v.tensor_tensor(mods[:, c, bass.ds(col, per)], ps[:, MODB, per * c:per * c + per], bias, ALU.add)
                ins.then_inc(mod_done, 1)

            def ffn_in(st, ph):
                kind, c, g, count, item0 = ph
                per = 2 * st.nh
                if c == 0:
                    dve.wait_ge(h_lo, KT * pres_done[0])
                with dve.Fori(0, count) as i:
                    for x in range(per):
                        t, (c0, c1) = x % 2, st.halves[x // 2]
                        n = c1 - c0
                        item = item0 + per * i + x
                        gitem = g_total[0] + per * i + x
                        if has_mods(st, ph):
                            chunk = mod_chunk0(st, ph) + 2 * i + x // 2
                            mod_part(x % 2, chunk, 16 * chunk)
                        dve.wait_ge(pair_act, item + 1)
                        dve.wait_ge(g_free, gitem + 1)
                        v.tensor_tensor(dve_tmp[:, t, :n], ps[:, 2 * t + 1, :n], act_tmp[:, t, :n], ALU.mult).then_inc(in_free, 1)
                        if has_mods(st, ph) and x % 2 == 1:
                            mod_finish(chunk)
                g_total[0] += per * count

            def conv(tile, tile_no):
                def col(name, k=0):
                    return vecs[:, bass.ds(VEC[name] + k * KT + tile, 1)]

                src = rg_yu[:, 1, bass.ds(tile, 1)]
                dst = rg_uc[:, bass.ds(tile, 1)]
                step = CONV_STEPS * tile
                v.tensor_scalar(dst, src, col("conv_w", 2), col("conv_b"), ALU.mult, ALU.add).then_inc(conv_step, 1)
                n = 0
                for k in (1, 3, 0):
                    back = 2 - k
                    for a, b in ((0, CTX), (CTX, TOK)):
                        n += 1
                        lo, hi = (a + back, b) if back > 0 else (a, b + back)
                        dve.wait_ge(conv_step, step + n)
                        v.scalar_tensor_tensor(dst[:, :, lo:hi], src[:, :, lo - back:hi - back], col("conv_w", k),
                                               dst[:, :, lo:hi], ALU.mult, ALU.add).then_inc(conv_step, 1)

            def rg(st, ph):
                kind, c, g, count, item0 = ph
                if kind == "in":
                    with dve.Fori(0, count) as i:
                        for x in range(4):
                            t, (c0, c1) = x % 2, st.halves[x // 2]
                            dve.wait_ge(pair_act, item0 + 4 * i + x + 1)
                            v.tensor_copy(rg_yu[:, 1, bass.ds(2 * i + t, 1), c0:c1],
                                          ps[:, 2 * t + 1:2 * t + 2, :c1 - c0]).then_inc(in_free, 1)
                            if x >= 2:
                                dve.wait_ge(in_free, 2 + item0 + 4 * i + x + 1)
                                conv(2 * i + t, x)
                    return
                for m in range(KT):
                    w = rg_work[:, m % 2]
                    step = RG_STEPS * m

                    def link(ins, number):
                        ins.then_inc(rg_step, 1)
                        dve.wait_ge(rg_step, step + number)

                    for d in range(2):
                        s, b, a = w[:, d, 0], w[:, d, 1], w[:, d, 2]
                        dve.wait_ge(coef_done, 2 * m + d + 1)
                        link(v.scalar_tensor_tensor(s, a, 1.0, s, ALU.add, ALU.mult), 3 * d + 1)
                        dve.wait_ge(iu_done, 2 * m + d + 1)
                        link(v.tensor_tensor(b, s, b, ALU.mult), 3 * d + 2)
                        if d == 0:
                            link(v.tensor_tensor_scan(s, a, b, 0.0, ALU.mult, ALU.add), 3)
                        else:
                            link(v.tensor_tensor_scan(s[:, CTX - 1::-1], a[:, CTX - 1::-1], b[:, CTX - 1::-1], 0.0,
                                                      ALU.mult, ALU.add), 6)
                            link(v.tensor_tensor_scan(s[:, TOK - 1:CTX - 1:-1], a[:, TOK - 1:CTX - 1:-1],
                                                      b[:, TOK - 1:CTX - 1:-1], s[:, 0:1], ALU.mult, ALU.add), 7)
                    link(v.tensor_tensor(w[:, 0, 0], w[:, 0, 0], w[:, 1, 0], ALU.add), 8)
                    link(v.tensor_tensor(w[:, 0, 0], w[:, 0, 0], rg_yu[:, 0, m], ALU.mult), 9)

            def mla(st, ph):
                kind, c, g, count, _ = ph
                if kind == "latent":
                    places = []
                    for h in range(2):
                        c0, c1 = HALVES[h]
                        places += [ckv_raw[:, 0, c0:c1], ckv_raw[:, 1, c0:c1], kr_raw[:, c0:c1]]
                    places += [kr_swap[:]] + [cq_raw[:, t] for t in range(4)]

                    def apply_norm(which):
                        src, col, cols, size = latent_norms()[which]
                        dve.wait_ge(lat_rs, which + 1)
                        for k, x in enumerate(src):
                            v.scalar_tensor_tensor(x[0], x[0], vecs[:, col + k:col + k + 1], rstd[:, :cols],
                                                   ALU.mult, ALU.mult).then_inc(lat_step, 1)

                    for n, dst in enumerate(places):
                        dve.wait_ge(lat_ready, n + 1)
                        v.tensor_copy(dst, ps[:, n % 4, :dst.shape[-1]]).then_inc(lat_read, 1)
                        if n == 6:
                            dve.wait_ge(rope_in, 48)
                            dve.wait_ge(lat_read, 7)
                            v.tensor_tensor(rot_tmp[:, 0], kr_raw[:, CTX:], cos_t[:], ALU.mult).then_inc(kr_step, 1)
                            v.tensor_tensor(rot_tmp[:, 1], kr_swap[:], sin_t[:], ALU.mult).then_inc(kr_step, 1)
                            dve.wait_ge(kr_step, 2)
                            v.tensor_tensor(kr_raw[:, CTX:], rot_tmp[:, 0], rot_tmp[:, 1], ALU.add).then_inc(kr_step, 1)
                        if n >= 8:
                            apply_norm(n - 8)
                    return
                with dve.Fori(0, count) as i:
                    for n, (what, a, half) in enumerate(PROJ):
                        if what == "qr":
                            dve.wait_ge(prj_ready, len(PROJ) * i + 1)
                            v.tensor_tensor(rot_tmp[:, 0], ps[:, 0, :LAT], cos_t[:], ALU.mult).then_inc(qr_step, 1)
                            v.stream_shuffle(rot_tmp[:, 1], ps[:, 0, :LAT], [(k + 16) % 32 for k in range(32)]).then_inc(qr_step, 1)
                            dve.wait_ge(qr_step, 4 * i + 2)
                            v.tensor_tensor(rot_tmp[:, 1], rot_tmp[:, 1], sin_t[:], ALU.mult).then_inc(qr_step, 1)
                            dve.wait_ge(qr_step, 4 * i + 3)
                            v.tensor_tensor(rot_tmp[:, 0], rot_tmp[:, 0], rot_tmp[:, 1], ALU.add).then_inc(qr_step, 1)
                            dve.wait_ge(prj_hi, len(PROJ) * i + 1)
                            v.tensor_tensor(qr_pair[:, 1], rot_tmp[:, 0], qr_pair[:, 0].bitcast(F32),
                                            ALU.subtract).then_inc(prj_free, 1)
                            continue
                        width = {"q": LAT, "k": TOK // 2, "v": 2 * VD}[what]
                        hi, lo = proj_dst(what, a, half)
                        dve.wait_ge(prj_hi, len(PROJ) * i + n + 1)
                        v.tensor_tensor(lo, ps[:, n % 4, :width], hi.bitcast(F32), ALU.subtract).then_inc(prj_free, 1)

                    def weigh(u):
                        dve.wait_ge(s_exp, 8 * i + u + 3)
                        v.reciprocal(soft_max[:, u % 2, 3:4], soft_max[:, u % 2, 2:3]).then_inc(p_rcp, 1)
                        dve.wait_ge(p_rcp, 8 * i + u + 1)
                        v.tensor_scalar(p_soft[:, u % 2], p_soft[:, u % 2], soft_max[:, u % 2, 3:4], None,
                                        ALU.mult).then_inc(p_ready, 1)

                    weighed = 0
                    for what, u in PAIR:
                        if what == "S":
                            dve.wait_ge(s_ready, 8 * i + u + 1)
                            v.tensor_reduce(soft_max[:, u % 2, 0:1], ps[:, 2 * (u % 2):2 * (u % 2) + 2, :TOK // 2],
                                            AX.XY, ALU.max).then_inc(s_max, 1)
                            dve.wait_ge(s_max, 16 * i + 2 * u + 1)
                            v.tensor_scalar(soft_max[:, u % 2, 1:2], soft_max[:, u % 2, 0:1], -SCALE, None,
                                            ALU.mult).then_inc(s_max, 1)
                            if u > 0:
                                weigh(u - 1)
                                weighed = u
                        elif what == "T":
                            if weighed == u:
                                weigh(u)
                                weighed = u + 1
                            src, dst = turned(u)
                            dve.wait_ge(t_hi, 8 * i + u + 1)
                            v.tensor_tensor(dst[1], src, dst[0].bitcast(F32), ALU.subtract).then_inc(t_free, 1)
                        else:
                            dve.wait_ge(o_hi, 2 * i + u + 1)
                            place = att_o[:, :, bass.ds(2 * i + u, 1)]
                            v.tensor_tensor(place[:, 1], ps[:, 6:7, :LAT], place[:, 0].bitcast(F32),
                                            ALU.subtract).then_inc(o_free, 1)

            dve.wait_ge(vec_in, 16)
            softplus()
            dve.wait_ge(mod_sum0, 1)
            first = MOD_FIRST * MOD_W // P
            for c in range(2):
                ins = v.tensor_tensor(mods[:, c, 0:first], ps[:, 6, c:2 * first:2],
                                      vecs[:, VEC["mod_b"]:VEC["mod_b"] + first], ALU.add)
            ins.then_inc(mod_done, 1)
            dve.wait_ge(mod_done, 1)
            g_total, pres_done = [0], [0]
            tail_steps(TAILS[0])
            for n, st in enumerate(STAGES):
                for ph in phases(st):
                    kind, c, g, count, item0 = ph
                    if st.kind == "rg" and kind != "out":
                        rg(st, ph)
                    elif st.kind == "mla" and kind != "out":
                        mla(st, ph)
                    elif kind == "in":
                        ffn_in(st, ph)
                    elif ph != last_out(st):
                        nh = st.nh
                        with dve.Fori(0, count) as i:
                            for x in range(4 * nh):
                                h, q = x // 4, x % 4
                                c0, c1 = st.halves[h]
                                evict(item0 + 4 * nh * i + x, y_acc[:, bass.ds(4 * i + q, 1), c0:c1],
                                      ps[:, BANKS[nh][x]:BANKS[nh][x] + 1, :c1 - c0], c1 - c0, c == 0)
                if st.kind == "ffn" and st.layer == 0:
                    dve.wait_ge(mod_done, 1 + st.mod0 - MOD_FIRST + 16)
                tail_steps(TAILS[n + 1])

        @block.tensor
        def _(pe):
            mm = nc.tensor.matmul

            def product(out, w, x, blocks, start=True, stop=True):
                for k in range(blocks):
                    for n, (a, b) in enumerate(((0, 0), (0, 1), (1, 0))):
                        last = mm(out, w(a, k), x(b, k), start=start and k == 0 and n == 0,
                                  stop=stop and k == blocks - 1 and n == 2)
                return last

            def slot(q, first=0, width=P):
                return lambda a, k: w_slot[:, q, a, first + k]

            def stat(tail, x):
                c0, c1 = tail.halves[x[1]]
                s = tail.stat[x]
                if x[0] == "post":
                    squares = tail.square[("E", x[1], KT - 1)]
                else:
                    squares = tail.square[("post", x[1], KT - 1)]
                pe.wait_ge(ss_added, squares)
                wait_pos(pe, ln_done, s - 1)
                mm(ps[:, STAT, :c1 - c0], ones[:], sum_sq[:, c0:c1], start=True, stop=True).then_inc(stat_ready, 1)

            def input_ready(tail, h):
                pe.wait_ge(h_lo, KT * (tail.pre_no[h] + 1))

            def pair_item(st, n, x, item, first_unit):
                t, (c0, c1) = x % 2, st.halves[x // 2]
                for b in range(2):
                    pe.wait_ge(w_lo, first_unit + 2 * t + b + 1)
                    if b == 0:
                        pe.wait_ge(in_free, item + 1)
                    last = product(ps[:, 2 * t + b, :c1 - c0], slot(2 * t + b), lambda a, k: h_in[:, a, k, c0:c1], KT)
                last.then_inc(in_ready, 1)

            def mod_sums(chunk):
                pe.wait_ge(mod_step, 16 * chunk + 16)
                for c in range(2):
                    for j in range(MOD_W // P):
                        last = mm(ps[:, MODB, 4 * c + j:4 * c + j + 1], mod_acc[:, c, j * P:(j + 1) * P], ones[:, 0:1],
                                  start=True, stop=True)
                last.then_inc(mod_sum, 1)

            def in_phase(n, st, ph):
                kind, c, g, count, item0 = ph
                per = 2 * st.nh
                tail = TAILS[n]

                def group(i, peeled):
                    for x in range(per):
                        if peeled and c == 0 and x in (0, 2):
                            input_ready(tail, x // 2 if len(tail.halves) == 2 else 0)
                        pair_item(st, n, x, item0 + per * i + x, (g + i) * NSLOT)
                        if peeled and c == 0 and x == 0 and len(tail.halves) == 2:
                            stat(tail, ("pre", 1))
                        if has_mods(st, ph) and x % 2 == 1:
                            if peeled and c == 0 and x == 1:
                                pe.wait_ge(ln_done, tail.end[1])
                            mod_sums(mod_chunk0(st, ph) + 2 * i + x // 2)

                start = 0
                if c == 0:
                    group(0, True)
                    start = 1
                with pe.Fori(start, count) as i:
                    group(i, False)

            def out_item_products(st, h, q, x, item, unit, blocks, src):
                c0, c1 = st.halves[h]
                pe.wait_ge(w_lo, unit + 1)
                pe.wait_ge(out_free, 3 + item - BACK[st.nh][x] + 1)
                product(ps[:, BANKS[st.nh][x], :c1 - c0], slot(q), lambda a, k: src(a, k, c0, c1), blocks).then_inc(out_ready, 1)

            def out_phase(n, st, ph):
                kind, c, g, count, item0 = ph
                nh = st.nh
                tail = TAILS[n + 1]
                final = ph == last_out(st)
                if st.kind == "ffn":
                    blocks, src = CHUNKS[c], lambda a, k, c0, c1: g_act[:, a, k, c0:c1]
                    done = g_total[0]
                    pe.wait_ge(g_free, 2 + done - (2 if nh == 2 else 0))
                elif st.kind == "rg":
                    blocks, src = KT, lambda a, k, c0, c1: rg_m[:, a, k, c0:c1]
                    pe.wait_ge(m_lo, KT)
                else:
                    blocks, src = KT, lambda a, k, c0, c1: att_o[:, a, k, :]
                    pe.wait_ge(o_free, 1 + HEADS)

                def group(i):
                    for x in range(4 * nh):
                        h, q = x // 4, x % 4
                        if st.kind == "ffn" and nh == 2 and x == 4:
                            pe.wait_ge(g_free, 2 + done)
                        out_item_products(st, h, q, x, item0 + 4 * nh * i + x, (g + i) * NSLOT + q, blocks, src)
                        if final and i == 1 and nh == 2:
                            if x == 4:
                                if st.kind == "ffn" and st.layer == 0:
                                    pe.wait_ge(mod_done, 1 + st.mod0 - MOD_FIRST + 16)
                                stat(tail, ("post", 0))
                            if x == 6 and tail.pre:
                                stat(tail, ("pre", 0))

                if final:
                    for i in range(count):
                        group(i)
                    stat(tail, ("post", nh - 1))
                    if nh == 1 and tail.pre:
                        stat(tail, ("pre", 0))
                else:
                    with pe.Fori(0, count) as i:
                        group(i)

            def gates(st, ph):
                kind, c, g, count, _ = ph
                pe.wait_ge(in_free, 2 + st.in0 + KT * st.nh)
                for j in range(NSLOT):
                    pe.wait_ge(w_lo, g * NSLOT + j + 1)
                for m in range(KT):
                    pe.wait_ge(uc_lo, m + 1)
                    for d in range(2):
                        if m:
                            pe.wait_ge(sig_done, 2 * (m - 1) + d + 1)
                        for k in range(2):
                            for h, (c0, c1) in enumerate(HALVES):
                                last = product(ps[:, 4 * d + 2 * k + h, :c1 - c0],
                                               lambda a, b: w_slot[:, m // 2, a, 4 * (m % 2) + 2 * d + k],
                                               lambda a, b: rg_split[:, m % 2, a, c0:c1], 1)
                        last.then_inc(gate_ready, 1)

            def latents(n, ph):
                kind, c, g, count, _ = ph
                tail = TAILS[n]
                items = [(q, h) for h in range(2) for q in range(3)] + [(3, None)] + [(q, None) for q in range(4)]
                sums = [0]

                def norm_sums(which):
                    src, _, cols, _ = latent_norms()[which]
                    if which:
                        pe.wait_ge(lat_ln, which)
                    for k in range(len(src)):
                        sums[0] += 1
                        pe.wait_ge(lat_sq, sums[0])
                        mm(ps[:, 6, :cols], ones[:], mla_sq[:, (sums[0] - 1) % 2, :cols], start=k == 0,
                           stop=k == len(src) - 1).then_inc(lat_sum, 1)

                for i, (q, h) in enumerate(items):
                    c0, c1 = HALVES[h] if h is not None else (CTX, TOK)
                    if i in (0, 3):
                        input_ready(tail, h)
                    unit = g * NSLOT + q if i < 7 else (g + 1) * NSLOT + q
                    pe.wait_ge(w_lo, unit + 1)
                    wait_pos(pe, lat_read, i - 3)
                    product(ps[:, i % 4, :c1 - c0], slot(q), lambda a, k: h_in[:, a, k, c0:c1], KT).then_inc(lat_ready, 1)
                    if i == 0:
                        stat(tail, ("pre", 1))
                    if i == 6:
                        norm_sums(0)
                    if i == 9:
                        norm_sums(1)
                norm_sums(2)

            def heads(ph):
                kind, c, g, count, _ = ph
                pe.wait_ge(lat_lo, 1 + len(latent_splits()))
                with pe.Fori(0, count) as i:
                    pe.wait_ge(s_exp, 8 * i + 2)
                    for n, (what, a, half) in enumerate(PROJ):
                        q = {"qr": 0, "q": 1 + a, "k": 1 + a, "v": 3}[what]
                        pe.wait_ge(w_lo, (g + i) * NSLOT + q + 1)
                        if n >= 4:
                            pe.wait_ge(prj_free, len(PROJ) * i + n - 3)
                        bank = n % 4
                        if what in ("qr", "q"):
                            last = product(ps[:, bank, :LAT], slot(q), lambda b, k: cq_n[:, b, k], QL // P)
                        elif what == "k":
                            c0, c1 = HALVES[half]
                            last = product(ps[:, bank, :c1 - c0], slot(q, QL // P), lambda b, k: ckv_n[:, b, k, c0:c1], KVL // P)
                        else:
                            last = product(ps[:, bank, :2 * VD], lambda b, k: ckv_n[:, b, k, a * P:(a + 1) * P],
                                           lambda b, k: w_slot[:, 3, b, 2 * k:2 * k + 2].rearrange("p k c -> p (k c)"),
                                           KVL // P)
                        last.then_inc(prj_ready, 1)
                    pe.wait_ge(prj_free, len(PROJ) * (i + 1))
                    for what, u in PAIR:
                        hd, cols = u // QT, slice((u % QT) * P, (u % QT + 1) * P)
                        if what == "S":
                            pe.wait_ge(s_exp, 8 * i + u + 1)
                            for h, (c0, c1) in enumerate(HALVES):
                                bank = ps[:, 2 * (u % 2) + h, :c1 - c0]
                                product(bank, lambda a, k: q_head[hd][a][:, cols], lambda a, k: k_head[hd][:, a, c0:c1], 1,
                                        stop=False)
                                r0 = ROPE * hd
                                last = product(bank, lambda a, k: qr_pair[r0:r0 + ROPE, a, cols],
                                               lambda a, k: kr_n[r0:r0 + ROPE, a, c0:c1], 1, start=False)
                            last.then_inc(s_ready, 1)
                        elif what == "T":
                            pe.wait_ge(p_ready, 8 * i + u + 1)
                            pe.wait_ge(t_free, 8 * i + u + 1)
                            for t in range(CKT):
                                last = nc.tensor.transpose(ps[:, 4 + t // 3, (t % 3) * P:(t % 3 + 1) * P],
                                                           p_soft[:, u % 2, t * P:(t + 1) * P], ident[:])
                            last.then_inc(t_ready, 1)
                        else:
                            pe.wait_ge(t_free, 1 + 8 * i + 4 * u + 4)
                            pe.wait_ge(o_free, 2 * i + u + 1)
                            product(ps[:, 6, :LAT], lambda a, k: v_pair[:, a, k, u * VD:(u + 1) * VD],
                                    lambda a, k: p_turned[:, a, k], CKT).then_inc(o_ready, 1)

            pe.wait_ge(cond_done, 1)
            for c in range(MOD_FIRST):
                pe.wait_ge(mod0_in[c], 16)
                for j in range(MOD_W // P):
                    col = 2 * (4 * c + j)
                    for k in range(KT):
                        last = mm(ps[:, 6, col:col + 2], mod_first[c][:, k, j * P:(j + 1) * P], cond[:, 2 * k:2 * k + 2],
                                  start=k == 0, stop=k == KT - 1)
            last.then_inc(mod_sum0, 1)
            pe.wait_ge(consts, 2)
            stat(TAILS[0], ("pre", 0))
            g_total = [0]
            for n, st in enumerate(STAGES):
                for ph in phases(st):
                    kind = ph[0]
                    if kind == "in":
                        in_phase(n, st, ph)
                        if st.kind == "ffn":
                            g_total[0] += 2 * st.nh * ph[3]
                    elif kind == "out":
                        out_phase(n, st, ph)
                    elif kind == "gates":
                        gates(st, ph)
                    elif kind == "latent":
                        latents(n, ph)
                    else:
                        heads(ph)


def rope_tables():
    grid_w, base, quarter = 64, 10000.0, ROPE // 4
    inv_freq = np.float32(base) ** (-np.arange(quarter, dtype=np.float32) / np.float32(quarter))
    t = np.arange(LAT)
    pos = np.stack([t // grid_w, t % grid_w]).astype(np.float32)
    r = np.arange(P) % ROPE
    angle = pos[r // (2 * quarter)] * inv_freq[r % quarter][:, None]
    sign = np.where(r % (2 * quarter) < quarter, -1.0, 1.0)[:, None]
    return np.cos(angle).astype(np.float32), (np.sin(angle) * sign).astype(np.float32)


def kernel(**inputs):
    import numpy as _np
    import concourse.bacc as _bacc
    from concourse import mybir as _mybir
    from concourse.bass_utils import run_bass_kernel_spmd as _run

    a = {k: _np.asarray(v) for k, v in inputs.items()}

    def unit_blocks(w):
        r, c = w.shape
        return w.reshape(r // P, P, c // P, P).transpose(2, 1, 0, 3)

    def units_of(w, at, dst):
        u = unit_blocks(w)
        dst[at:at + u.shape[0], :, :u.shape[2]] = u

    units = _np.zeros((GROUPS * NSLOT, P, KT, P), _np.float32)
    for st in STAGES:
        n = st.group0 * NSLOT
        l, s = "l%d_" % st.layer, st.sub // 2
        if st.kind == "ffn":
            w_in, w_out = a[l + "ffn_w_in"][s], a[l + "ffn_w_out"][s]
            t0 = 0
            for tiles in CHUNKS:
                rows = slice(t0 * P, (t0 + tiles) * P)
                units[n:n + 2 * tiles:2] = unit_blocks(w_in[:, :DFF][:, rows])
                units[n + 1:n + 2 * tiles:2] = unit_blocks(w_in[:, DFF:][:, rows])
                n += 2 * tiles
                units_of(w_out[rows], n, units)
                n += KT
                t0 += tiles
        elif st.kind == "rg":
            w_in = a[l + "rg_w_in"]
            units[n:n + 2 * KT:2] = unit_blocks(w_in[:, :D])
            units[n + 1:n + 2 * KT:2] = unit_blocks(w_in[:, D:])
            n += 2 * KT
            gw = a[l + "rg_gate_w"]
            units[n:n + NSLOT] = gw.transpose(2, 3, 0, 1, 4).reshape(NSLOT, 2, P, 4, P).transpose(0, 2, 1, 3, 4).reshape(
                NSLOT, P, KT, P)
            n += NSLOT
            units_of(a[l + "rg_w_out"], n, units)
        else:
            w_a, w_qb, w_kvb = a[l + "mla_w_a"], a[l + "mla_w_qb"], a[l + "mla_w_kvb"]
            rope = w_a[:, QL + KVL:]
            swap = rope.reshape(D, 2, 2, ROPE // 4)[:, :, ::-1].reshape(D, ROPE)
            units_of(_np.concatenate([w_a[:, QL:QL + KVL], rope, rope, swap, swap, w_a[:, :QL]], 1), n, units)
            n += 2 * NSLOT
            wq = w_qb.reshape(QL, HEADS, QKD)
            wkv = w_kvb.reshape(KVL, HEADS, NOPE + VD)
            for p in range(HEADS // 2):
                units_of(wq[:, 2 * p:2 * p + 2, NOPE:].reshape(QL, 2 * ROPE), n, units)
                for h in range(2):
                    units[n + 1 + h, :, :4] = unit_blocks(wq[:, 2 * p + h, :NOPE])[0]
                    units[n + 1 + h, :, 4:6] = unit_blocks(wkv[:, 2 * p + h, :NOPE])[0]
                v = wkv[:, 2 * p:2 * p + 2, NOPE:].reshape(2, P, 2, VD)
                units[n + 3, :, :4] = v.transpose(1, 0, 2, 3).reshape(P, 4, VD)
                n += NSLOT
            units_of(a[l + "mla_w_o"], n, units)

    def mod_blocks(w):
        return w.reshape(KT, P, -1, MOD_W).transpose(2, 1, 0, 3)

    modw = _np.concatenate([mod_blocks(a["l0_mod_w"]), mod_blocks(a["l1_mod_w"])], 0)
    mod_start = _np.ascontiguousarray(modw[:MOD_FIRST])
    pieces = modw[MOD_FIRST:].reshape(-1, P, 4, 2, MOD_W).transpose(0, 2, 1, 3, 4).reshape(-1, P, 2, MOD_W)

    def cols(v):
        return _np.asarray(v).reshape(-1, P).T

    cond = _np.stack([cols(a["c"]), cols(a["c_ctx"])], 2).reshape(P, 2 * KT)
    vecs = _np.concatenate([cond, cols(a["l0_norm_g"]), cols(a["l1_norm_g"]), cols(a["l0_mod_b"]), cols(a["l1_mod_b"]),
                            cols(a["l0_rg_conv_w"]), cols(a["l0_rg_conv_b"]), cols(a["l0_rg_gate_b"]),
                            cols(a["l0_rg_lambda"]), cols(a["l1_mla_q_norm"]), cols(a["l1_mla_kv_norm"])], 1)
    tokens = _np.concatenate([a["ctx"][0], a["x"][0]], 0)
    x_t = tokens.T.reshape(KT, P, TOK).transpose(1, 0, 2)
    cos, sin = rope_tables()

    nc = _bacc.Bacc("TRN2", target_bir_lowering=False, num_devices=1, dynamic_dma_scratch_size=1024)
    arrays = {}

    def dram(name, value):
        arrays[name] = _np.ascontiguousarray(value)
        return nc.dram_tensor(name, arrays[name].shape, _mybir.dt.float32, kind="ExternalInput").ap()

    out_tok = TOK if STAGES[-1].nh == 2 else LAT
    out_d = nc.dram_tensor("out_t", (KT, P, out_tok), _mybir.dt.float32, kind="ExternalOutput").ap()
    io = (dram("units", units), dram("mod_pieces", pieces), dram("mod_start", mod_start), dram("x_t", x_t),
          dram("vecs_in", vecs), [dram("cos_in", cos), dram("sin_in", sin), dram("ident_in", _np.eye(P, dtype=_np.float32))],
          out_d)
    build(nc, io)
    got = _run(nc, [arrays], core_ids=[0]).results[0]["out_t"]
    return _np.ascontiguousarray(got.reshape(D, out_tok).T[None])
```

```python
import numpy as np
import concourse.bass as bass
from concourse import mybir
from contextlib import ExitStack

F32 = mybir.dt.float32
F32R = mybir.dt.float32r
ALU = mybir.AluOpType
ACT = mybir.ActivationFunctionType
AX = mybir.AxisListType

P = 128
D = 1024
KT = D // P
KP = KT // 2
CTX, LAT = 256, 512
TOK = CTX + LAT
DFF = 2816
FT = DFF // P
CHUNKS = (FT - 16, 8, 8)
HALVES = ((0, TOK // 2), (TOK // 2, TOK))
LATENT = ((CTX, TOK),)
EPS = 1e-6
NSLOT = 4
NRAW = 4
MOD_W = 512
MOD_CHUNKS = 2 * 9 * D // MOD_W
MOD_FIRST = 4
HEADS = 8
NOPE, ROPE, VD = 128, 64, 128
QL, KVL = 512, 256
QKD = NOPE + ROPE
SCALE = float(QKD) ** -0.5
QT = LAT // P
CKT = TOK // P
RG_C = 8.0
CONV = 4

VEC = {}
_at = 0
for _name, _n in (("cond", 16), ("norm_g", 96), ("mod_b", 144), ("conv_w", 32), ("conv_b", 8), ("gate_b", 32),
                  ("lam", 16), ("q_norm", 4), ("kv_norm", 2), ("pick", 2)):
    VEC[_name] = _at
    _at += _n
NVEC = _at


class Stage:

    def __init__(self, kind, layer, sub, halves, group0, in0, out0, mod0):
        self.kind, self.layer, self.sub, self.halves = kind, layer, sub, halves
        self.group0, self.in0, self.out0, self.mod0 = group0, in0, out0, mod0
        self.nh = len(halves)


def plan():
    stages, g, i, o, mod = [], 0, 0, 0, MOD_FIRST
    for kind, layer, sub, halves in (("ffn", 0, 0, HALVES), ("rg", 0, 1, HALVES), ("ffn", 0, 2, HALVES),
                                     ("ffn", 1, 0, HALVES), ("mla", 1, 1, LATENT), ("ffn", 1, 2, LATENT)):
        stages.append(Stage(kind, layer, sub, halves, g, i, o, mod))
        nh = len(halves)
        if kind == "ffn":
            g += FT // 2 + 2 * len(CHUNKS) + nh - 1
            i += FT * nh
            o += KT * nh * len(CHUNKS)
            if layer == 0:
                mod += 16
        elif kind == "rg":
            g += KT // 2 + 1 + 2 + nh - 1
            i += KT * nh
            o += KT * nh
        else:
            g += 2 + HEADS // 2 + 2
            o += KT * nh
    return stages, g


STAGES, GROUPS = plan()


FINAL = [(0, m) for m in range(KT)] + [(1, m) for m in range(KP, KT)] + [(1, m) for m in range(KP)]


class Tail:

    def __init__(self, n, stage, pre, squares, stats, posts, pres):
        self.n, self.stage, self.pre = n, stage, pre
        two = stage is None or stage.nh == 2
        self.halves = HALVES if two else LATENT

        def chain(which, h):
            return [("rs", h, which)] + [(which, h, j) for j in range(KP)]

        if stage is None:
            self.order = [("sq", 0, 0), ("sq", 1, 0)]
            for h in range(2):
                self.order += [("rs", h, "pre")] + [("norm", h, j) for j in range(KP)]
            self.order += [("pre", h, j) for h in range(2) for j in range(KP)]
        elif stage.nh == 2:
            e = [("E", h, m) for h, m in FINAL]
            a, b = chain("post", 0), chain("pre", 0)
            self.order = (e[:9] + a[:2] + e[9:10] + a[2:4] + e[10:11] + a[4:] + e[11:13] + b[:2] + e[13:14] + b[2:3]
                          + e[14:15] + b[3:] + e[15:] + chain("post", 1) + chain("pre", 1))
        else:
            self.order = [("E", 0, m) for m in range(KT)] + chain("post", 0) + chain("pre", 0)
        if not pre:
            self.order = [x for x in self.order if x[0] != "pre" and x[2] != "pre"]
        self.square, self.stat, self.post, self.pre_no, self.sums = {}, {}, {}, {}, {}
        for x in self.order:
            h = x[1]
            if x[0] == "E":
                squares += 1
                self.square[x] = squares
                self.sums["post", h] = squares
            elif x[0] == "rs":
                stats += 1
                self.stat[x[2], h] = stats
                if x[2] == "post":
                    self.post[h] = posts
                    posts += 1
                else:
                    self.pre_no[h] = pres
                    pres += 1
            elif x[0] == "post" and pre and self.direct(h):
                self.sums["pre", h] = KT * (self.post[h] // 2 + 1)
            elif x[0] == "sq" or (x[0] == "post" and pre):
                for m in range(KT) if x[0] == "sq" else (2 * x[2], 2 * x[2] + 1):
                    squares += 1
                    self.square[("x", h, m)] = squares
                self.sums["pre", h] = squares
        self.end = squares, stats, posts, pres

    def direct(self, h):
        return self.stage is not None and self.pre and self.stage.nh == 2 and h == 0


def tails():
    out = [Tail(0, None, True, 0, 0, 0, 0)]
    for n, s in enumerate(STAGES):
        out.append(Tail(n + 1, s, n < len(STAGES) - 1, *out[-1].end))
    return out


TAILS = tails()
MLA_TAIL = 5


def segments(c0, c1):
    out = []
    if c0 < CTX:
        out.append((1, c0, min(c1, CTX)))
    if c1 > CTX:
        out.append((0, max(c0, CTX), c1))
    return out


def build(nc, io):
    ctx = ExitStack()
    with ctx:
        KB = 1024
        X_AT, H_AT, G_AT, Y_AT = 0, 24 * KB, 72 * KB, 120 * KB
        W_AT, RAW_AT, MISC_AT = 144 * KB, 176 * KB, 192 * KB
        base = ((nc.sbuf_base + 63) // 64) * 64

        def at(name, offset, shape, dt=F32):
            return nc.alloc_sbuf_tensor_at(name, [P, *shape], dt, offset=base + offset)

        def sem(name):
            return ctx.enter_context(nc.semaphore(name))

        x_res = at("x_res", X_AT, [KT, TOK])
        h_in = at("h_in", H_AT, [2, KT, TOK], F32R)
        g_act = at("g_act", G_AT, [2, KT, TOK], F32R)
        y_acc = at("y_acc", Y_AT, [KT, TOK])
        w_slot = at("w_slot", W_AT, [NSLOT, 2, KT, P], F32R)
        raw = at("raw", RAW_AT, [NSLOT, KT, P])
        mod_raw = at("mod_raw", MISC_AT, [2, 2, MOD_W])
        mod_acc = at("mod_acc", MISC_AT + 8 * KB, [2, MOD_W])
        act_tmp = at("act_tmp", MISC_AT + 12 * KB, [2, 512])
        dve_tmp = at("dve_tmp", MISC_AT + 16 * KB, [2, 512])
        sum_sq = at("sum_sq", MISC_AT + 20 * KB, [TOK])
        rstd = at("rstd", MISC_AT + 23 * KB, [512])
        small_at = [MISC_AT + 25 * KB]

        def small(name, *shape):
            offset = small_at[0]
            small_at[0] += (4 * int(np.prod(shape)) + 31) // 32 * 32
            return at(name, offset, shape)

        vecs = small("vecs", NVEC)
        mods = small("mods", 2, 2 * 72)
        cond = small("cond", 16)
        post_gain = small("post_gain", 2, KT)
        pre_gain = small("pre_gain", 2, KT)
        decay = small("decay", 2, 16)
        eps_col = small("eps_col", 1)
        soft_max = small("soft_max", 2, 4)
        soft = small("soft", 6, 16)
        ones = small("ones", P)
        ident = small("ident", P)
        assert base + small_at[0] <= nc.sbuf_usable_end

        x_sq = at("x_sq", MISC_AT, [KT, TOK // 2])

        mod_first_g = at("mod_first_g", G_AT, [MOD_FIRST - 1, KT, MOD_W])
        mod_first_h = at("mod_first_h", H_AT + 24 * KB, [KT, MOD_W])
        mod_first = [mod_first_g[:, n] for n in range(MOD_FIRST - 1)] + [mod_first_h[:]]
        mod_row = at("mod_row", MISC_AT, [MOD_FIRST, MOD_W])

        rg_yu = at("rg_yu", G_AT, [2, KT, TOK])
        rg_uc = at("rg_uc", Y_AT, [KT, TOK])
        rg_m = g_act
        rg_split = at("rg_split", H_AT, [2, 2, TOK], F32R)
        rg_work = at("rg_work", H_AT + 12 * KB, [2, 2, 3, TOK])

        cq_raw = at("cq_raw", G_AT + 16 * KB, [4, LAT])
        ckv_raw = at("ckv_raw", G_AT + 24 * KB, [2, TOK])
        kr_raw = at("kr_raw", G_AT + 30 * KB, [TOK])
        kr_swap = at("kr_swap", G_AT + 33 * KB, [LAT])
        mla_sq = at("mla_sq", G_AT + 35 * KB, [2, LAT])
        cq_n = at("cq_n", G_AT, [2, 4, LAT], F32R)
        att_o = at("att_o", G_AT + 16 * KB, [2, HEADS, LAT], F32R)
        ckv_n = at("ckv_n", Y_AT, [2, 2, TOK], F32R)
        kr_n = at("kr_n", Y_AT + 12 * KB, [2, TOK], F32R)
        k_head = [at("k_head0", Y_AT + 18 * KB, [2, TOK], F32R), at("k_head1", H_AT + 40 * KB, [2, TOK], F32R)]
        v_pair = at("v_pair", H_AT, [2, CKT, 2 * VD], F32R)
        p_turned = at("p_turned", H_AT + 12 * KB, [2, CKT, LAT], F32R)
        q_head = [[at("q_head0h", H_AT + 36 * KB, [LAT], F32R), at("q_head0l", H_AT + 38 * KB, [LAT], F32R)],
                  [at("q_head1h", H_AT + 46 * KB, [LAT], F32R), at("q_head1l", MISC_AT + 18 * KB, [LAT], F32R)]]
        p_soft = at("p_soft", MISC_AT + 12 * KB, [2, TOK])
        cos_t = at("cos_t", MISC_AT, [LAT])
        sin_t = at("sin_t", MISC_AT + 2 * KB, [LAT])
        qr_pair = at("qr_pair", MISC_AT + 4 * KB, [2, LAT], F32R)
        rot_tmp = at("rot_tmp", MISC_AT + 8 * KB, [2, LAT])

        ps = ctx.enter_context(nc.psum_tensor("ps", [P, 8, 512], F32))
        STAT, MODB = 7, 7

        vec_in = sem("vec_in")
        x_in = sem("x_in")
        mod0_in = [sem(f"mod0_in{n}") for n in range(4)]
        raw_in = [sem(f"raw_in{n}") for n in range(NSLOT)]
        w_hi = sem("w_hi")
        w_lo = sem("w_lo")
        modp_in = [sem(f"modp_in{n}") for n in range(2)]
        modp_free = sem("modp_free")
        mod_step = sem("mod_step")
        mod_sum = sem("mod_sum")
        mod_done = sem("mod_done")
        consts = sem("consts")
        row_ready = sem("row_ready")
        row_copied = sem("row_copied")
        mod_sum0 = sem("mod_sum0")
        cond_done = sem("cond_done")
        in_ready = sem("in_ready")
        pair_act = sem("pair_act")
        in_free = sem("in_free")
        g_hi = sem("g_hi")
        g_free = sem("g_free")
        out_ready = sem("out_ready")
        out_free = sem("out_free")
        sq_done = sem("sq_done")
        xsq_done = sem("xsq_done")
        ss_added = sem("ss_added")
        ss_zero = sem("ss_zero")
        stat_ready = sem("stat_ready")
        ln_done = sem("ln_done")
        rs_ready = sem("rs_ready")
        gain_done = sem("gain_done")
        y_normed = sem("y_normed")
        x_upd = sem("x_upd")
        x_normed = sem("x_normed")
        h_f32 = sem("h_f32")
        h_hi = sem("h_hi")
        h_lo = sem("h_lo")
        soft_step = sem("soft_step")
        soft_exp = sem("soft_exp")
        conv_step = sem("conv_step")
        uc_hi, uc_lo = sem("uc_hi"), sem("uc_lo")
        gate_ready = sem("gate_ready")
        sig_done = sem("sig_done")
        expd = sem("expd")
        coef_done = sem("coef_done")
        iu_done = sem("iu_done")
        rg_step = sem("rg_step")
        m_hi, m_lo = sem("m_hi"), sem("m_lo")
        rope_in = sem("rope_in")
        lat_ready = sem("lat_ready")
        lat_read = sem("lat_read")
        lat_sq, lat_step = sem("lat_sq"), sem("lat_step")
        lat_sum, lat_ln, lat_rs = sem("lat_sum"), sem("lat_ln"), sem("lat_rs")
        lat_hi, lat_lo = sem("lat_hi"), sem("lat_lo")
        kr_step = sem("kr_step")
        prj_ready, prj_hi, prj_free = sem("prj_ready"), sem("prj_hi"), sem("prj_free")
        qr_step = sem("qr_step")
        s_ready, s_max, s_exp, p_ready = sem("s_ready"), sem("s_max"), sem("s_exp"), sem("p_ready")
        p_rcp = sem("p_rcp")
        t_ready, t_hi, t_free = sem("t_ready"), sem("t_hi"), sem("t_free")
        o_ready, o_hi, o_free = sem("o_ready"), sem("o_hi"), sem("o_free")
        out_sent = sem("out_sent")

        units, mod_pieces, mod_start, x_t, vec_d, rope_d, out_d = io
        block = ctx.enter_context(nc.Block())

        def mod_at(layer, sub, what):
            return layer * 72 + (sub * 3 + what) * KT

        def gain_at(layer, row):
            return VEC["norm_g"] + (layer * 6 + row) * KT

        def wait_pos(eng, s, value):
            if value > 0:
                eng.wait_ge(s, value)

        def phases(st):
            if st.kind == "ffn":
                out, g, i, o = [], st.group0, st.in0, st.out0
                for c, tiles in enumerate(CHUNKS):
                    out.append(("in", c, g, tiles // 2, i))
                    g += tiles // 2
                    i += tiles * st.nh
                    count = 1 + st.nh if c == len(CHUNKS) - 1 else 2
                    out.append(("out", c, g, count, o))
                    g += count
                    o += KT * st.nh
                return out
            if st.kind == "rg":
                g = st.group0
                return [("in", 0, g, KT // 2, st.in0), ("gates", 0, g + KT // 2, 1, 0),
                        ("out", 0, g + KT // 2 + 1, 3, st.out0)]
            g = st.group0
            return [("latent", 0, g, 2, 0), ("heads", 0, g + 2, HEADS // 2, 0),
                    ("out", 0, g + 2 + HEADS // 2, 2, st.out0)]

        def last_out(st):
            return phases(st)[-1]

        def mods_before(st):
            return 1 + st.mod0 - MOD_FIRST + 15

        def carries_mods(st):
            return st.kind == "ffn" and st.layer == 0

        def has_mods(st, ph):
            return st.kind == "ffn" and st.layer == 0 and ph[0] == "in" and ph[1] > 0

        def mod_chunk0(st, ph):
            return st.mod0 - MOD_FIRST + 8 * (ph[1] - 1)

        BANKS = {2: (4, 5, 6, 4, 5, 6, 4, 5), 1: (4, 5, 6, 5)}
        BACK = {2: (2, 2, 3, 3, 3, 3, 3, 3), 1: (3, 2, 3, 2)}

        CONV_STEPS, RG_STEPS = 7, 9

        def pair_bank(st, x, first):
            return 4 if first and x == 2 and st.kind == "ffn" and st.nh == 2 else 2 * (x % 2)

        def out_bank(st, x):
            return BANKS[st.nh][x % len(BANKS[st.nh])]

        def out_item(st, x):
            return last_out(st)[4] + (FINAL.index(x[1:]) if st.nh == 2 else x[2])

        def split_behind(st, x):
            j = out_item(st, x) - last_out(st)[4]
            if st.nh == 2:
                step = {0: 1, 2: 2, 3: 3}.get(j // 4)
            else:
                step = j // 4 + 1
            if step is None or last_out(st)[2] + step >= GROUPS:
                return None
            return last_out(st)[2] + step, j % 4

        def latent_norms():
            out = []
            for h in range(2):
                c0, c1 = HALVES[h]
                out.append(([(ckv_raw[:, t, c0:c1], 3 * h + t + 1) for t in range(2)], VEC["kv_norm"], c1 - c0, KVL))
            out.append(([(cq_raw[:, t], 7 + t + 1) for t in range(4)], VEC["q_norm"], LAT, QL))
            return out

        def rg_pool(m, split_lo, g):
            pool = nc.gpsimd
            if m == 0:
                rg_split_lo(0)
                rg_split_lo(1)
            for d in range(2):
                pool.wait_ge(sig_done, 2 * m + d + 1)
                gate = rg_work[:, m % 2, d, 1]
                pool.tensor_tensor(gate, gate, rg_uc[:, m], ALU.mult).then_inc(iu_done, 1)
            if m % 2 == 1:
                split_lo(g + 1, m // 2)
            pool.wait_ge(m_hi, m + 1)
            pool.tensor_tensor(rg_m[:, 1, m], rg_work[:, m % 2, 0, 0], rg_m[:, 0, m].bitcast(F32),
                               ALU.subtract).then_inc(m_lo, 1)
            if m + 2 < KT:
                rg_split_lo(m + 2)

        def rg_split_lo(m):
            pool = nc.gpsimd
            pool.wait_ge(uc_hi, m + 1)
            pool.tensor_tensor(rg_split[:, m % 2, 1], rg_uc[:, m], rg_split[:, m % 2, 0].bitcast(F32),
                               ALU.subtract).then_inc(uc_lo, 1)

        def latent_splits():
            out = []
            for h in range(2):
                c0, c1 = HALVES[h]
                for t in range(2):
                    out.append((ckv_n[:, :, t, c0:c1], ckv_raw[:, t, c0:c1]))
            for t in range(4):
                out.append((cq_n[:, :, t], cq_raw[:, t]))
            return out

        def mla_latent_pool(split_lo, g):
            pool = nc.gpsimd
            for q in range(NSLOT):
                split_lo(g + 1, q)
            pool.wait_ge(lat_hi, 1)
            pool.tensor_tensor(kr_n[:, 1], kr_raw[:], kr_n[:, 0].bitcast(F32), ALU.subtract).then_inc(lat_lo, 1)
            for n, (dst, src) in enumerate(latent_splits()):
                if n == 4:
                    for q in range(NSLOT):
                        split_lo(g + 2, q)
                pool.wait_ge(lat_hi, n + 2)
                pool.tensor_tensor(dst[:, 1], src, dst[:, 0].bitcast(F32), ALU.subtract).then_inc(lat_lo, 1)

        @block.sync
        def _(sp):
            sp.dma_start(vecs[:], vec_d).then_inc(vec_in, 16)
            sp.dma_start(x_res[:], x_t).then_inc(x_in, 16)
            for c in range(MOD_FIRST):
                sp.dma_start(mod_first[c], mod_start[c]).then_inc(mod0_in[c], 16)

            def load_unit(group, q):
                if not (isinstance(group, int) and group == 0):
                    sp.wait_ge(w_lo, (group - 1) * NSLOT + q + 1)
                sp.dma_start(raw[:, q], units[bass.ds(group * NSLOT + q, 1)]).then_inc(raw_in[q], 16)

            for q in range(NSLOT):
                load_unit(0, q)
            for st in STAGES:
                for ph in phases(st):
                    kind, c, g, count, _ = ph
                    if kind == "latent":
                        sp.wait_ge(mod_done, MOD_CHUNKS - MOD_FIRST + 1)
                        sp.wait_ge(stat_ready, TAILS[STAGES.index(st)].stat["pre", 0])
                        for dst, src in zip((cos_t, sin_t, ident), rope_d):
                            sp.dma_start(dst[:], src).then_inc(rope_in, 16)
                    last = g + count == GROUPS
                    n = count - last
                    with sp.Fori(0, n) as i:
                        if not has_mods(st, ph):
                            for q in range(NSLOT):
                                load_unit(g + 1 + i, q)
                            continue
                        for j in range(8):
                            piece = 4 * mod_chunk0(st, ph) + 8 * i + j
                            sp.wait_ge(modp_free, piece + 1)
                            sp.dma_start(mod_raw[:, j % 2], mod_pieces[bass.ds(piece, 1)]).then_inc(modp_in[j % 2], 16)
                            if 1 <= j <= NSLOT:
                                load_unit(g + 1 + i, j - 1)
            st = STAGES[-1]
            tail = TAILS[len(STAGES)]
            n = 0
            for h in range(st.nh):
                c0, c1 = st.halves[h]
                for m in range(KT):
                    sp.wait_ge(x_upd, KT * tail.post[h] + m + 1)
                    sp.dma_start(out_d[m, :, c0 - (TOK - out_d.shape[2]):c1 - (TOK - out_d.shape[2])],
                                 x_res[:, m, c0:c1]).then_inc(out_sent, 16)
                    n += 16
            sp.wait_ge(out_sent, n)

        @block.gpsimd
        def _(pool):
            nc.gpsimd.memset(ones[:], 1.0).then_inc(consts, 1)
            nc.gpsimd.memset(eps_col[:], EPS).then_inc(consts, 1)
            nc.gpsimd.memset(sum_sq[:], 0.0).then_inc(ss_zero, 1)

            def split_lo(group, q):
                pool.wait_ge(w_hi, group * NSLOT + q + 1)
                nc.gpsimd.tensor_tensor(w_slot[:, q, 1], raw[:, q], w_slot[:, q, 0].bitcast(F32),
                                        ALU.subtract).then_inc(w_lo, 1)

            def add_square(number, c0, c1):
                pool.wait_ge(sq_done, number)
                wait_pos(pool, ss_added, number - 1)
                nc.gpsimd.tensor_tensor(sum_sq[:, c0:c1], sum_sq[:, c0:c1], act_tmp[:, (number - 1) % 2, :c1 - c0],
                                        ALU.add).then_inc(ss_added, 1)

            cleared = [1]

            def clear_sums(stat, c0, c1):
                cleared[0] += 1
                pool.wait_ge(stat_ready, stat)
                nc.gpsimd.memset(sum_sq[:, c0:c1], 0.0).then_inc(ss_zero, 1)
                pool.wait_ge(ss_zero, cleared[0])

            def tail_steps(tail):
                if tail.n == 0:
                    pool.wait_ge(ss_zero, 1)
                for x in tail.order:
                    h = x[1]
                    c0, c1 = tail.halves[h]
                    if x[0] == "E":
                        add_square(tail.square[x], c0, c1)
                        unit = split_behind(tail.stage, x)
                        late = x in (("E", 1, 2), ("E", 1, 3)) and unit
                        if unit and not late:
                            split_lo(*unit)
                        if late and x[2] == 3:
                            for q in (2, 3):
                                split_lo(unit[0], q)
                    elif x[0] == "rs":
                        if tail.pre and not (x[2] == "pre" and tail.direct(h)):
                            clear_sums(tail.stat[x[2], h], c0, c1)
                    elif x[0] == "pre":
                        j = x[2]
                        pool.wait_ge(h_hi, KP * tail.pre_no[h] + j + 1)
                        nc.gpsimd.tensor_tensor(h_in[:, 1, 2 * j:2 * j + 2, c0:c1], y_acc[:, 2 * j:2 * j + 2, c0:c1],
                                                h_in[:, 0, 2 * j:2 * j + 2, c0:c1].bitcast(F32),
                                                ALU.subtract).then_inc(h_lo, 1)
                        if tail.stage is None and (h, j) == (0, KP - 1):
                            split_lo(0, 2)
                            split_lo(0, 3)
                    elif x[0] == "norm":
                        if x[1:] == (1, KP - 1):
                            split_lo(0, 0)
                            split_lo(0, 1)
                    elif tail.pre and not tail.direct(h):
                        for m in range(KT) if x[0] == "sq" else (2 * x[2], 2 * x[2] + 1):
                            add_square(tail.square[("x", h, m)], c0, c1)

            g_items = 0
            tail_steps(TAILS[0])
            for n, st in enumerate(STAGES):
                for ph in phases(st):
                    kind, c, g, count, item0 = ph
                    per = 2 * st.nh
                    if kind == "in" and st.kind == "ffn":
                        with pool.Fori(0, count) as i:
                            for x in range(per):
                                t, (c0, c1) = x % 2, st.halves[x // 2]
                                pool.wait_ge(g_hi, g_items + per * i + x + 1)
                                dst = g_act[:, :, bass.ds(2 * i + t, 1), c0:c1]
                                nc.gpsimd.tensor_tensor(dst[:, 1], dve_tmp[:, x % 2:x % 2 + 1, :c1 - c0], dst[:, 0].bitcast(F32),
                                                        ALU.subtract).then_inc(g_free, 1)
                                for q in ((0, 1), (2, 3))[x % 2] if x >= per - 2 else ():
                                    split_lo(g + i + 1, q)
                        g_items += per * count
                    elif kind == "in":
                        with pool.Fori(0, count) as i:
                            for q in range(NSLOT):
                                split_lo(g + i + 1, q)
                    elif kind == "gates":
                        for m in range(KT):
                            rg_pool(m, split_lo, g)
                    elif kind == "latent":
                        mla_latent_pool(split_lo, g)
                    elif kind == "heads":
                        with pool.Fori(0, count) as i:
                            for q in range(NSLOT):
                                split_lo(g + i + 1, q)
                    elif ph != last_out(st):
                        with pool.Fori(0, count) as i:
                            for q in range(NSLOT):
                                split_lo(g + i + 1, q)
                tail_steps(TAILS[n + 1])

        PAIR = [("S", 0), ("S", 1), ("T", 0), ("S", 2), ("T", 1), ("S", 3), ("T", 2), ("S", 4), ("T", 3), ("S", 5),
                ("V", 0), ("T", 4), ("S", 6), ("T", 5), ("S", 7), ("T", 6), ("T", 7), ("V", 1)]
        PROJ = ([("qr", 0, 0)] + [x for h in range(2) for x in (("q", h, 0), ("k", h, 0), ("k", h, 1))]
                + [("v", t, 0) for t in range(CKT)])

        def proj_dst(kind, n, half):
            if kind == "q":
                return q_head[n][0][:], q_head[n][1][:]
            if kind == "k":
                c0, c1 = HALVES[half]
                return k_head[n][:, 0, c0:c1], k_head[n][:, 1, c0:c1]
            return v_pair[:, 0, n], v_pair[:, 1, n]

        def turned(u):
            src = ps[:, 4:6, :3 * P].rearrange("p b (t q) -> p b t q", t=3)
            c = (u % QT) * P
            dst = [p_turned[:, n, :, c:c + P].rearrange("p (b t) q -> p b t q", b=2) for n in range(2)]
            return src, dst

        @block.scalar
        def _(act):
            def split_hi(group, q):
                act.wait_ge(raw_in[q], 16 * (group + 1))
                nc.scalar.activation(w_slot[:, q, 0], raw[:, q], ACT.Copy).then_inc(w_hi, 1)

            def square(number, src, n):
                wait_pos(act, ss_added, number - 2)
                nc.scalar.activation(act_tmp[:, (number - 1) % 2, :n], src, ACT.Square).then_inc(sq_done, 1)

            def rsqrt_mean(stat, n):
                act.wait_ge(stat_ready, stat)
                nc.scalar.activation(rstd[:, :n], ps[:, STAT, :n], ACT.Ln, bias=eps_col[:], scale=1.0 / D).then_inc(ln_done, 1)
                act.wait_ge(ln_done, stat)
                nc.scalar.activation(rstd[:, :n], rstd[:, :n], ACT.Exp, scale=-0.5).then_inc(rs_ready, 1)

            def tail_steps(tail):
                st = tail.stage
                if st is not None and st.kind == "ffn":
                    act.wait_ge(in_free, 2 + st.in0 + FT * st.nh)
                for x in tail.order:
                    h = x[1]
                    c0, c1 = tail.halves[h]
                    n = c1 - c0
                    if x[0] == "E":
                        act.wait_ge(out_free, 3 + out_item(st, x) + 1)
                        square(tail.square[x], y_acc[:, x[2], c0:c1], n)
                        unit = split_behind(st, x)
                        if unit:
                            split_hi(*unit)
                    elif x[0] == "rs":
                        if st is None and h == 1:
                            act.wait_ge(x_normed, KP)
                        rsqrt_mean(tail.stat[x[2], h], n)
                    elif x[0] == "pre":
                        j = x[2]
                        act.wait_ge(h_f32, KP * tail.pre_no[h] + j + 1)
                        nc.scalar.activation(h_in[:, 0, 2 * j:2 * j + 2, c0:c1], y_acc[:, 2 * j:2 * j + 2, c0:c1],
                                             ACT.Copy).then_inc(h_hi, 1)
                        if st is None and (h, j) == (0, KP - 1):
                            split_hi(0, 2)
                            split_hi(0, 3)
                    elif x[0] == "norm":
                        if x[1:] == (1, KP - 1):
                            for c in range(MOD_FIRST):
                                if c == MOD_FIRST - 1:
                                    split_hi(0, 0)
                                    split_hi(0, 1)
                                act.wait_ge(row_ready, c + 1)
                                nc.scalar.activation(mod_row[0:2, c], ps[0:2, c, :MOD_W], ACT.Copy).then_inc(row_copied, 1)
                    elif x[0] == "sq":
                        act.wait_ge(x_in, 16)
                        for m in range(KT):
                            square(tail.square[("x", h, m)], x_res[:, m, c0:c1], n)
                    elif tail.pre:
                        for m in (2 * x[2], 2 * x[2] + 1):
                            act.wait_ge(x_upd, KT * tail.post[h] + m + 1)
                            if tail.direct(h):
                                nc.scalar.activation(x_sq[:, m], x_res[:, m, c0:c1], ACT.Square).then_inc(xsq_done, 1)
                                continue
                            square(tail.square[("x", h, m)], x_res[:, m, c0:c1], n)

            def ffn_in(st, c, g, count, item0, g0):
                per = 2 * st.nh

                def group(i, first):
                    for x in range(per):
                        t, (c0, c1) = x % 2, st.halves[x // 2]
                        item = item0 + per * i + x
                        act.wait_ge(in_ready, item + 1)
                        act.wait_ge(in_free, item + 1)
                        nc.scalar.activation(act_tmp[:, t, :c1 - c0], ps[:, pair_bank(st, x, first), :c1 - c0],
                                             ACT.Silu).then_inc(pair_act, 1)
                        act.wait_ge(in_free, item + 3)
                        nc.scalar.activation(g_act[:, 0, bass.ds(2 * i + t, 1), c0:c1], dve_tmp[:, t:t + 1, :c1 - c0],
                                             ACT.Copy).then_inc(g_hi, 1)
                        for q in ((0, 1), (2, 3))[x % 2] if x >= per - 2 else ():
                            split_hi(g + i + 1, q)

                if c == 0:
                    group(0, True)
                with act.Fori(1 if c == 0 else 0, count) as i:
                    group(i, False)

            def out_loop(st, g, count, item0):
                nh = st.nh
                with act.Fori(0, count) as i:
                    for q in range(NSLOT):
                        act.wait_ge(out_ready, item0 + 4 * nh * i + 4 * (nh - 1) + q + 1)
                        split_hi(g + i + 1, q)

            def rg(st, ph):
                kind, c, g, count, item0 = ph
                if kind == "in":
                    with act.Fori(0, count) as i:
                        for x in range(4):
                            t, (c0, c1) = x % 2, st.halves[x // 2]
                            act.wait_ge(in_ready, item0 + 4 * i + x + 1)
                            nc.scalar.activation(rg_yu[:, 0, bass.ds(2 * i + t, 1), c0:c1], ps[:, 2 * t:2 * t + 1, :c1 - c0],
                                                 ACT.Gelu_apprx_tanh).then_inc(pair_act, 1)
                            for q in ((0, 1), (2, 3))[t] if x >= 2 else ():
                                split_hi(g + i + 1, q)
                elif kind == "gates":
                    for m in range(KT):
                        if m >= 2:
                            act.wait_ge(m_lo, m - 1)
                        for d in range(2):
                            act.wait_ge(gate_ready, 2 * m + d + 1)
                            for k in range(2):
                                col = VEC["gate_b"] + (d * 2 + k) * KT + m
                                ins = nc.scalar.activation(
                                    rg_work[:, m % 2, d, k].rearrange("p (h c) -> p h c", h=2),
                                    ps[:, 4 * d + 2 * k:4 * d + 2 * k + 2, :TOK // 2], ACT.Sigmoid,
                                    bias=vecs[:, col:col + 1])
                            ins.then_inc(sig_done, 1)
                        if m % 2 == 1:
                            split_hi(g + 1, m // 2)
                        act.wait_ge(sig_done, 2 * m + 2)
                        for d in range(2):
                            w = rg_work[:, m % 2, d]
                            col = d * KT + m
                            nc.scalar.activation(w[:, 2], w[:, 0], ACT.Exp, scale=decay[:, 0, col:col + 1]).then_inc(expd, 1)
                        for d in range(2):
                            w = rg_work[:, m % 2, d]
                            col = d * KT + m
                            nc.scalar.activation(w[:, 0], w[:, 0], ACT.Tanh, scale=decay[:, 1, col:col + 1]).then_inc(expd, 1)
                        for d in range(2):
                            act.wait_ge(expd, 4 * m + 3 + d)
                            w = rg_work[:, m % 2, d]
                            nc.scalar.activation(w[:, 0], w[:, 0], ACT.Sqrt).then_inc(coef_done, 1)

            def mla(st, ph):
                kind, c, g, count, _ = ph
                if kind == "latent":
                    for q in range(NSLOT):
                        act.wait_ge(lat_ready, q + 4)
                        split_hi(g + 1, q)
                    sums = 0
                    norms = latent_norms()
                    for n, (src, gains, cols, size) in enumerate(norms):
                        for x in src:
                            sums += 1
                            act.wait_ge(lat_read, x[1])
                            wait_pos(act, lat_sum, sums - 2)
                            nc.scalar.activation(mla_sq[:, (sums - 1) % 2, :cols], x[0], ACT.Square).then_inc(lat_sq, 1)
                        if n == 0:
                            act.wait_ge(kr_step, 3)
                            act.wait_ge(lat_read, 6)
                            nc.scalar.activation(kr_n[:, 0], kr_raw[:], ACT.Copy).then_inc(lat_hi, 1)
                        if n == 2:
                            for q in range(NSLOT):
                                act.wait_ge(lat_ready, 8 + q)
                                split_hi(g + 2, q)
                        act.wait_ge(lat_sum, sums)
                        nc.scalar.activation(rstd[:, :cols], ps[:, 6, :cols], ACT.Ln, bias=eps_col[:],
                                             scale=1.0 / size).then_inc(lat_ln, 1)
                        act.wait_ge(lat_ln, n + 1)
                        nc.scalar.activation(rstd[:, :cols], rstd[:, :cols], ACT.Exp, scale=-0.5).then_inc(lat_rs, 1)
                        for k, x in enumerate(src):
                            act.wait_ge(lat_step, sums - len(src) + k + 1)
                            dst = latent_splits()[sums - len(src) + k][0]
                            nc.scalar.activation(dst[:, 0], x[0], ACT.Copy).then_inc(lat_hi, 1)
                    return
                with act.Fori(0, count) as i:
                    for n, (what, a, half) in enumerate(PROJ):
                        if what == "qr":
                            act.wait_ge(qr_step, 4 * i + 4)
                            nc.scalar.activation(qr_pair[:, 0], rot_tmp[:, 0], ACT.Copy).then_inc(prj_hi, 1)
                            continue
                        width = {"q": LAT, "k": TOK // 2, "v": 2 * VD}[what]
                        act.wait_ge(prj_ready, len(PROJ) * i + n + 1)
                        nc.scalar.activation(proj_dst(what, a, half)[0], ps[:, n % 4, :width], ACT.Copy).then_inc(prj_hi, 1)
                    for q in range(NSLOT):
                        split_hi(g + i + 1, q)
                    for what, u in PAIR:
                        if what == "S":
                            act.wait_ge(t_ready, 8 * i + u + 1)
                            act.wait_ge(s_max, 16 * i + 2 * u + 2)
                            nc.scalar.activation(p_soft[:, u % 2].rearrange("p (b c) -> p b c", b=2),
                                                 ps[:, 2 * (u % 2):2 * (u % 2) + 2, :TOK // 2], ACT.Exp,
                                                 bias=soft_max[:, u % 2, 1:2], scale=SCALE,
                                                 accum_out=soft_max[:, u % 2, 2:3]).then_inc(s_exp, 1)
                        elif what == "T":
                            act.wait_ge(t_ready, 8 * i + u + 3)
                            src, dst = turned(u)
                            nc.scalar.activation(dst[0], src, ACT.Copy).then_inc(t_hi, 1)
                        else:
                            act.wait_ge(o_ready, 2 * i + u + 1)
                            nc.scalar.activation(att_o[:, 0, bass.ds(2 * i + u, 1)], ps[:, 6:7, :LAT], ACT.Copy).then_inc(o_hi, 1)

            act.wait_ge(vec_in, 16)
            nc.scalar.activation(cond[:], vecs[:, VEC["cond"]:VEC["cond"] + 16], ACT.Silu).then_inc(cond_done, 1)
            act.wait_ge(soft_step, 1)
            nc.scalar.activation(soft[:, 1], soft[:, 0], ACT.Exp).then_inc(soft_exp, 1)
            act.wait_ge(consts, 2)
            tail_steps(TAILS[0])
            g_items = 0
            for n, st in enumerate(STAGES):
                if st.kind == "ffn":
                    wait_pos(act, ss_added, TAILS[n].end[0])
                for ph in phases(st):
                    kind, c, g, count, item0 = ph
                    if st.kind == "rg" and kind != "out":
                        rg(st, ph)
                    elif st.kind == "mla" and kind != "out":
                        mla(st, ph)
                    elif kind == "in":
                        ffn_in(st, c, g, count, item0, g_items)
                        g_items += 2 * st.nh * count
                    elif ph != last_out(st):
                        out_loop(st, g, count, item0)
                tail_steps(TAILS[n + 1])

        @block.vector
        def _(dve):
            v = nc.vector
            dve.sem_inc(in_free, 2)
            dve.sem_inc(out_free, 3)
            dve.sem_inc(g_free, 2)
            dve.sem_inc(modp_free, 2)
            dve.sem_inc(t_ready, 2)
            dve.sem_inc(s_exp, 2)
            dve.sem_inc(t_free, 1)
            dve.sem_inc(o_free, 1)
            soft_n = [0]

            def soft_link(ins):
                soft_n[0] += 1
                ins.then_inc(soft_step, 1)
                dve.wait_ge(soft_step, soft_n[0])

            def softplus():
                z, e, s, s2, acc = (soft[:, n] for n in range(5))
                lam = vecs[:, VEC["lam"]:VEC["lam"] + 16]
                v.tensor_scalar(acc, lam, -1.0, None, ALU.mult).then_inc(soft_exp, 1)
                dve.wait_ge(soft_exp, 1)
                soft_link(v.tensor_tensor(z, lam, acc, ALU.min))
                dve.wait_ge(soft_exp, 2)
                soft_link(v.tensor_scalar(s, e, 2.0, None, ALU.add))
                soft_link(v.reciprocal(s, s))
                soft_link(v.tensor_tensor(s, s, e, ALU.mult))
                soft_link(v.tensor_tensor(s2, s, s, ALU.mult))
                soft_link(v.tensor_scalar(e, s2, 1.0 / 15, 1.0 / 13, ALU.mult, ALU.add))
                for k in (11, 9, 7, 5, 3, 1):
                    soft_link(v.tensor_tensor(e, e, s2, ALU.mult))
                    soft_link(v.tensor_scalar(e, e, 1.0 / k, None, ALU.add))
                soft_link(v.tensor_tensor(e, e, s, ALU.mult))
                soft_link(v.tensor_scalar(acc, acc, 0.0, None, ALU.max))
                soft_link(v.scalar_tensor_tensor(e, e, 2.0, acc, ALU.mult, ALU.add))
                soft_link(v.tensor_scalar(decay[:, 0], e, -RG_C, None, ALU.mult))
                soft_link(v.tensor_scalar(decay[:, 1], e, RG_C / 2, None, ALU.mult))

            gains = [0]

            def gain_link(ins):
                gains[0] += 1
                ins.then_inc(gain_done, 1)

            def make_gains(tail):
                st = tail.stage
                if st is not None:
                    w = 0.5 if st.kind == "ffn" else 1.0
                    a, b = mod_at(st.layer, st.sub, 2), gain_at(st.layer, 2 * st.sub + 1)
                    for k in range(2):
                        gain_link(v.scalar_tensor_tensor(post_gain[:, k], mods[:, k, a:a + KT], w, vecs[:, b:b + KT],
                                                         ALU.mult, ALU.mult))
                if tail.pre:
                    nx = STAGES[tail.n]
                    a, b = mod_at(nx.layer, nx.sub, 1), gain_at(nx.layer, 2 * nx.sub)
                    for k in range(2):
                        gain_link(v.scalar_tensor_tensor(pre_gain[:, k], mods[:, k, a:a + KT], 1.0, vecs[:, b:b + KT],
                                                         ALU.add, ALU.mult))
                dve.wait_ge(gain_done, gains[0])

            def evict(item, dst, bank, n, first):
                dve.wait_ge(out_ready, item + 1)
                if first:
                    v.tensor_copy(dst, bank).then_inc(out_free, 1)
                else:
                    v.tensor_tensor(dst, bank, dst, ALU.add).then_inc(out_free, 1)

            def tail_steps(tail):
                st = tail.stage
                if st is not None:
                    make_gains(tail)
                for x in tail.order:
                    h = x[1]
                    c0, c1 = tail.halves[h]
                    n = c1 - c0
                    segs = segments(c0, c1)
                    pair = y_acc[:, 2 * x[2]:2 * x[2] + 2, c0:c1] if x[0] in ("post", "norm", "pre") else None
                    scale = rstd[:, :n].unsqueeze(1).to_broadcast([P, 2, n])
                    if x[0] == "E":
                        item = out_item(st, x)
                        evict(item, y_acc[:, x[2], c0:c1], ps[:, out_bank(st, item - last_out(st)[4]), :n], n,
                              st.kind != "ffn")
                        if carries_mods(st) and x == ("E", 0, 2):
                            mod_finish(st.mod0 - MOD_FIRST + 15)
                            dve.wait_ge(mod_done, mods_before(st) + 1)
                    elif x[0] == "rs":
                        dve.wait_ge(rs_ready, tail.stat[x[2], h])
                        if x[2] == "pre" and st is None:
                            dve.wait_ge(x_in, 16)
                    elif x[0] == "post":
                        v.tensor_tensor(pair, pair, scale, ALU.mult).then_inc(y_normed, 1)
                        dve.wait_ge(y_normed, KP * tail.post[h] + x[2] + 1)
                        for m in (2 * x[2], 2 * x[2] + 1):
                            for k, a, b in segs:
                                ins = v.scalar_tensor_tensor(x_res[:, m, a:b], y_acc[:, m, a:b],
                                                             post_gain[:, k, m:m + 1], x_res[:, m, a:b], ALU.mult, ALU.add)
                            ins.then_inc(x_upd, 1)
                    elif x[0] == "norm":
                        norm(x, pair, scale, c0, c1)
                    elif x[0] == "pre":
                        nx = STAGES[tail.n]
                        shift = mod_at(nx.layer, nx.sub, 0)
                        if st is not None:
                            norm(x, pair, scale, c0, c1)
                        elif x[1:] == (0, 0):
                            first_mods()
                            make_gains(tail)
                        dve.wait_ge(x_normed, KP * tail.pre_no[h] + x[2] + 1)
                        for m in (2 * x[2], 2 * x[2] + 1):
                            for k, a, b in segs:
                                part = y_acc[:, m, a:b]
                                ins = v.tensor_scalar(part, part, pre_gain[:, k, m:m + 1],
                                                      mods[:, k, shift + m:shift + m + 1], ALU.mult, ALU.add)
                        ins.then_inc(h_f32, 1)
                        pres_done[0] = tail.pre_no[h] + 1

            def norm(x, pair, scale, c0, c1):
                v.tensor_tensor(pair, x_res[:, 2 * x[2]:2 * x[2] + 2, c0:c1], scale, ALU.mult).then_inc(x_normed, 1)

            def first_mods():
                dve.wait_ge(mod_sum0, 1)
                first = MOD_FIRST * MOD_W // P
                for c in range(2):
                    ins = v.tensor_tensor(mods[:, c, 0:first], ps[:, 6, c:2 * first:2],
                                          vecs[:, VEC["mod_b"]:VEC["mod_b"] + first], ALU.add)
                ins.then_inc(mod_done, 1)
                dve.wait_ge(mod_done, 1)

            def mod_part(j, chunk, step0):
                for b in range(2):
                    dve.wait_ge(modp_in[b], 16 * (2 * chunk + j + 1))
                    for kk in range(2):
                        k = 4 * j + 2 * b + kk
                        for c in range(2):
                            step = step0 + 8 * j + 4 * b + 2 * kk + c
                            if k == 0:
                                ins = v.tensor_scalar(mod_acc[:, c], mod_raw[:, b, kk], cond[:, 2 * k + c:2 * k + c + 1],
                                                      None, ALU.mult)
                            else:
                                dve.wait_ge(mod_step, step - 1)
                                ins = v.scalar_tensor_tensor(mod_acc[:, c], mod_raw[:, b, kk],
                                                             cond[:, 2 * k + c:2 * k + c + 1], mod_acc[:, c],
                                                             ALU.mult, ALU.add)
                            ins.then_inc(mod_step, 1)
                    dve.wait_ge(mod_step, step + 1)
                    dve.sem_inc(modp_free, 1)

            def mod_finish(chunk):
                dve.wait_ge(mod_sum, chunk + 1)
                per = MOD_W // P
                col = (MOD_FIRST + chunk) * per
                bias = vecs[:, bass.ds(VEC["mod_b"] + col, per)]
                for c in range(2):
                    ins = v.tensor_tensor(mods[:, c, bass.ds(col, per)], ps[:, MODB, per * c:per * c + per], bias, ALU.add)
                ins.then_inc(mod_done, 1)

            def ffn_in(st, ph):
                kind, c, g, count, item0 = ph
                per = 2 * st.nh

                def group(i, peeled):
                    for x in range(per):
                        t, (c0, c1) = x % 2, st.halves[x // 2]
                        n = c1 - c0
                        item = item0 + per * i + x
                        gitem = g_total[0] + per * i + x
                        dve.wait_ge(pair_act, item + 1)
                        dve.wait_ge(g_free, gitem + 1)
                        v.tensor_tensor(dve_tmp[:, t, :n], ps[:, pair_bank(st, x, peeled and c == 0) + 1, :n], act_tmp[:, t, :n], ALU.mult).then_inc(in_free, 1)
                        if has_mods(st, ph):
                            chunk = mod_chunk0(st, ph) + 2 * i + x // 2
                            if x % 2 == 0 and not (peeled and x == 0):
                                mod_finish(chunk - 1)
                            mod_part(x % 2, chunk, 16 * chunk)

                peel = has_mods(st, ph) or c == 0
                if peel:
                    group(0, True)
                with dve.Fori(1 if peel else 0, count) as i:
                    group(i, False)
                g_total[0] += per * count

            def conv(tile, tile_no):
                def col(name, k=0):
                    return vecs[:, bass.ds(VEC[name] + k * KT + tile, 1)]

                src = rg_yu[:, 1, bass.ds(tile, 1)]
                dst = rg_uc[:, bass.ds(tile, 1)]
                step = CONV_STEPS * tile
                v.tensor_scalar(dst, src, col("conv_w", 2), col("conv_b"), ALU.mult, ALU.add).then_inc(conv_step, 1)
                n = 0
                for k in (1, 3, 0):
                    back = 2 - k
                    for a, b in ((0, CTX), (CTX, TOK)):
                        n += 1
                        lo, hi = (a + back, b) if back > 0 else (a, b + back)
                        dve.wait_ge(conv_step, step + n)
                        v.scalar_tensor_tensor(dst[:, :, lo:hi], src[:, :, lo - back:hi - back], col("conv_w", k),
                                               dst[:, :, lo:hi], ALU.mult, ALU.add).then_inc(conv_step, 1)

            def rg(st, ph):
                kind, c, g, count, item0 = ph
                if kind == "in":
                    with dve.Fori(0, count) as i:
                        for x in range(4):
                            t, (c0, c1) = x % 2, st.halves[x // 2]
                            dve.wait_ge(pair_act, item0 + 4 * i + x + 1)
                            v.tensor_copy(rg_yu[:, 1, bass.ds(2 * i + t, 1), c0:c1],
                                          ps[:, 2 * t + 1:2 * t + 2, :c1 - c0]).then_inc(in_free, 1)
                            if x >= 2:
                                dve.wait_ge(in_free, 2 + item0 + 4 * i + x + 1)
                                conv(2 * i + t, x)
                    return

                def uc_split(m):
                    if m >= 2:
                        dve.wait_ge(gate_ready, 2 * (m - 1))
                    v.tensor_copy(rg_split[:, m % 2, 0], rg_uc[:, m]).then_inc(uc_hi, 1)

                dve.wait_ge(conv_step, CONV_STEPS * KT)
                uc_split(0)
                uc_split(1)
                for m in range(KT):
                    w = rg_work[:, m % 2]
                    step = RG_STEPS * m

                    def link(ins, number):
                        ins.then_inc(rg_step, 1)
                        dve.wait_ge(rg_step, step + number)

                    for d in range(2):
                        s, b, a = w[:, d, 0], w[:, d, 1], w[:, d, 2]
                        dve.wait_ge(coef_done, 2 * m + d + 1)
                        link(v.scalar_tensor_tensor(s, a, 1.0, s, ALU.add, ALU.mult), 3 * d + 1)
                        dve.wait_ge(iu_done, 2 * m + d + 1)
                        link(v.tensor_tensor(b, s, b, ALU.mult), 3 * d + 2)
                        if d == 0:
                            link(v.tensor_tensor_scan(s, a, b, 0.0, ALU.mult, ALU.add), 3)
                        else:
                            link(v.tensor_tensor_scan(s[:, CTX - 1::-1], a[:, CTX - 1::-1], b[:, CTX - 1::-1], 0.0,
                                                      ALU.mult, ALU.add), 6)
                            link(v.tensor_tensor_scan(s[:, TOK - 1:CTX - 1:-1], a[:, TOK - 1:CTX - 1:-1],
                                                      b[:, TOK - 1:CTX - 1:-1], s[:, 0:1], ALU.mult, ALU.add), 7)
                    link(v.tensor_tensor(w[:, 0, 0], w[:, 0, 0], w[:, 1, 0], ALU.add), 8)
                    link(v.tensor_tensor(w[:, 0, 0], w[:, 0, 0], rg_yu[:, 0, m], ALU.mult), 9)
                    v.tensor_copy(rg_m[:, 0, m], w[:, 0, 0]).then_inc(m_hi, 1)
                    if m + 2 < KT:
                        uc_split(m + 2)

            def mla(st, ph):
                kind, c, g, count, _ = ph
                if kind == "latent":
                    places = []
                    for h in range(2):
                        c0, c1 = HALVES[h]
                        places += [ckv_raw[:, 0, c0:c1], ckv_raw[:, 1, c0:c1], kr_raw[:, c0:c1]]
                    places += [kr_swap[:]] + [cq_raw[:, t] for t in range(4)]

                    def apply_norm(which):
                        src, col, cols, size = latent_norms()[which]
                        dve.wait_ge(lat_rs, which + 1)
                        for k, x in enumerate(src):
                            v.scalar_tensor_tensor(x[0], x[0], vecs[:, col + k:col + k + 1], rstd[:, :cols],
                                                   ALU.mult, ALU.mult).then_inc(lat_step, 1)

                    for n, dst in enumerate(places):
                        dve.wait_ge(lat_ready, n + 1)
                        v.tensor_copy(dst, ps[:, n % 4, :dst.shape[-1]]).then_inc(lat_read, 1)
                        if n == 6:
                            dve.wait_ge(rope_in, 48)
                            dve.wait_ge(lat_read, 7)
                            v.tensor_tensor(rot_tmp[:, 0], kr_raw[:, CTX:], cos_t[:], ALU.mult).then_inc(kr_step, 1)
                            v.tensor_tensor(rot_tmp[:, 1], kr_swap[:], sin_t[:], ALU.mult).then_inc(kr_step, 1)
                            dve.wait_ge(kr_step, 2)
                            v.tensor_tensor(kr_raw[:, CTX:], rot_tmp[:, 0], rot_tmp[:, 1], ALU.add).then_inc(kr_step, 1)
                        if n >= 8:
                            apply_norm(n - 8)
                    return
                with dve.Fori(0, count) as i:
                    for n, (what, a, half) in enumerate(PROJ):
                        if what == "qr":
                            dve.wait_ge(prj_ready, len(PROJ) * i + 1)
                            v.tensor_tensor(rot_tmp[:, 0], ps[:, 0, :LAT], cos_t[:], ALU.mult).then_inc(qr_step, 1)
                            v.stream_shuffle(rot_tmp[:, 1], ps[:, 0, :LAT], [(k + 16) % 32 for k in range(32)]).then_inc(qr_step, 1)
                            dve.wait_ge(qr_step, 4 * i + 2)
                            v.tensor_tensor(rot_tmp[:, 1], rot_tmp[:, 1], sin_t[:], ALU.mult).then_inc(qr_step, 1)
                            dve.wait_ge(qr_step, 4 * i + 3)
                            v.tensor_tensor(rot_tmp[:, 0], rot_tmp[:, 0], rot_tmp[:, 1], ALU.add).then_inc(qr_step, 1)
                            dve.wait_ge(prj_hi, len(PROJ) * i + 1)
                            v.tensor_tensor(qr_pair[:, 1], rot_tmp[:, 0], qr_pair[:, 0].bitcast(F32),
                                            ALU.subtract).then_inc(prj_free, 1)
                            continue
                        width = {"q": LAT, "k": TOK // 2, "v": 2 * VD}[what]
                        hi, lo = proj_dst(what, a, half)
                        dve.wait_ge(prj_hi, len(PROJ) * i + n + 1)
                        v.tensor_tensor(lo, ps[:, n % 4, :width], hi.bitcast(F32), ALU.subtract).then_inc(prj_free, 1)

                    def weigh(u):
                        dve.wait_ge(s_exp, 8 * i + u + 3)
                        v.reciprocal(soft_max[:, u % 2, 3:4], soft_max[:, u % 2, 2:3]).then_inc(p_rcp, 1)
                        dve.wait_ge(p_rcp, 8 * i + u + 1)
                        v.tensor_scalar(p_soft[:, u % 2], p_soft[:, u % 2], soft_max[:, u % 2, 3:4], None,
                                        ALU.mult).then_inc(p_ready, 1)

                    for what, u in PAIR:
                        if what == "S":
                            dve.wait_ge(s_ready, 8 * i + u + 1)
                            v.tensor_reduce(soft_max[:, u % 2, 0:1], ps[:, 2 * (u % 2):2 * (u % 2) + 2, :TOK // 2],
                                            AX.XY, ALU.max).then_inc(s_max, 1)
                            dve.wait_ge(s_max, 16 * i + 2 * u + 1)
                            v.tensor_scalar(soft_max[:, u % 2, 1:2], soft_max[:, u % 2, 0:1], -SCALE, None,
                                            ALU.mult).then_inc(s_max, 1)
                            weigh(u)
                        elif what == "T":
                            src, dst = turned(u)
                            dve.wait_ge(t_hi, 8 * i + u + 1)
                            v.tensor_tensor(dst[1], src, dst[0].bitcast(F32), ALU.subtract).then_inc(t_free, 1)
                        else:
                            dve.wait_ge(o_hi, 2 * i + u + 1)
                            place = att_o[:, :, bass.ds(2 * i + u, 1)]
                            v.tensor_tensor(place[:, 1], ps[:, 6:7, :LAT], place[:, 0].bitcast(F32),
                                            ALU.subtract).then_inc(o_free, 1)

            dve.wait_ge(vec_in, 16)
            softplus()
            g_total, pres_done = [0], [0]
            tail_steps(TAILS[0])
            for n, st in enumerate(STAGES):
                for ph in phases(st):
                    kind, c, g, count, item0 = ph
                    if st.kind == "rg" and kind != "out":
                        rg(st, ph)
                    elif st.kind == "mla" and kind != "out":
                        mla(st, ph)
                    elif kind == "in":
                        ffn_in(st, ph)
                    elif ph != last_out(st):
                        nh = st.nh
                        if c == 0:
                            dve.wait_ge(h_lo, KP * pres_done[0])
                        with dve.Fori(0, count) as i:
                            for x in range(4 * nh):
                                h, q = x // 4, x % 4
                                c0, c1 = st.halves[h]
                                evict(item0 + 4 * nh * i + x, y_acc[:, bass.ds(4 * i + q, 1), c0:c1],
                                      ps[:, BANKS[nh][x]:BANKS[nh][x] + 1, :c1 - c0], c1 - c0, c == 0)
                        if has_mods(st, ("in", c)):
                            mod_finish(mod_chunk0(st, ph) + 7)
                if carries_mods(st):
                    dve.wait_ge(mod_done, mods_before(st))
                tail_steps(TAILS[n + 1])

        @block.tensor
        def _(pe):
            mm = nc.tensor.matmul

            def product(out, w, x, blocks, start=True, stop=True, before=None):
                for k in range(blocks):
                    if before and k % 2 == 0:
                        before(k)
                    for n, (a, b) in enumerate(((0, 0), (0, 1), (1, 0))):
                        last = mm(out, w(a, k), x(b, k), start=start and k == 0 and n == 0,
                                  stop=stop and k == blocks - 1 and n == 2)
                return last

            def slot(q, first=0, width=P):
                return lambda a, k: w_slot[:, q, a, first + k]

            def stat(tail, which, h):
                c0, c1 = tail.halves[h]
                wait_pos(pe, ln_done, tail.stat[which, h] - 1)
                pe.wait_ge(ss_added, tail.sums[which, h])
                mm(ps[:, STAT, :c1 - c0], ones[:], sum_sq[:, c0:c1], start=True, stop=True).then_inc(stat_ready, 1)

            def direct_sums(tail, m0, m1):
                wait_pos(pe, ln_done, tail.stat["pre", 0] - 1)
                for m in range(m0, m1):
                    pe.wait_ge(xsq_done, tail.sums["pre", 0] - KT + m + 1)
                    last = mm(ps[:, STAT, :TOK // 2], ones[:], x_sq[:, m], start=m == 0, stop=m == KT - 1)
                if m1 == KT:
                    last.then_inc(stat_ready, 1)

            def input_ready(tail, h, k=KT - 1):
                pe.wait_ge(h_lo, KP * tail.pre_no[h] + k // 2 + 1)

            def pair_item(st, x, item, first_unit, bank, before=None, between=None):
                t, (c0, c1) = x % 2, st.halves[x // 2]
                for b in range(2):
                    pe.wait_ge(w_lo, first_unit + 2 * t + b + 1)
                    if b == 0 and bank == 4:
                        wait_pos(pe, out_free, 3 + st.out0 if st.out0 else 0)
                    elif b == 0:
                        pe.wait_ge(in_free, item + 1)
                    if b == 1 and between:
                        between()
                    last = product(ps[:, bank + b, :c1 - c0], slot(2 * t + b), lambda a, k: h_in[:, a, k, c0:c1], KT,
                                   before=before if b == 0 else None)
                last.then_inc(in_ready, 1)

            def mod_sums(chunk):
                pe.wait_ge(mod_step, 16 * chunk + 16)
                for c in range(2):
                    for j in range(MOD_W // P):
                        last = mm(ps[:, MODB, 4 * c + j:4 * c + j + 1], mod_acc[:, c, j * P:(j + 1) * P], ones[:, 0:1],
                                  start=True, stop=True)
                last.then_inc(mod_sum, 1)

            def in_phase(n, st, ph):
                kind, c, g, count, item0 = ph
                per = 2 * st.nh
                tail = TAILS[n]

                def group(i, peeled):
                    for x in range(per):
                        first_use, two = peeled and c == 0 and x in (0, 2), len(tail.halves) == 2

                        def before(k):
                            if k == 4 and x == 0 and two and tail.stage:
                                stat(tail, "post", 1)
                            input_ready(tail, x // 2 if two else 0, k)

                        late = peeled and c == 0 and x == 1 and two and tail.stage
                        pair_item(st, x, item0 + per * i + x, (g + i) * NSLOT, pair_bank(st, x, peeled and c == 0),
                                  before=before if first_use else None,
                                  between=(lambda: stat(tail, "pre", 1)) if late else None)
                        if has_mods(st, ph) and x % 2 == 0 and not (peeled and x == 0):
                            if peeled and c == 1:
                                pe.wait_ge(ln_done, tail.end[1])
                            mod_sums(mod_chunk0(st, ph) + 2 * i + x // 2 - 1)

                start = 0
                if c == 0 or has_mods(st, ph):
                    group(0, True)
                    start = 1
                with pe.Fori(start, count) as i:
                    group(i, False)

            def out_item_products(st, h, q, x, item, unit, blocks, src):
                c0, c1 = st.halves[h]
                pe.wait_ge(w_lo, unit + 1)
                place = x % len(BANKS[st.nh])
                pe.wait_ge(out_free, 3 + item - BACK[st.nh][place] + 1)
                product(ps[:, BANKS[st.nh][place], :c1 - c0], slot(q), lambda a, k: src(a, k, c0, c1), blocks).then_inc(out_ready, 1)

            def out_phase(n, st, ph):
                kind, c, g, count, item0 = ph
                nh = st.nh
                tail = TAILS[n + 1]
                final = ph == last_out(st)
                if st.kind == "ffn":
                    blocks, src = CHUNKS[c], lambda a, k, c0, c1: g_act[:, a, k, c0:c1]
                    done = g_total[0]
                    pe.wait_ge(g_free, 2 + done - (2 if nh == 2 else 0))
                elif st.kind == "rg":
                    blocks, src = KT, lambda a, k, c0, c1: rg_m[:, a, k, c0:c1]
                    pe.wait_ge(m_lo, KT)
                else:
                    blocks, src = KT, lambda a, k, c0, c1: att_o[:, a, k, :]
                    pe.wait_ge(o_free, 1 + HEADS)

                def item(h, q, j, unit):
                    out_item_products(st, h, q, j, item0 + j, unit, blocks, src)

                if final and nh == 2:
                    for j, (h, m) in enumerate(FINAL):
                        if st.kind == "ffn" and j == KT:
                            pe.wait_ge(g_free, 2 + done)
                        item(h, m % 4, j, (g + (0, 1, 1, 2)[j // 4]) * NSLOT + m % 4)
                        if carries_mods(st) and j == 1:
                            mod_sums(st.mod0 - MOD_FIRST + 15)
                        if j == KT:
                            if carries_mods(st):
                                pe.wait_ge(mod_done, mods_before(st) + 1)
                            stat(tail, "post", 0)
                        if j == KT + 3 and tail.pre:
                            direct_sums(tail, 0, KP)
                        if j == KT + 4 and tail.pre:
                            direct_sums(tail, KP, KT)
                    if not tail.pre:
                        stat(tail, "post", 1)
                elif final:
                    for m in range(KT):
                        item(0, m % 4, m, g * NSLOT + m)
                    stat(tail, "post", 0)
                    if tail.pre:
                        stat(tail, "pre", 0)
                else:
                    with pe.Fori(0, count) as i:
                        for x in range(4 * nh):
                            h, q = x // 4, x % 4
                            if st.kind == "ffn" and nh == 2 and x == 4:
                                pe.wait_ge(g_free, 2 + done)
                            out_item_products(st, h, q, x, item0 + 4 * nh * i + x, (g + i) * NSLOT + q, blocks, src)
                    if has_mods(st, ("in", c)):
                        mod_sums(mod_chunk0(st, ph) + 7)

            def gates(st, ph):
                kind, c, g, count, _ = ph
                pe.wait_ge(in_free, 2 + st.in0 + KT * st.nh)
                for j in range(NSLOT):
                    pe.wait_ge(w_lo, g * NSLOT + j + 1)
                for m in range(KT):
                    pe.wait_ge(uc_lo, m + 1)
                    for d in range(2):
                        if m:
                            pe.wait_ge(sig_done, 2 * (m - 1) + d + 1)
                        for k in range(2):
                            for h, (c0, c1) in enumerate(HALVES):
                                last = product(ps[:, 4 * d + 2 * k + h, :c1 - c0],
                                               lambda a, b: w_slot[:, m // 2, a, 4 * (m % 2) + 2 * d + k],
                                               lambda a, b: rg_split[:, m % 2, a, c0:c1], 1)
                        last.then_inc(gate_ready, 1)

            def latents(n, ph):
                kind, c, g, count, _ = ph
                tail = TAILS[n]
                items = [(q, h) for h in range(2) for q in range(3)] + [(3, None)] + [(q, None) for q in range(4)]
                sums = [0]

                def norm_sums(which):
                    src, _, cols, _ = latent_norms()[which]
                    if which:
                        pe.wait_ge(lat_ln, which)
                    for k in range(len(src)):
                        sums[0] += 1
                        pe.wait_ge(lat_sq, sums[0])
                        mm(ps[:, 6, :cols], ones[:], mla_sq[:, (sums[0] - 1) % 2, :cols], start=k == 0,
                           stop=k == len(src) - 1).then_inc(lat_sum, 1)

                for i, (q, h) in enumerate(items):
                    c0, c1 = HALVES[h] if h is not None else (CTX, TOK)
                    unit = g * NSLOT + q if i < 7 else (g + 1) * NSLOT + q
                    pe.wait_ge(w_lo, unit + 1)
                    wait_pos(pe, lat_read, i - 3)
                    product(ps[:, i % 4, :c1 - c0], slot(q), lambda a, k: h_in[:, a, k, c0:c1], KT,
                            before=(lambda k: input_ready(tail, h, k)) if i in (0, 3) else None).then_inc(lat_ready, 1)
                    if i == 0:
                        stat(tail, "post", 1)
                    if i == 2:
                        stat(tail, "pre", 1)
                    if i == 6:
                        norm_sums(0)
                    if i == 9:
                        norm_sums(1)
                norm_sums(2)

            def heads(ph):
                kind, c, g, count, _ = ph
                pe.wait_ge(lat_lo, 1 + len(latent_splits()))
                with pe.Fori(0, count) as i:
                    pe.wait_ge(s_exp, 8 * i + 2)
                    for n, (what, a, half) in enumerate(PROJ):
                        q = {"qr": 0, "q": 1 + a, "k": 1 + a, "v": 3}[what]
                        pe.wait_ge(w_lo, (g + i) * NSLOT + q + 1)
                        if n >= 4:
                            pe.wait_ge(prj_free, len(PROJ) * i + n - 3)
                        bank = n % 4
                        if what in ("qr", "q"):
                            last = product(ps[:, bank, :LAT], slot(q), lambda b, k: cq_n[:, b, k], QL // P)
                        elif what == "k":
                            c0, c1 = HALVES[half]
                            last = product(ps[:, bank, :c1 - c0], slot(q, QL // P), lambda b, k: ckv_n[:, b, k, c0:c1], KVL // P)
                        else:
                            last = product(ps[:, bank, :2 * VD], lambda b, k: ckv_n[:, b, k, a * P:(a + 1) * P],
                                           lambda b, k: w_slot[:, 3, b, 2 * k:2 * k + 2].rearrange("p k c -> p (k c)"),
                                           KVL // P)
                        last.then_inc(prj_ready, 1)
                    pe.wait_ge(prj_free, len(PROJ) * (i + 1))
                    for what, u in PAIR:
                        hd, cols = u // QT, slice((u % QT) * P, (u % QT + 1) * P)
                        if what == "S":
                            pe.wait_ge(s_exp, 8 * i + u + 1)
                            for h, (c0, c1) in enumerate(HALVES):
                                bank = ps[:, 2 * (u % 2) + h, :c1 - c0]
                                product(bank, lambda a, k: q_head[hd][a][:, cols], lambda a, k: k_head[hd][:, a, c0:c1], 1,
                                        stop=False)
                                r0 = ROPE * hd
                                last = product(bank, lambda a, k: qr_pair[r0:r0 + ROPE, a, cols],
                                               lambda a, k: kr_n[r0:r0 + ROPE, a, c0:c1], 1, start=False)
                            last.then_inc(s_ready, 1)
                        elif what == "T":
                            pe.wait_ge(p_ready, 8 * i + u + 1)
                            pe.wait_ge(t_free, 8 * i + u + 1)
                            for t in range(CKT):
                                last = nc.tensor.transpose(ps[:, 4 + t // 3, (t % 3) * P:(t % 3 + 1) * P],
                                                           p_soft[:, u % 2, t * P:(t + 1) * P], ident[:])
                            last.then_inc(t_ready, 1)
                        else:
                            pe.wait_ge(t_free, 1 + 8 * i + 4 * u + 4)
                            pe.wait_ge(o_free, 2 * i + u + 1)
                            product(ps[:, 6, :LAT], lambda a, k: v_pair[:, a, k, u * VD:(u + 1) * VD],
                                    lambda a, k: p_turned[:, a, k], CKT).then_inc(o_ready, 1)

            pe.wait_ge(cond_done, 1)
            pe.wait_ge(consts, 2)
            for c in range(MOD_FIRST):
                pe.wait_ge(mod0_in[c], 16)
                for k in range(KT):
                    last = mm(ps[0:2, c, :MOD_W], cond[:, 2 * k:2 * k + 2], mod_first[c][:, k], start=k == 0, stop=k == KT - 1)
                last.then_inc(row_ready, 1)
                if c < 2:
                    stat(TAILS[0], "pre", c)
            for c in range(MOD_FIRST):
                pe.wait_ge(row_copied, c + 1)
                for j in range(MOD_W // P):
                    col = 2 * (4 * c + j)
                    last = mm(ps[:, 6, col:col + 2], mod_row[0:2, c, j * P:(j + 1) * P],
                              vecs[0:2, VEC["pick"]:VEC["pick"] + 2], start=True, stop=True)
            last.then_inc(mod_sum0, 1)
            g_total = [0]
            for n, st in enumerate(STAGES):
                for ph in phases(st):
                    kind = ph[0]
                    if kind == "in":
                        in_phase(n, st, ph)
                        if st.kind == "ffn":
                            g_total[0] += 2 * st.nh * ph[3]
                    elif kind == "out":
                        out_phase(n, st, ph)
                    elif kind == "gates":
                        gates(st, ph)
                    elif kind == "latent":
                        latents(n, ph)
                    else:
                        heads(ph)


def rope_tables():
    grid_w, base, quarter = 64, 10000.0, ROPE // 4
    inv_freq = np.float32(base) ** (-np.arange(quarter, dtype=np.float32) / np.float32(quarter))
    t = np.arange(LAT)
    pos = np.stack([t // grid_w, t % grid_w]).astype(np.float32)
    r = np.arange(P) % ROPE
    angle = pos[r // (2 * quarter)] * inv_freq[r % quarter][:, None]
    sign = np.where(r % (2 * quarter) < quarter, -1.0, 1.0)[:, None]
    return np.cos(angle).astype(np.float32), (np.sin(angle) * sign).astype(np.float32)


def kernel(**inputs):
    import numpy as _np
    import concourse.bacc as _bacc
    from concourse import mybir as _mybir
    from concourse.bass_utils import run_bass_kernel_spmd as _run

    a = {k: _np.asarray(v) for k, v in inputs.items()}

    def unit_blocks(w):
        r, c = w.shape
        return w.reshape(r // P, P, c // P, P).transpose(2, 1, 0, 3)

    def units_of(w, at, dst):
        u = unit_blocks(w)
        dst[at:at + u.shape[0], :, :u.shape[2]] = u

    units = _np.zeros((GROUPS * NSLOT, P, KT, P), _np.float32)
    def again(n):
        units[n:n + NSLOT] = units[n - KT:n - KT + NSLOT]

    for st in STAGES:
        n = st.group0 * NSLOT
        l, s = "l%d_" % st.layer, st.sub // 2
        if st.kind == "ffn":
            w_in, w_out = a[l + "ffn_w_in"][s], a[l + "ffn_w_out"][s]
            t0 = 0
            for tiles in CHUNKS:
                rows = slice(t0 * P, (t0 + tiles) * P)
                units[n:n + 2 * tiles:2] = unit_blocks(w_in[:, :DFF][:, rows])
                units[n + 1:n + 2 * tiles:2] = unit_blocks(w_in[:, DFF:][:, rows])
                n += 2 * tiles
                units_of(w_out[rows], n, units)
                n += KT
                t0 += tiles
            if st.nh == 2:
                again(n)
        elif st.kind == "rg":
            w_in = a[l + "rg_w_in"]
            units[n:n + 2 * KT:2] = unit_blocks(w_in[:, :D])
            units[n + 1:n + 2 * KT:2] = unit_blocks(w_in[:, D:])
            n += 2 * KT
            gw = a[l + "rg_gate_w"]
            units[n:n + NSLOT] = gw.transpose(2, 3, 0, 1, 4).reshape(NSLOT, 2, P, 4, P).transpose(0, 2, 1, 3, 4).reshape(
                NSLOT, P, KT, P)
            n += NSLOT
            units_of(a[l + "rg_w_out"], n, units)
            again(n + KT)
        else:
            w_a, w_qb, w_kvb = a[l + "mla_w_a"], a[l + "mla_w_qb"], a[l + "mla_w_kvb"]
            rope = w_a[:, QL + KVL:]
            swap = rope.reshape(D, 2, 2, ROPE // 4)[:, :, ::-1].reshape(D, ROPE)
            units_of(_np.concatenate([w_a[:, QL:QL + KVL], rope, rope, swap, swap, w_a[:, :QL]], 1), n, units)
            n += 2 * NSLOT
            wq = w_qb.reshape(QL, HEADS, QKD)
            wkv = w_kvb.reshape(KVL, HEADS, NOPE + VD)
            for p in range(HEADS // 2):
                units_of(wq[:, 2 * p:2 * p + 2, NOPE:].reshape(QL, 2 * ROPE), n, units)
                for h in range(2):
                    units[n + 1 + h, :, :4] = unit_blocks(wq[:, 2 * p + h, :NOPE])[0]
                    units[n + 1 + h, :, 4:6] = unit_blocks(wkv[:, 2 * p + h, :NOPE])[0]
                v = wkv[:, 2 * p:2 * p + 2, NOPE:].reshape(2, P, 2, VD)
                units[n + 3, :, :4] = v.transpose(1, 0, 2, 3).reshape(P, 4, VD)
                n += NSLOT
            units_of(a[l + "mla_w_o"], n, units)

    def mod_blocks(w):
        return w.reshape(KT, P, -1, MOD_W).transpose(2, 1, 0, 3)

    modw = _np.concatenate([mod_blocks(a["l0_mod_w"]), mod_blocks(a["l1_mod_w"])], 0)
    mod_start = _np.ascontiguousarray(modw[:MOD_FIRST])
    pieces = modw[MOD_FIRST:].reshape(-1, P, 4, 2, MOD_W).transpose(0, 2, 1, 3, 4).reshape(-1, P, 2, MOD_W)

    def cols(v):
        return _np.asarray(v).reshape(-1, P).T

    cond = _np.stack([cols(a["c"]), cols(a["c_ctx"])], 2).reshape(P, 2 * KT)
    vecs = _np.concatenate([cond, cols(a["l0_norm_g"]), cols(a["l1_norm_g"]), cols(a["l0_mod_b"]), cols(a["l1_mod_b"]),
                            cols(a["l0_rg_conv_w"]), cols(a["l0_rg_conv_b"]), cols(a["l0_rg_gate_b"]),
                            cols(a["l0_rg_lambda"]), cols(a["l1_mla_q_norm"]), cols(a["l1_mla_kv_norm"]),
                            _np.eye(P, 2, dtype=_np.float32)], 1)
    tokens = _np.concatenate([a["ctx"][0], a["x"][0]], 0)
    x_t = tokens.T.reshape(KT, P, TOK).transpose(1, 0, 2)
    cos, sin = rope_tables()

    nc = _bacc.Bacc("TRN2", target_bir_lowering=False, num_devices=1, dynamic_dma_scratch_size=1024)
    arrays = {}

    def dram(name, value):
        arrays[name] = _np.ascontiguousarray(value)
        return nc.dram_tensor(name, arrays[name].shape, _mybir.dt.float32, kind="ExternalInput").ap()

    out_tok = TOK if STAGES[-1].nh == 2 else LAT
    out_d = nc.dram_tensor("out_t", (KT, P, out_tok), _mybir.dt.float32, kind="ExternalOutput").ap()
    io = (dram("units", units), dram("mod_pieces", pieces), dram("mod_start", mod_start), dram("x_t", x_t),
          dram("vecs_in", vecs), [dram("cos_in", cos), dram("sin_in", sin), dram("ident_in", _np.eye(P, dtype=_np.float32))],
          out_d)
    build(nc, io)
    got = _run(nc, [arrays], core_ids=[0]).results[0]["out_t"]
    return _np.ascontiguousarray(got.reshape(D, out_tok).T[None])
```

```python
import numpy as np
import concourse.bass as bass
from concourse import mybir
from contextlib import ExitStack

F32 = mybir.dt.float32
F32R = mybir.dt.float32r
ALU = mybir.AluOpType
ACT = mybir.ActivationFunctionType
AX = mybir.AxisListType

P = 128
D = 1024
KT = D // P
KP = KT // 2
CTX, LAT = 256, 512
TOK = CTX + LAT
DFF = 2816
FT = DFF // P
CHUNKS = (FT - 16, 8, 8)
HALVES = ((0, TOK // 2), (TOK // 2, TOK))
LATENT = ((CTX, TOK),)
EPS = 1e-6
NSLOT = 4
NRAW = 4
MOD_W = 512
MOD_CHUNKS = 2 * 9 * D // MOD_W
MOD_FIRST = 4
HEADS = 8
NOPE, ROPE, VD = 128, 64, 128
QL, KVL = 512, 256
QKD = NOPE + ROPE
SCALE = float(QKD) ** -0.5
QT = LAT // P
CKT = TOK // P
RG_C = 8.0
CONV = 4

VEC = {}
_at = 0
for _name, _n in (("cond", 16), ("norm_g", 96), ("mod_b", 144), ("conv_w", 32), ("conv_b", 8), ("gate_b", 32),
                  ("lam", 16), ("q_norm", 4), ("kv_norm", 2), ("pick", 2)):
    VEC[_name] = _at
    _at += _n
NVEC = _at


class Stage:

    def __init__(self, kind, layer, sub, halves, group0, in0, out0, mod0):
        self.kind, self.layer, self.sub, self.halves = kind, layer, sub, halves
        self.group0, self.in0, self.out0, self.mod0 = group0, in0, out0, mod0
        self.nh = len(halves)


RG_UNITS = [("y", 0), ("gate", 0), ("y", 1), ("y", 2), ("gate", 1), ("y", 3), ("y", 4), ("gate", 2), ("y", 5), ("y", 6),
            ("gate", 3), ("y", 7)]
RG_SPLITS = {0: (4, 5, 6), 1: (7,), 2: (8, 9), 3: (10,), 4: (11, 12), 5: (13,), 6: (14, 15)}


def plan():
    stages, g, i, o, mod = [], 0, 0, 0, MOD_FIRST
    for kind, layer, sub, halves in (("ffn", 0, 0, HALVES), ("rg", 0, 1, HALVES), ("ffn", 0, 2, HALVES),
                                     ("ffn", 1, 0, HALVES), ("mla", 1, 1, LATENT), ("ffn", 1, 2, LATENT)):
        stages.append(Stage(kind, layer, sub, halves, g, i, o, mod))
        nh = len(halves)
        if kind == "ffn":
            g += FT // 2 + 2 * len(CHUNKS) + nh - 1
            i += FT * nh
            o += KT * nh * len(CHUNKS)
            if layer == 0:
                mod += 16
        elif kind == "rg":
            g += KT // NSLOT + len(RG_UNITS) // NSLOT + 3
            i += KT // 2 * nh
            o += KT * nh
        else:
            g += 2 + HEADS // 2 + 2
            o += KT * nh
    return stages, g


STAGES, GROUPS = plan()


FINAL = [(0, m) for m in range(KT)] + [(1, m) for m in range(KP, KT)] + [(1, m) for m in range(KP)]


class Tail:

    def __init__(self, n, stage, pre, squares, stats, posts, pres):
        self.n, self.stage, self.pre = n, stage, pre
        two = stage is None or stage.nh == 2
        self.halves = HALVES if two else LATENT

        def chain(which, h):
            return [("rs", h, which)] + [(which, h, j) for j in range(KP)]

        if stage is None:
            self.order = [("sq", 0, 0), ("sq", 1, 0)]
            for h in range(2):
                self.order += [("rs", h, "pre")] + [("norm", h, j) for j in range(KP)]
            self.order += [("pre", h, j) for h in range(2) for j in range(KP)]
        elif stage.nh == 2:
            e = [("E", h, m) for h, m in FINAL]
            a, b = chain("post", 0), chain("pre", 0)
            self.order = (e[:9] + a[:2] + e[9:10] + a[2:4] + e[10:11] + a[4:] + e[11:13] + b[:2] + e[13:14] + b[2:3]
                          + e[14:15] + b[3:] + e[15:] + chain("post", 1) + chain("pre", 1))
        else:
            self.order = [("E", 0, m) for m in range(KT)] + chain("post", 0) + chain("pre", 0)
        if not pre:
            self.order = [x for x in self.order if x[0] != "pre" and x[2] != "pre"]
        self.square, self.stat, self.post, self.pre_no, self.sums = {}, {}, {}, {}, {}
        for x in self.order:
            h = x[1]
            if x[0] == "E":
                squares += 1
                self.square[x] = squares
                self.sums["post", h] = squares
            elif x[0] == "rs":
                stats += 1
                self.stat[x[2], h] = stats
                if x[2] == "post":
                    self.post[h] = posts
                    posts += 1
                else:
                    self.pre_no[h] = pres
                    pres += 1
            elif x[0] == "post" and pre and self.direct(h):
                self.sums["pre", h] = KT * (self.post[h] // 2 + 1)
            elif x[0] == "sq" or (x[0] == "post" and pre):
                for m in range(KT) if x[0] == "sq" else (2 * x[2], 2 * x[2] + 1):
                    squares += 1
                    self.square[("x", h, m)] = squares
                self.sums["pre", h] = squares
        self.end = squares, stats, posts, pres

    def direct(self, h):
        return self.stage is not None and self.pre and self.stage.nh == 2 and h == 0


def tails():
    out = [Tail(0, None, True, 0, 0, 0, 0)]
    for n, s in enumerate(STAGES):
        out.append(Tail(n + 1, s, n < len(STAGES) - 1, *out[-1].end))
    return out


TAILS = tails()
MLA_TAIL = 5


def segments(c0, c1):
    out = []
    if c0 < CTX:
        out.append((1, c0, min(c1, CTX)))
    if c1 > CTX:
        out.append((0, max(c0, CTX), c1))
    return out


def build(nc, io):
    ctx = ExitStack()
    with ctx:
        KB = 1024
        X_AT, H_AT, G_AT, Y_AT = 0, 24 * KB, 72 * KB, 120 * KB
        W_AT, RAW_AT, MISC_AT = 144 * KB, 176 * KB, 192 * KB
        base = ((nc.sbuf_base + 63) // 64) * 64

        def at(name, offset, shape, dt=F32):
            return nc.alloc_sbuf_tensor_at(name, [P, *shape], dt, offset=base + offset)

        def sem(name):
            return ctx.enter_context(nc.semaphore(name))

        x_res = at("x_res", X_AT, [KT, TOK])
        h_in = at("h_in", H_AT, [2, KT, TOK], F32R)
        g_act = at("g_act", G_AT, [2, KT, TOK], F32R)
        y_acc = at("y_acc", Y_AT, [KT, TOK])
        w_slot = at("w_slot", W_AT, [NSLOT, 2, KT, P], F32R)
        raw = at("raw", RAW_AT, [NSLOT, KT, P])
        mod_raw = at("mod_raw", MISC_AT, [2, 2, MOD_W])
        mod_acc = at("mod_acc", MISC_AT + 8 * KB, [2, MOD_W])
        act_tmp = at("act_tmp", MISC_AT + 12 * KB, [2, 512])
        dve_tmp = at("dve_tmp", MISC_AT + 16 * KB, [2, 512])
        sum_sq = at("sum_sq", MISC_AT + 20 * KB, [TOK])
        rstd = at("rstd", MISC_AT + 23 * KB, [512])
        small_at = [MISC_AT + 25 * KB]

        def small(name, *shape):
            offset = small_at[0]
            small_at[0] += (4 * int(np.prod(shape)) + 31) // 32 * 32
            return at(name, offset, shape)

        vecs = small("vecs", NVEC)
        mods = small("mods", 2, 2 * 72)
        cond = small("cond", 16)
        post_gain = small("post_gain", 2, KT)
        pre_gain = small("pre_gain", 2, KT)
        decay = small("decay", 2, 16)
        eps_col = small("eps_col", 1)
        soft_max = small("soft_max", 2, 4)
        soft = small("soft", 6, 16)
        ones = small("ones", P)
        ident = small("ident", P)
        assert base + small_at[0] <= nc.sbuf_usable_end

        x_sq = at("x_sq", MISC_AT, [KT, TOK // 2])

        mod_first_g = at("mod_first_g", G_AT, [MOD_FIRST - 1, KT, MOD_W])
        mod_first_h = at("mod_first_h", H_AT + 24 * KB, [KT, MOD_W])
        mod_first = [mod_first_g[:, n] for n in range(MOD_FIRST - 1)] + [mod_first_h[:]]
        mod_row = at("mod_row", MISC_AT, [MOD_FIRST, MOD_W])

        rg_y = at("rg_y", G_AT, [KT, TOK])
        rg_u = at("rg_u", G_AT + 24 * KB, [KT, TOK])
        rg_uc = at("rg_uc", Y_AT, [KT, TOK])
        rg_m = [at("rg_m_hi", G_AT, [KT, TOK], F32R), at("rg_m_lo", Y_AT, [KT, TOK], F32R)]
        rg_work = [at("rg_work0", MISC_AT, [2, 3, TOK]), at("rg_work1", G_AT + 24 * KB, [2, 3, TOK])]
        rg_split = [at("rg_split0", MISC_AT + 18 * KB, [2, TOK], F32R),
                    at("rg_split1", G_AT + 42 * KB, [2, TOK], F32R)]
        rg_acc = at("rg_acc", G_AT + 24 * KB, [KT, TOK])

        cq_raw = at("cq_raw", G_AT + 16 * KB, [4, LAT])
        ckv_raw = at("ckv_raw", G_AT + 24 * KB, [2, TOK])
        kr_raw = at("kr_raw", G_AT + 30 * KB, [TOK])
        kr_swap = at("kr_swap", G_AT + 33 * KB, [LAT])
        mla_sq = at("mla_sq", G_AT + 35 * KB, [2, LAT])
        cq_n = at("cq_n", G_AT, [2, 4, LAT], F32R)
        att_o = at("att_o", G_AT + 16 * KB, [2, HEADS, LAT], F32R)
        ckv_n = at("ckv_n", Y_AT, [2, 2, TOK], F32R)
        kr_n = at("kr_n", Y_AT + 12 * KB, [2, TOK], F32R)
        k_head = [at("k_head0", Y_AT + 18 * KB, [2, TOK], F32R), at("k_head1", H_AT + 40 * KB, [2, TOK], F32R)]
        v_pair = at("v_pair", H_AT, [2, CKT, 2 * VD], F32R)
        p_turned = at("p_turned", H_AT + 12 * KB, [2, CKT, LAT], F32R)
        q_head = [[at("q_head0h", H_AT + 36 * KB, [LAT], F32R), at("q_head0l", H_AT + 38 * KB, [LAT], F32R)],
                  [at("q_head1h", H_AT + 46 * KB, [LAT], F32R), at("q_head1l", MISC_AT + 18 * KB, [LAT], F32R)]]
        p_soft = at("p_soft", MISC_AT + 12 * KB, [2, TOK])
        cos_t = at("cos_t", MISC_AT, [LAT])
        sin_t = at("sin_t", MISC_AT + 2 * KB, [LAT])
        qr_pair = at("qr_pair", MISC_AT + 4 * KB, [2, LAT], F32R)
        rot_tmp = at("rot_tmp", MISC_AT + 8 * KB, [2, LAT])

        ps = ctx.enter_context(nc.psum_tensor("ps", [P, 8, 512], F32))
        STAT, MODB = 7, 7

        vec_in = sem("vec_in")
        x_in = sem("x_in")
        mod0_in = [sem(f"mod0_in{n}") for n in range(2 * MOD_FIRST)]
        raw_in = [sem(f"raw_in{n}") for n in range(NSLOT)]
        w_hi = sem("w_hi")
        w_lo = sem("w_lo")
        modp_in = [sem(f"modp_in{n}") for n in range(2)]
        modp_free = sem("modp_free")
        mod_step = sem("mod_step")
        mod_sum = sem("mod_sum")
        mod_done = sem("mod_done")
        consts = sem("consts")
        row_ready = sem("row_ready")
        row_copied = sem("row_copied")
        mod_sum0 = sem("mod_sum0")
        cond_done = sem("cond_done")
        in_ready = sem("in_ready")
        pair_act = sem("pair_act")
        in_free = sem("in_free")
        g_hi = sem("g_hi")
        g_free = sem("g_free")
        out_ready = sem("out_ready")
        out_free = sem("out_free")
        sq_done = sem("sq_done")
        xsq_done = sem("xsq_done")
        ss_added = sem("ss_added")
        ss_zero = sem("ss_zero")
        stat_ready = sem("stat_ready")
        ln_done = sem("ln_done")
        rs_ready = sem("rs_ready")
        gain_done = sem("gain_done")
        y_normed = sem("y_normed")
        x_upd = sem("x_upd")
        x_normed = sem("x_normed")
        h_f32 = sem("h_f32")
        h_hi = sem("h_hi")
        h_lo = sem("h_lo")
        soft_step = sem("soft_step")
        soft_exp = sem("soft_exp")
        conv_step = sem("conv_step")
        uc_hi = sem("uc_hi")
        uc_lo = sem("uc_lo")
        gate_ready = sem("gate_ready")
        sig_done = sem("sig_done")
        y_ready = sem("y_ready")
        y_copied = sem("y_copied")
        y_gelu = sem("y_gelu")
        expd = sem("expd")
        coef_done = sem("coef_done")
        iu_done = sem("iu_done")
        rg_step = sem("rg_step")
        m_hi = sem("m_hi")
        m_lo = sem("m_lo")
        rope_in = sem("rope_in")
        lat_ready = sem("lat_ready")
        lat_read = sem("lat_read")
        lat_sq = sem("lat_sq")
        lat_sum = sem("lat_sum")
        lat_ln = sem("lat_ln")
        lat_rs = sem("lat_rs")
        lat_step = sem("lat_step")
        lat_hi = sem("lat_hi")
        lat_lo = sem("lat_lo")
        cq_lo = sem("cq_lo")
        kr_step = sem("kr_step")
        prj_ready = sem("prj_ready")
        prj_hi = sem("prj_hi")
        prj_free = sem("prj_free")
        qr_step = sem("qr_step")
        s_ready = sem("s_ready")
        s_max = sem("s_max")
        s_exp = sem("s_exp")
        s_rcp = sem("s_rcp")
        p_ready = sem("p_ready")
        t_ready = sem("t_ready")
        t_hi = sem("t_hi")
        t_free = sem("t_free")
        o_ready = sem("o_ready")
        o_hi = sem("o_hi")
        o_free = sem("o_free")
        out_sent = sem("out_sent")

        units, mod_pieces, mod_start, x_t, vec_d, rope_d, out_d = io
        block = ctx.enter_context(nc.Block())

        def mod_at(layer, sub, what):
            return layer * 72 + (sub * 3 + what) * KT

        def gain_at(layer, row):
            return VEC["norm_g"] + (layer * 6 + row) * KT

        def wait_pos(eng, s, value):
            if value > 0:
                eng.wait_ge(s, value)

        def phases(st):
            if st.kind == "ffn":
                out, g, i, o = [], st.group0, st.in0, st.out0
                for c, tiles in enumerate(CHUNKS):
                    out.append(("in", c, g, tiles // 2, i))
                    g += tiles // 2
                    i += tiles * st.nh
                    count = 1 + st.nh if c == len(CHUNKS) - 1 else 2
                    out.append(("out", c, g, count, o))
                    g += count
                    o += KT * st.nh
                return out
            if st.kind == "rg":
                g = st.group0
                gates, out = g + KT // NSLOT, g + (KT + len(RG_UNITS)) // NSLOT
                return [("in", 0, g, gates - g, st.in0), ("gates", 0, gates, out - gates, 0), ("out", 0, out, 3, st.out0)]
            g = st.group0
            return [("latent", 0, g, 2, 0), ("heads", 0, g + 2, HEADS // 2, 0),
                    ("out", 0, g + 2 + HEADS // 2, 2, st.out0)]

        def last_out(st):
            return phases(st)[-1]

        def mods_before(st):
            return 1 + st.mod0 - MOD_FIRST + 15

        def mod_conds(st, c):
            return 1 if (st.layer, st.sub, c) == (0, 2, 2) else 2

        def carries_mods(st):
            return st.kind == "ffn" and st.layer == 0

        def has_mods(st, ph):
            return st.kind == "ffn" and st.layer == 0 and ph[0] == "in" and ph[1] > 0

        def mod_chunk0(st, ph):
            return st.mod0 - MOD_FIRST + 8 * (ph[1] - 1)

        BANKS = {2: (4, 5, 6, 4, 5, 6, 4, 5), 1: (4, 5, 6, 5)}
        BACK = {2: (2, 2, 3, 3, 3, 3, 3, 3), 1: (3, 2, 3, 2)}

        CONV_STEPS, RG_STEPS = 7, 9

        def pair_bank(st, x, first):
            return 4 if first and x == 2 and st.nh == 2 else 2 * (x % 2)

        def out_bank(st, x):
            return BANKS[st.nh][x % len(BANKS[st.nh])]

        def out_item(st, x):
            return last_out(st)[4] + (FINAL.index(x[1:]) if st.nh == 2 else x[2])

        def split_behind(st, x):
            j = out_item(st, x) - last_out(st)[4]
            if st.nh == 2:
                step = {0: 1, 2: 2, 3: 3}.get(j // 4)
            else:
                step = j // 4 + 1
            if step is None or last_out(st)[2] + step >= GROUPS:
                return None
            return last_out(st)[2] + step, j % 4

        def latent_norms():
            out = []
            for h in range(2):
                c0, c1 = HALVES[h]
                out.append(([(ckv_raw[:, t, c0:c1], 3 * h + t + 1) for t in range(2)], VEC["kv_norm"], c1 - c0, KVL))
            out.append(([(cq_raw[:, t], 7 + t + 1) for t in range(4)], VEC["q_norm"], LAT, QL))
            return out

        def rg_unit_ordinal(g, p):
            return g * NSLOT + p

        def acc(st):
            return rg_acc if st is not None and st.kind == "rg" else y_acc

        def rg_pool(m, split_lo, g):
            pool = nc.gpsimd
            if m == 0:
                rg_split_lo(0)
            for d in range(2):
                pool.wait_ge(sig_done, 4 * m + 2 * d + 2)
                gate = rg_work[m % 2][:, d, 1]
                pool.tensor_tensor(gate, gate, rg_uc[:, m], ALU.mult).then_inc(iu_done, 1)
            if m + 1 < KT:
                rg_split_lo(m + 1)
            for n in ([m - 1] if m else []) + ([m] if m == KT - 1 else []):
                pool.wait_ge(m_hi, n + 1)
                pool.tensor_tensor(rg_m[1][:, n], rg_work[n % 2][:, 0, 0], rg_m[0][:, n].bitcast(F32),
                                   ALU.subtract).then_inc(m_lo, 1)
                for p in RG_SPLITS.get(n, ()):
                    split_lo(g + p // NSLOT, p % NSLOT)

        def rg_split_lo(m):
            pool = nc.gpsimd
            pool.wait_ge(uc_hi, m + 1)
            pool.tensor_tensor(rg_split[m % 2][:, 1], rg_uc[:, m], rg_split[m % 2][:, 0].bitcast(F32),
                               ALU.subtract).then_inc(uc_lo, 1)

        def latent_splits():
            out = []
            for h in range(2):
                c0, c1 = HALVES[h]
                for t in range(2):
                    out.append((ckv_n[:, :, t, c0:c1], ckv_raw[:, t, c0:c1]))
            for t in range(4):
                out.append((cq_n[:, :, t], cq_raw[:, t]))
            return out

        def mla_latent_pool(split_lo, g):
            pool = nc.gpsimd
            for q in range(NSLOT):
                split_lo(g + 1, q)
            pool.wait_ge(lat_hi, 1)
            pool.tensor_tensor(kr_n[:, 1], kr_raw[:], kr_n[:, 0].bitcast(F32), ALU.subtract).then_inc(lat_lo, 1)
            for n, (dst, src) in enumerate(latent_splits()):
                if n == 4:
                    for q in range(NSLOT):
                        split_lo(g + 2, q)
                    break
                pool.wait_ge(lat_hi, n + 2)
                pool.tensor_tensor(dst[:, 1], src, dst[:, 0].bitcast(F32), ALU.subtract).then_inc(lat_lo, 1)

        PAIR = [("S", 0), ("P", 11), ("P", 12), ("S", 1), ("T", 0), ("S", 2), ("T", 1), ("S", 3), ("T", 2), ("S", 4),
                ("T", 3), ("S", 5), ("V", 0), ("T", 4), ("S", 6), ("T", 5), ("S", 7), ("T", 6), ("T", 7), ("V", 1)]
        PAIR_PE = list(PAIR)
        PAIR_PE.remove(("S", 6))
        PAIR_PE.insert(PAIR_PE.index(("V", 0)), ("S", 6))
        PROJ = [("k", 0, 0), ("k", 0, 1), ("k", 1, 0), ("k", 1, 1), ("v", 0, 0), ("v", 1, 0), ("qr", 0, 0), ("q", 0, 0),
                ("q", 1, 0), ("v", 2, 0), ("v", 3, 0), ("v", 4, 0), ("v", 5, 0)]
        PROJ_BANK = (0, 1, 2, 3, 4, 5, 0, 1, 2, 6, 7, 4, 5)
        FIRST_PROJ, QK_PROJ = 11, 9

        def proj_dst(kind, n, half):
            if kind == "q":
                return q_head[n][0][:], q_head[n][1][:]
            if kind == "k":
                c0, c1 = HALVES[half]
                return k_head[n][:, 0, c0:c1], k_head[n][:, 1, c0:c1]
            return v_pair[:, 0, n], v_pair[:, 1, n]

        def turn_bank(what, u):
            item = u + (u >= QT) if what == "T" else (QT + 1) * (u + 1) - 1
            return 4 + 2 * (item % 2)

        def turned(u):
            bank = turn_bank("T", u)
            src = ps[:, bank:bank + 2, :3 * P].rearrange("p b (t q) -> p b t q", t=3)
            c = (u % QT) * P
            dst = [p_turned[:, n, :, c:c + P].rearrange("p (b t) q -> p b t q", b=2) for n in range(2)]
            return src, dst

        @block.sync
        def _(sp):
            sp.dma_start(vecs[:], vec_d).then_inc(vec_in, 16)
            for c in range(MOD_FIRST):
                for k in (0, KP):
                    if (c, k) == (1, KP):
                        sp.dma_start(x_res[:], x_t).then_inc(x_in, 16)
                    sp.dma_start(mod_first[c][:, k:k + KP], mod_start[c, :, k:k + KP]).then_inc(mod0_in[2 * c + k // KP], 16)

            def load_unit(group, q):
                if not (isinstance(group, int) and group == 0):
                    sp.wait_ge(w_lo, (group - 1) * NSLOT + q + 1)
                sp.dma_start(raw[:, q], units[bass.ds(group * NSLOT + q, 1)]).then_inc(raw_in[q], 16)

            for q in range(NSLOT):
                load_unit(0, q)
            for st in STAGES:
                for ph in phases(st):
                    kind, c, g, count, _ = ph
                    if kind == "latent":
                        sp.wait_ge(mod_done, MOD_CHUNKS - MOD_FIRST + 1)
                        sp.wait_ge(stat_ready, TAILS[STAGES.index(st)].stat["pre", 0])
                        for dst, src in zip((cos_t, sin_t, ident), rope_d):
                            sp.dma_start(dst[:], src).then_inc(rope_in, 16)
                    last = g + count == GROUPS
                    n = count - last
                    with sp.Fori(0, n) as i:
                        if not has_mods(st, ph):
                            for q in range(NSLOT):
                                load_unit(g + 1 + i, q)
                            continue
                        for j in range(8):
                            piece = 4 * mod_chunk0(st, ph) + 8 * i + j
                            sp.wait_ge(modp_free, piece + 1)
                            sp.dma_start(mod_raw[:, j % 2], mod_pieces[bass.ds(piece, 1)]).then_inc(modp_in[j % 2], 16)
                            if 1 <= j <= NSLOT:
                                load_unit(g + 1 + i, j - 1)
            st = STAGES[-1]
            tail = TAILS[len(STAGES)]
            n = 0
            for h in range(st.nh):
                c0, c1 = st.halves[h]
                for m in range(KT):
                    sp.wait_ge(x_upd, KT * tail.post[h] + m + 1)
                    sp.dma_start(out_d[m, :, c0 - (TOK - out_d.shape[2]):c1 - (TOK - out_d.shape[2])],
                                 x_res[:, m, c0:c1]).then_inc(out_sent, 16)
                    n += 16
            sp.wait_ge(out_sent, n)

        @block.gpsimd
        def _(pool):
            nc.gpsimd.memset(ones[:], 1.0).then_inc(consts, 1)
            nc.gpsimd.memset(eps_col[:], EPS).then_inc(consts, 1)
            nc.gpsimd.memset(sum_sq[:], 0.0).then_inc(ss_zero, 1)

            def split_lo(group, q):
                pool.wait_ge(w_hi, group * NSLOT + q + 1)
                nc.gpsimd.tensor_tensor(w_slot[:, q, 1], raw[:, q], w_slot[:, q, 0].bitcast(F32),
                                        ALU.subtract).then_inc(w_lo, 1)

            def add_square(number, c0, c1):
                pool.wait_ge(sq_done, number)
                wait_pos(pool, ss_added, number - 1)
                nc.gpsimd.tensor_tensor(sum_sq[:, c0:c1], sum_sq[:, c0:c1], act_tmp[:, (number - 1) % 2, :c1 - c0],
                                        ALU.add).then_inc(ss_added, 1)

            cleared = [1]

            def clear_sums(stat, c0, c1):
                cleared[0] += 1
                pool.wait_ge(stat_ready, stat)
                nc.gpsimd.memset(sum_sq[:, c0:c1], 0.0).then_inc(ss_zero, 1)
                pool.wait_ge(ss_zero, cleared[0])

            def tail_steps(tail):
                if tail.n == 0:
                    pool.wait_ge(ss_zero, 1)
                for x in tail.order:
                    h = x[1]
                    c0, c1 = tail.halves[h]
                    if x[0] == "E":
                        add_square(tail.square[x], c0, c1)
                        unit = split_behind(tail.stage, x)
                        late = x in (("E", 1, 2), ("E", 1, 3)) and unit
                        if unit and not late:
                            split_lo(*unit)
                        if late and x[2] == 3:
                            for q in (2, 3):
                                split_lo(unit[0], q)
                    elif x[0] == "rs":
                        if tail.pre and not (x[2] == "pre" and tail.direct(h)):
                            clear_sums(tail.stat[x[2], h], c0, c1)
                    elif x[0] == "pre":
                        j = x[2]
                        pool.wait_ge(h_hi, KP * tail.pre_no[h] + j + 1)
                        nc.gpsimd.tensor_tensor(h_in[:, 1, 2 * j:2 * j + 2, c0:c1],
                                                acc(tail.stage)[:, 2 * j:2 * j + 2, c0:c1],
                                                h_in[:, 0, 2 * j:2 * j + 2, c0:c1].bitcast(F32),
                                                ALU.subtract).then_inc(h_lo, 1)
                        if tail.stage is None and (h, j) == (0, KP - 1):
                            split_lo(0, 2)
                            split_lo(0, 3)
                    elif x[0] == "norm":
                        if x[1:] == (1, KP - 1):
                            split_lo(0, 0)
                            split_lo(0, 1)
                    elif tail.pre and not tail.direct(h):
                        for m in range(KT) if x[0] == "sq" else (2 * x[2], 2 * x[2] + 1):
                            add_square(tail.square[("x", h, m)], c0, c1)

            g_items = 0
            tail_steps(TAILS[0])
            for n, st in enumerate(STAGES):
                for ph in phases(st):
                    kind, c, g, count, item0 = ph
                    per = 2 * st.nh
                    if kind == "in" and st.kind == "ffn":
                        with pool.Fori(0, count) as i:
                            for x in range(per):
                                t, (c0, c1) = x % 2, st.halves[x // 2]
                                pool.wait_ge(g_hi, g_items + per * i + x + 1)
                                dst = g_act[:, :, bass.ds(2 * i + t, 1), c0:c1]
                                nc.gpsimd.tensor_tensor(dst[:, 1], dve_tmp[:, x % 2:x % 2 + 1, :c1 - c0], dst[:, 0].bitcast(F32),
                                                        ALU.subtract).then_inc(g_free, 1)
                                for q in ((0, 1), (2, 3))[x % 2] if x >= per - 2 else ():
                                    split_lo(g + i + 1, q)
                        g_items += per * count
                    elif kind == "in":
                        with pool.Fori(0, count) as i:
                            for q in range(NSLOT):
                                split_lo(g + i + 1, q)
                    elif kind == "gates":
                        for m in range(KT):
                            rg_pool(m, split_lo, g)
                        cleared[0] += 1
                        nc.gpsimd.memset(sum_sq[:], 0.0).then_inc(ss_zero, 1)
                        pool.wait_ge(ss_zero, cleared[0])
                    elif kind == "latent":
                        mla_latent_pool(split_lo, g)
                    elif kind == "heads":
                        with pool.Fori(0, count) as i:
                            for q in range(NSLOT):
                                split_lo(g + i + 1, q)
                    elif ph != last_out(st):
                        with pool.Fori(0, count) as i:
                            for q in range(NSLOT):
                                split_lo(g + i + 1, q)
                tail_steps(TAILS[n + 1])

        @block.scalar
        def _(act):
            def split_hi(group, q):
                act.wait_ge(raw_in[q], 16 * (group + 1))
                nc.scalar.activation(w_slot[:, q, 0], raw[:, q], ACT.Copy).then_inc(w_hi, 1)

            def square(number, src, n):
                wait_pos(act, ss_added, number - 2)
                nc.scalar.activation(act_tmp[:, (number - 1) % 2, :n], src, ACT.Square).then_inc(sq_done, 1)

            def rsqrt_mean(stat, n):
                act.wait_ge(stat_ready, stat)
                nc.scalar.activation(rstd[:, :n], ps[:, STAT, :n], ACT.Ln, bias=eps_col[:], scale=1.0 / D).then_inc(ln_done, 1)
                act.wait_ge(ln_done, stat)
                nc.scalar.activation(rstd[:, :n], rstd[:, :n], ACT.Exp, scale=-0.5).then_inc(rs_ready, 1)

            def tail_steps(tail):
                st = tail.stage
                if st is not None and st.kind == "ffn":
                    act.wait_ge(in_free, 2 + st.in0 + FT * st.nh)
                for x in tail.order:
                    h = x[1]
                    c0, c1 = tail.halves[h]
                    n = c1 - c0
                    if x[0] == "E":
                        act.wait_ge(out_free, 3 + out_item(st, x) + 1)
                        square(tail.square[x], acc(st)[:, x[2], c0:c1], n)
                        unit = split_behind(st, x)
                        if unit:
                            split_hi(*unit)
                    elif x[0] == "rs":
                        if st is None and h == 1:
                            act.wait_ge(x_normed, KP)
                        rsqrt_mean(tail.stat[x[2], h], n)
                    elif x[0] == "pre":
                        j = x[2]
                        act.wait_ge(h_f32, KP * tail.pre_no[h] + j + 1)
                        nc.scalar.activation(h_in[:, 0, 2 * j:2 * j + 2, c0:c1], acc(st)[:, 2 * j:2 * j + 2, c0:c1],
                                             ACT.Copy).then_inc(h_hi, 1)
                        if st is None and (h, j) == (0, KP - 1):
                            split_hi(0, 2)
                            split_hi(0, 3)
                    elif x[0] == "norm":
                        if x[1:] == (1, KP - 1):
                            for c in range(MOD_FIRST):
                                if c == MOD_FIRST - 1:
                                    split_hi(0, 0)
                                    split_hi(0, 1)
                                act.wait_ge(row_ready, c + 1)
                                nc.scalar.activation(mod_row[0:2, c], ps[0:2, c, :MOD_W], ACT.Copy).then_inc(row_copied, 1)
                    elif x[0] == "sq":
                        act.wait_ge(x_in, 16)
                        for m in range(KT):
                            square(tail.square[("x", h, m)], x_res[:, m, c0:c1], n)
                    elif tail.pre:
                        for m in (2 * x[2], 2 * x[2] + 1):
                            act.wait_ge(x_upd, KT * tail.post[h] + m + 1)
                            if tail.direct(h):
                                nc.scalar.activation(x_sq[:, m], x_res[:, m, c0:c1], ACT.Square).then_inc(xsq_done, 1)
                                continue
                            square(tail.square[("x", h, m)], x_res[:, m, c0:c1], n)

            def ffn_in(st, c, g, count, item0, g0):
                per = 2 * st.nh

                def group(i, first):
                    for x in range(per):
                        t, (c0, c1) = x % 2, st.halves[x // 2]
                        item = item0 + per * i + x
                        act.wait_ge(in_ready, item + 1)
                        act.wait_ge(in_free, item + 1)
                        nc.scalar.activation(act_tmp[:, t, :c1 - c0], ps[:, pair_bank(st, x, first), :c1 - c0],
                                             ACT.Silu).then_inc(pair_act, 1)
                        act.wait_ge(in_free, item + 3)
                        nc.scalar.activation(g_act[:, 0, bass.ds(2 * i + t, 1), c0:c1], dve_tmp[:, t:t + 1, :c1 - c0],
                                             ACT.Copy).then_inc(g_hi, 1)
                        for q in ((0, 1), (2, 3))[x % 2] if x >= per - 2 else ():
                            split_hi(g + i + 1, q)

                if c == 0:
                    group(0, True)
                with act.Fori(1 if c == 0 else 0, count) as i:
                    group(i, False)

            def out_loop(st, g, count, item0):
                nh = st.nh
                with act.Fori(0, count) as i:
                    for q in range(NSLOT):
                        act.wait_ge(out_ready, item0 + 4 * nh * i + 4 * (nh - 1) + q + 1)
                        split_hi(g + i + 1, q)

            def rg(st, ph):
                kind, c, g, count, item0 = ph
                if kind == "in":
                    for i in range(count):
                        for x in range(4):
                            t, (c0, c1) = x % 2, st.halves[x // 2]
                            act.wait_ge(in_ready, item0 + 4 * i + x + 1)
                            tile, bank = 4 * i + 2 * t, pair_bank(st, x, i == 0)
                            nc.scalar.activation(rg_u[:, tile:tile + 2, c0:c1], ps[:, bank:bank + 2, :c1 - c0],
                                                 ACT.Copy).then_inc(pair_act, 1)
                            for q in ((0, 1), (2, 3))[t] if x >= 2 else ():
                                split_hi(g + i + 1, q)
                elif kind == "gates":
                    for m in range(KT):
                        if m >= 2:
                            act.wait_ge(m_lo, m - 1)
                        for d in range(2):
                            for k in range(2):
                                n = 4 * m + 2 * d + k
                                act.wait_ge(gate_ready, n + 1)
                                if n == 4:
                                    act.wait_ge(conv_step, CONV_STEPS * KT)
                                col = VEC["gate_b"] + (d * 2 + k) * KT + m
                                nc.scalar.activation(
                                    rg_work[m % 2][:, d, k].rearrange("p (h c) -> p h c", h=2),
                                    ps[:, 2 * (n % 3):2 * (n % 3) + 2, :TOK // 2], ACT.Sigmoid,
                                    bias=vecs[:, col:col + 1]).then_inc(sig_done, 1)
                        act.wait_ge(sig_done, 4 * m + 4)
                        for d in range(2):
                            w = rg_work[m % 2][:, d]
                            col = d * KT + m
                            nc.scalar.activation(w[:, 2], w[:, 0], ACT.Exp, scale=decay[:, 0, col:col + 1]).then_inc(expd, 1)
                        for d in range(2):
                            w = rg_work[m % 2][:, d]
                            col = d * KT + m
                            nc.scalar.activation(w[:, 0], w[:, 0], ACT.Tanh, scale=decay[:, 1, col:col + 1]).then_inc(expd, 1)
                        for d in range(2):
                            act.wait_ge(expd, 4 * m + 3 + d)
                            w = rg_work[m % 2][:, d]
                            nc.scalar.activation(w[:, 0], w[:, 0], ACT.Sqrt).then_inc(coef_done, 1)
                        if m % 2 == 0:
                            act.wait_ge(y_copied, m + 2)
                            nc.scalar.activation(rg_y[:, m:m + 2], rg_y[:, m:m + 2], ACT.Gelu_apprx_tanh).then_inc(y_gelu, 1)

            def mla(st, ph):
                kind, c, g, count, _ = ph
                if kind == "latent":
                    for q in range(NSLOT):
                        act.wait_ge(lat_ready, q + 4)
                        split_hi(g + 1, q)
                    sums = 0
                    norms = latent_norms()
                    for n, (src, gains, cols, size) in enumerate(norms):
                        for x in src:
                            sums += 1
                            act.wait_ge(lat_read, x[1])
                            wait_pos(act, lat_sum, sums - 2)
                            nc.scalar.activation(mla_sq[:, (sums - 1) % 2, :cols], x[0], ACT.Square).then_inc(lat_sq, 1)
                        if n == 0:
                            act.wait_ge(kr_step, 3)
                            act.wait_ge(lat_read, 6)
                            nc.scalar.activation(kr_n[:, 0], kr_raw[:], ACT.Copy).then_inc(lat_hi, 1)
                        if n == 2:
                            for q in range(NSLOT):
                                act.wait_ge(lat_ready, 8 + q)
                                split_hi(g + 2, q)
                        act.wait_ge(lat_sum, sums)
                        nc.scalar.activation(rstd[:, :cols], ps[:, 6, :cols], ACT.Ln, bias=eps_col[:],
                                             scale=1.0 / size).then_inc(lat_ln, 1)
                        act.wait_ge(lat_ln, n + 1)
                        nc.scalar.activation(rstd[:, :cols], rstd[:, :cols], ACT.Exp, scale=-0.5).then_inc(lat_rs, 1)
                        for k, x in enumerate(src):
                            act.wait_ge(lat_step, sums - len(src) + k + 1)
                            dst = latent_splits()[sums - len(src) + k][0]
                            nc.scalar.activation(dst[:, 0], x[0], ACT.Copy).then_inc(lat_hi, 1)
                    return
                with act.Fori(0, count) as i:
                    def project(n):
                        what, a, half = PROJ[n]
                        if what == "qr":
                            act.wait_ge(qr_step, 4 * i + 4)
                            nc.scalar.activation(qr_pair[:, 0], rot_tmp[:, 0], ACT.Copy).then_inc(prj_hi, 1)
                            return
                        width = {"q": LAT, "k": TOK // 2, "v": 2 * VD}[what]
                        act.wait_ge(prj_ready, len(PROJ) * i + n + 1)
                        nc.scalar.activation(proj_dst(what, a, half)[0], ps[:, PROJ_BANK[n], :width], ACT.Copy).then_inc(prj_hi, 1)

                    for n in range(FIRST_PROJ):
                        project(n)
                    for q in range(3):
                        split_hi(g + i + 1, q)
                    for what, u in PAIR:
                        if what == "P":
                            project(u)
                        elif what == "S":
                            act.wait_ge(t_ready, 8 * i + u + 1)
                            act.wait_ge(s_max, 16 * i + 2 * u + 2)
                            nc.scalar.activation(p_soft[:, u % 2].rearrange("p (b c) -> p b c", b=2),
                                                 ps[:, 2 * (u % 2):2 * (u % 2) + 2, :TOK // 2], ACT.Exp,
                                                 bias=soft_max[:, u % 2, 1:2], scale=SCALE,
                                                 accum_out=soft_max[:, u % 2, 2:3]).then_inc(s_exp, 1)
                            act.wait_ge(s_rcp, 8 * i + u + 1)
                            nc.scalar.activation(p_soft[:, u % 2], p_soft[:, u % 2], ACT.Copy,
                                                 scale=soft_max[:, u % 2, 3:4]).then_inc(p_ready, 1)
                        elif what == "T":
                            act.wait_ge(t_ready, 8 * i + u + 3)
                            src, dst = turned(u)
                            nc.scalar.activation(dst[0], src, ACT.Copy).then_inc(t_hi, 1)
                            if u == 0:
                                split_hi(g + i + 1, 3)
                        else:
                            act.wait_ge(o_ready, 2 * i + u + 1)
                            nc.scalar.activation(att_o[:, 0, bass.ds(2 * i + u, 1)], ps[:, turn_bank("V", u):turn_bank("V", u) + 1, :LAT],
                                                 ACT.Copy).then_inc(o_hi, 1)

            act.wait_ge(vec_in, 16)
            nc.scalar.activation(cond[:], vecs[:, VEC["cond"]:VEC["cond"] + 16], ACT.Silu).then_inc(cond_done, 1)
            act.wait_ge(soft_step, 1)
            nc.scalar.activation(soft[:, 1], soft[:, 0], ACT.Exp).then_inc(soft_exp, 1)
            act.wait_ge(consts, 2)
            tail_steps(TAILS[0])
            g_items = 0
            for n, st in enumerate(STAGES):
                if st.kind == "ffn":
                    wait_pos(act, ss_added, TAILS[n].end[0])
                for ph in phases(st):
                    kind, c, g, count, item0 = ph
                    if st.kind == "rg" and kind != "out":
                        rg(st, ph)
                    elif st.kind == "mla" and kind != "out":
                        mla(st, ph)
                    elif kind == "in":
                        ffn_in(st, c, g, count, item0, g_items)
                        g_items += 2 * st.nh * count
                    elif ph != last_out(st):
                        out_loop(st, g, count, item0)
                tail_steps(TAILS[n + 1])

        @block.vector
        def _(dve):
            v = nc.vector
            dve.sem_inc(in_free, 2)
            dve.sem_inc(out_free, 3)
            dve.sem_inc(g_free, 2)
            dve.sem_inc(modp_free, 2)
            dve.sem_inc(t_ready, 2)
            dve.sem_inc(s_exp, 2)
            dve.sem_inc(t_free, 1)
            dve.sem_inc(o_free, 1)
            soft_n = [0]

            def soft_link(ins):
                soft_n[0] += 1
                ins.then_inc(soft_step, 1)
                dve.wait_ge(soft_step, soft_n[0])

            def softplus():
                z, e, s, s2, acc = (soft[:, n] for n in range(5))
                lam = vecs[:, VEC["lam"]:VEC["lam"] + 16]
                v.tensor_scalar(acc, lam, -1.0, None, ALU.mult).then_inc(soft_exp, 1)
                dve.wait_ge(soft_exp, 1)
                soft_link(v.tensor_tensor(z, lam, acc, ALU.min))
                dve.wait_ge(soft_exp, 2)
                soft_link(v.tensor_scalar(s, e, 2.0, None, ALU.add))
                soft_link(v.reciprocal(s, s))
                soft_link(v.tensor_tensor(s, s, e, ALU.mult))
                soft_link(v.tensor_tensor(s2, s, s, ALU.mult))
                soft_link(v.tensor_scalar(e, s2, 1.0 / 15, 1.0 / 13, ALU.mult, ALU.add))
                for k in (11, 9, 7, 5, 3, 1):
                    soft_link(v.tensor_tensor(e, e, s2, ALU.mult))
                    soft_link(v.tensor_scalar(e, e, 1.0 / k, None, ALU.add))
                soft_link(v.tensor_tensor(e, e, s, ALU.mult))
                soft_link(v.tensor_scalar(acc, acc, 0.0, None, ALU.max))
                soft_link(v.scalar_tensor_tensor(e, e, 2.0, acc, ALU.mult, ALU.add))
                soft_link(v.tensor_scalar(decay[:, 0], e, -RG_C, None, ALU.mult))
                soft_link(v.tensor_scalar(decay[:, 1], e, RG_C / 2, None, ALU.mult))

            gains = [0]

            def gain_link(ins):
                gains[0] += 1
                ins.then_inc(gain_done, 1)

            def make_gains(tail):
                st = tail.stage
                if st is not None:
                    w = 0.5 if st.kind == "ffn" else 1.0
                    a, b = mod_at(st.layer, st.sub, 2), gain_at(st.layer, 2 * st.sub + 1)
                    for k in range(len(tail.halves)):
                        gain_link(v.scalar_tensor_tensor(post_gain[:, k], mods[:, k, a:a + KT], w, vecs[:, b:b + KT],
                                                         ALU.mult, ALU.mult))
                if tail.pre:
                    nx = STAGES[tail.n]
                    a, b = mod_at(nx.layer, nx.sub, 1), gain_at(nx.layer, 2 * nx.sub)
                    for k in range(len(tail.halves)):
                        gain_link(v.scalar_tensor_tensor(pre_gain[:, k], mods[:, k, a:a + KT], 1.0, vecs[:, b:b + KT],
                                                         ALU.add, ALU.mult))
                dve.wait_ge(gain_done, gains[0])

            def evict(item, dst, bank, n, first):
                dve.wait_ge(out_ready, item + 1)
                if first:
                    v.tensor_copy(dst, bank).then_inc(out_free, 1)
                else:
                    v.tensor_tensor(dst, bank, dst, ALU.add).then_inc(out_free, 1)

            def tail_steps(tail):
                st = tail.stage
                if st is not None:
                    make_gains(tail)
                for x in tail.order:
                    h = x[1]
                    c0, c1 = tail.halves[h]
                    n = c1 - c0
                    segs = segments(c0, c1)
                    pair = acc(st)[:, 2 * x[2]:2 * x[2] + 2, c0:c1] if x[0] in ("post", "norm", "pre") else None
                    scale = rstd[:, :n].unsqueeze(1).to_broadcast([P, 2, n])
                    if x[0] == "E":
                        item = out_item(st, x)
                        evict(item, acc(st)[:, x[2], c0:c1], ps[:, out_bank(st, item - last_out(st)[4]), :n], n,
                              st.kind != "ffn")
                        if carries_mods(st) and x == ("E", 0, 2):
                            mod_finish(st.mod0 - MOD_FIRST + 15, mod_conds(st, 2))
                            dve.wait_ge(mod_done, mods_before(st) + 1)
                    elif x[0] == "rs":
                        dve.wait_ge(rs_ready, tail.stat[x[2], h])
                        if x[2] == "pre" and st is None:
                            dve.wait_ge(x_in, 16)
                    elif x[0] == "post":
                        v.tensor_tensor(pair, pair, scale, ALU.mult).then_inc(y_normed, 1)
                        dve.wait_ge(y_normed, KP * tail.post[h] + x[2] + 1)
                        for m in (2 * x[2], 2 * x[2] + 1):
                            for k, a, b in segs:
                                ins = v.scalar_tensor_tensor(x_res[:, m, a:b], acc(st)[:, m, a:b],
                                                             post_gain[:, k, m:m + 1], x_res[:, m, a:b], ALU.mult, ALU.add)
                            ins.then_inc(x_upd, 1)
                    elif x[0] == "norm":
                        norm(x, pair, scale, c0, c1)
                    elif x[0] == "pre":
                        nx = STAGES[tail.n]
                        shift = mod_at(nx.layer, nx.sub, 0)
                        if st is not None:
                            norm(x, pair, scale, c0, c1)
                        elif x[1:] == (0, 0):
                            first_mods()
                            make_gains(tail)
                        dve.wait_ge(x_normed, KP * tail.pre_no[h] + x[2] + 1)
                        for m in (2 * x[2], 2 * x[2] + 1):
                            for k, a, b in segs:
                                part = acc(st)[:, m, a:b]
                                ins = v.tensor_scalar(part, part, pre_gain[:, k, m:m + 1],
                                                      mods[:, k, shift + m:shift + m + 1], ALU.mult, ALU.add)
                        ins.then_inc(h_f32, 1)
                        pres_done[0] = tail.pre_no[h] + 1

            def norm(x, pair, scale, c0, c1):
                v.tensor_tensor(pair, x_res[:, 2 * x[2]:2 * x[2] + 2, c0:c1], scale, ALU.mult).then_inc(x_normed, 1)

            def first_mods():
                dve.wait_ge(mod_sum0, 1)
                first = MOD_FIRST * MOD_W // P
                for c in range(2):
                    ins = v.tensor_tensor(mods[:, c, 0:first], ps[:, 6, c:2 * first:2],
                                          vecs[:, VEC["mod_b"]:VEC["mod_b"] + first], ALU.add)
                ins.then_inc(mod_done, 1)
                dve.wait_ge(mod_done, 1)

            def mod_part(j, chunk, step0, conds):
                for b in range(2):
                    dve.wait_ge(modp_in[b], 16 * (2 * chunk + j + 1))
                    for kk in range(2):
                        k = 4 * j + 2 * b + kk
                        for c in range(conds):
                            step = step0 + 8 * j + 4 * b + 2 * kk + c
                            if k == 0:
                                ins = v.tensor_scalar(mod_acc[:, c], mod_raw[:, b, kk], cond[:, 2 * k + c:2 * k + c + 1],
                                                      None, ALU.mult)
                            else:
                                dve.wait_ge(mod_step, step - conds + 1)
                                ins = v.scalar_tensor_tensor(mod_acc[:, c], mod_raw[:, b, kk],
                                                             cond[:, 2 * k + c:2 * k + c + 1], mod_acc[:, c],
                                                             ALU.mult, ALU.add)
                            ins.then_inc(mod_step, 2 // conds)
                    dve.wait_ge(mod_step, step + 2 // conds)
                    dve.sem_inc(modp_free, 1)

            def mod_finish(chunk, conds):
                dve.wait_ge(mod_sum, chunk + 1)
                per = MOD_W // P
                col = (MOD_FIRST + chunk) * per
                bias = vecs[:, bass.ds(VEC["mod_b"] + col, per)]
                for c in range(conds):
                    ins = v.tensor_tensor(mods[:, c, bass.ds(col, per)], ps[:, MODB, per * c:per * c + per], bias, ALU.add)
                ins.then_inc(mod_done, 1)

            def ffn_in(st, ph):
                kind, c, g, count, item0 = ph
                per = 2 * st.nh

                def group(i, peeled):
                    for x in range(per):
                        t, (c0, c1) = x % 2, st.halves[x // 2]
                        n = c1 - c0
                        item = item0 + per * i + x
                        gitem = g_total[0] + per * i + x
                        dve.wait_ge(pair_act, item + 1)
                        dve.wait_ge(g_free, gitem + 1)
                        v.tensor_tensor(dve_tmp[:, t, :n], ps[:, pair_bank(st, x, peeled and c == 0) + 1, :n], act_tmp[:, t, :n], ALU.mult).then_inc(in_free, 1)
                        if has_mods(st, ph):
                            chunk = mod_chunk0(st, ph) + 2 * i + x // 2
                            if x % 2 == 0 and not (peeled and x == 0):
                                mod_finish(chunk - 1, mod_conds(st, c))
                            mod_part(x % 2, chunk, 16 * chunk, mod_conds(st, c))

                peel = has_mods(st, ph) or c == 0
                if peel:
                    group(0, True)
                with dve.Fori(1 if peel else 0, count) as i:
                    group(i, False)
                g_total[0] += per * count

            def conv(tile):
                def col(name, k=0):
                    at = VEC[name] + k * KT + tile
                    return vecs[:, at:at + 1]

                src = rg_u[:, tile:tile + 1]
                dst = rg_uc[:, tile:tile + 1]
                step = CONV_STEPS * tile
                v.tensor_scalar(dst, src, col("conv_w", 2), col("conv_b"), ALU.mult, ALU.add).then_inc(conv_step, 1)
                n = 0
                for k in (1, 3, 0):
                    back = 2 - k
                    for a, b in ((0, CTX), (CTX, TOK)):
                        n += 1
                        lo, hi = (a + back, b) if back > 0 else (a, b + back)
                        dve.wait_ge(conv_step, step + n)
                        v.scalar_tensor_tensor(dst[:, :, lo:hi], src[:, :, lo - back:hi - back], col("conv_w", k),
                                               dst[:, :, lo:hi], ALU.mult, ALU.add).then_inc(conv_step, 1)

            def rg(st, ph):
                kind, c, g, count, item0 = ph

                def uc_split(m):
                    if m >= 2:
                        dve.wait_ge(gate_ready, 4 * (m - 1))
                    v.tensor_copy(rg_split[m % 2][:, 0], rg_uc[:, m]).then_inc(uc_hi, 1)

                if kind == "in":
                    for i in range(count):
                        for x in range(4):
                            dve.wait_ge(pair_act, item0 + 4 * i + x + 1)
                            dve.sem_inc(in_free, 1)
                            if x >= 2:
                                conv(4 * i + 2 * (x % 2))
                                conv(4 * i + 2 * (x % 2) + 1)
                        if i == 0:
                            dve.wait_ge(conv_step, CONV_STEPS)
                            uc_split(0)
                    return

                def y_copy(m):
                    dve.wait_ge(y_ready, m + 1)
                    v.tensor_copy(rg_y[:, m].rearrange("p (h c) -> p h c", h=2), ps[:, 6:8, :TOK // 2]).then_inc(y_copied, 1)

                dve.wait_ge(conv_step, CONV_STEPS * KT)
                uc_split(1)
                y_copy(0)
                y_copy(1)
                for m in range(KT):
                    w = rg_work[m % 2]
                    step = RG_STEPS * m

                    def link(ins, number):
                        ins.then_inc(rg_step, 1)
                        dve.wait_ge(rg_step, step + number)

                    if m + 2 < KT:
                        uc_split(m + 2)
                    for d in range(2):
                        s, b, a = w[:, d, 0], w[:, d, 1], w[:, d, 2]
                        dve.wait_ge(coef_done, 2 * m + d + 1)
                        link(v.scalar_tensor_tensor(s, a, 1.0, s, ALU.add, ALU.mult), 3 * d + 1)
                        dve.wait_ge(iu_done, 2 * m + d + 1)
                        link(v.tensor_tensor(b, s, b, ALU.mult), 3 * d + 2)
                        if d == 0:
                            link(v.tensor_tensor_scan(s, a, b, 0.0, ALU.mult, ALU.add), 3)
                        else:
                            link(v.tensor_tensor_scan(s[:, CTX - 1::-1], a[:, CTX - 1::-1], b[:, CTX - 1::-1], 0.0,
                                                      ALU.mult, ALU.add), 6)
                            link(v.tensor_tensor_scan(s[:, TOK - 1:CTX - 1:-1], a[:, TOK - 1:CTX - 1:-1],
                                                      b[:, TOK - 1:CTX - 1:-1], s[:, 0:1], ALU.mult, ALU.add), 7)
                    link(v.tensor_tensor(w[:, 0, 0], w[:, 0, 0], w[:, 1, 0], ALU.add), 8)
                    dve.wait_ge(y_gelu, m // 2 + 1)
                    link(v.tensor_tensor(w[:, 0, 0], w[:, 0, 0], rg_y[:, m], ALU.mult), 9)
                    v.tensor_copy(rg_m[0][:, m], w[:, 0, 0]).then_inc(m_hi, 1)
                    for p in RG_SPLITS.get(m, ()):
                        if p < 4 + len(RG_UNITS):
                            what, n = RG_UNITS[p - 4]
                            dve.wait_ge(y_ready if what == "y" else gate_ready, n + 1 if what == "y" else 8 * n + 8)
                        dve.wait_ge(w_hi, rg_unit_ordinal(g, p))
                        dve.wait_ge(raw_in[p % NSLOT], 16 * (g + p // NSLOT + 1))
                        v.tensor_copy(w_slot[:, p % NSLOT, 0], raw[:, p % NSLOT]).then_inc(w_hi, 1)
                    if m + 2 < KT:
                        y_copy(m + 2)

            def mla(st, ph):
                kind, c, g, count, _ = ph
                if kind == "latent":
                    places = []
                    for h in range(2):
                        c0, c1 = HALVES[h]
                        places += [ckv_raw[:, 0, c0:c1], ckv_raw[:, 1, c0:c1], kr_raw[:, c0:c1]]
                    places += [kr_swap[:]] + [cq_raw[:, t] for t in range(4)]

                    def apply_norm(which):
                        src, col, cols, size = latent_norms()[which]
                        dve.wait_ge(lat_rs, which + 1)
                        for k, x in enumerate(src):
                            v.scalar_tensor_tensor(x[0], x[0], vecs[:, col + k:col + k + 1], rstd[:, :cols],
                                                   ALU.mult, ALU.mult).then_inc(lat_step, 1)

                    for n, dst in enumerate(places):
                        dve.wait_ge(lat_ready, n + 1)
                        v.tensor_copy(dst, ps[:, n % 4, :dst.shape[-1]]).then_inc(lat_read, 1)
                        if n == 6:
                            dve.wait_ge(rope_in, 48)
                            dve.wait_ge(lat_read, 7)
                            v.tensor_tensor(rot_tmp[:, 0], kr_raw[:, CTX:], cos_t[:], ALU.mult).then_inc(kr_step, 1)
                            v.tensor_tensor(rot_tmp[:, 1], kr_swap[:], sin_t[:], ALU.mult).then_inc(kr_step, 1)
                            dve.wait_ge(kr_step, 2)
                            v.tensor_tensor(kr_raw[:, CTX:], rot_tmp[:, 0], rot_tmp[:, 1], ALU.add).then_inc(kr_step, 1)
                        if n >= 8:
                            apply_norm(n - 8)
                    for n, (dst, src) in enumerate(latent_splits()[4:]):
                        dve.wait_ge(lat_hi, 6 + n)
                        v.tensor_tensor(dst[:, 1], src, dst[:, 0].bitcast(F32), ALU.subtract).then_inc(cq_lo, 1)
                    return
                with dve.Fori(0, count) as i:
                    def project(n):
                        what, a, half = PROJ[n]
                        if what == "qr":
                            dve.wait_ge(prj_ready, len(PROJ) * i + n + 1)
                            v.tensor_tensor(rot_tmp[:, 0], ps[:, 0, :LAT], cos_t[:], ALU.mult).then_inc(qr_step, 1)
                            v.stream_shuffle(rot_tmp[:, 1], ps[:, 0, :LAT], [(k + 16) % 32 for k in range(32)]).then_inc(qr_step, 1)
                            dve.wait_ge(qr_step, 4 * i + 2)
                            v.tensor_tensor(rot_tmp[:, 1], rot_tmp[:, 1], sin_t[:], ALU.mult).then_inc(qr_step, 1)
                            dve.wait_ge(qr_step, 4 * i + 3)
                            v.tensor_tensor(rot_tmp[:, 0], rot_tmp[:, 0], rot_tmp[:, 1], ALU.add).then_inc(qr_step, 1)
                            dve.wait_ge(prj_hi, len(PROJ) * i + n + 1)
                            v.tensor_tensor(qr_pair[:, 1], rot_tmp[:, 0], qr_pair[:, 0].bitcast(F32),
                                            ALU.subtract).then_inc(prj_free, 1)
                            return
                        width = {"q": LAT, "k": TOK // 2, "v": 2 * VD}[what]
                        hi, lo = proj_dst(what, a, half)
                        dve.wait_ge(prj_hi, len(PROJ) * i + n + 1)
                        v.tensor_tensor(lo, ps[:, PROJ_BANK[n], :width], hi.bitcast(F32), ALU.subtract).then_inc(prj_free, 1)

                    for n in range(FIRST_PROJ):
                        project(n)

                    def turned_lo(u):
                        src, dst = turned(u)
                        dve.wait_ge(t_hi, 8 * i + u + 1)
                        v.tensor_tensor(dst[1], src, dst[0].bitcast(F32), ALU.subtract).then_inc(t_free, 1)

                    for what, u in PAIR:
                        if what == "P":
                            project(u)
                        elif what == "S":
                            dve.wait_ge(s_ready, 8 * i + u + 1)
                            v.tensor_reduce(soft_max[:, u % 2, 0:1], ps[:, 2 * (u % 2):2 * (u % 2) + 2, :TOK // 2],
                                            AX.XY, ALU.max).then_inc(s_max, 1)
                            dve.wait_ge(s_max, 16 * i + 2 * u + 1)
                            v.tensor_scalar(soft_max[:, u % 2, 1:2], soft_max[:, u % 2, 0:1], -SCALE, None,
                                            ALU.mult).then_inc(s_max, 1)
                            if u >= 2:
                                turned_lo(u - 2)
                            dve.wait_ge(s_exp, 8 * i + u + 3)
                            v.reciprocal(soft_max[:, u % 2, 3:4], soft_max[:, u % 2, 2:3]).then_inc(s_rcp, 1)
                        elif what == "T":
                            if u >= 2 * QT - 2:
                                turned_lo(u)
                        else:
                            dve.wait_ge(o_hi, 2 * i + u + 1)
                            place = att_o[:, :, bass.ds(2 * i + u, 1)]
                            v.tensor_tensor(place[:, 1], ps[:, turn_bank("V", u):turn_bank("V", u) + 1, :LAT], place[:, 0].bitcast(F32),
                                            ALU.subtract).then_inc(o_free, 1)

            dve.wait_ge(vec_in, 16)
            softplus()
            g_total, pres_done = [0], [0]
            tail_steps(TAILS[0])
            for n, st in enumerate(STAGES):
                for ph in phases(st):
                    kind, c, g, count, item0 = ph
                    if st.kind == "rg" and kind != "out":
                        rg(st, ph)
                    elif st.kind == "mla" and kind != "out":
                        mla(st, ph)
                    elif kind == "in":
                        ffn_in(st, ph)
                    elif ph != last_out(st):
                        nh = st.nh
                        if c == 0:
                            dve.wait_ge(h_lo, KP * pres_done[0])
                        with dve.Fori(0, count) as i:
                            for x in range(4 * nh):
                                h, q = x // 4, x % 4
                                c0, c1 = st.halves[h]
                                evict(item0 + 4 * nh * i + x, y_acc[:, bass.ds(4 * i + q, 1), c0:c1],
                                      ps[:, BANKS[nh][x]:BANKS[nh][x] + 1, :c1 - c0], c1 - c0, c == 0)
                        if has_mods(st, ("in", c)):
                            mod_finish(mod_chunk0(st, ph) + 7, mod_conds(st, c))
                if carries_mods(st):
                    dve.wait_ge(mod_done, mods_before(st))
                tail_steps(TAILS[n + 1])

        @block.tensor
        def _(pe):
            mm = nc.tensor.matmul

            def product(out, w, x, blocks, start=True, stop=True, before=None):
                for k in range(blocks):
                    if before and k % 2 == 0:
                        before(k)
                    for n, (a, b) in enumerate(((0, 0), (0, 1), (1, 0))):
                        last = mm(out, w(a, k), x(b, k), start=start and k == 0 and n == 0,
                                  stop=stop and k == blocks - 1 and n == 2)
                return last

            def slot(q, first=0, width=P):
                return lambda a, k: w_slot[:, q, a, first + k]

            def stat(tail, which, h):
                c0, c1 = tail.halves[h]
                wait_pos(pe, ln_done, tail.stat[which, h] - 1)
                pe.wait_ge(ss_added, tail.sums[which, h])
                mm(ps[:, STAT, :c1 - c0], ones[:], sum_sq[:, c0:c1], start=True, stop=True).then_inc(stat_ready, 1)

            def direct_sums(tail, m0, m1):
                wait_pos(pe, ln_done, tail.stat["pre", 0] - 1)
                for m in range(m0, m1):
                    pe.wait_ge(xsq_done, tail.sums["pre", 0] - KT + m + 1)
                    last = mm(ps[:, STAT, :TOK // 2], ones[:], x_sq[:, m], start=m == 0, stop=m == KT - 1)
                if m1 == KT:
                    last.then_inc(stat_ready, 1)

            def input_ready(tail, h, k=KT - 1):
                pe.wait_ge(h_lo, KP * tail.pre_no[h] + k // 2 + 1)

            def pair_item(st, x, item, first_unit, bank, before=None, between=None):
                t, (c0, c1) = x % 2, st.halves[x // 2]
                for b in range(2):
                    pe.wait_ge(w_lo, first_unit + 2 * t + b + 1)
                    if b == 0 and bank == 4:
                        wait_pos(pe, out_free, 3 + st.out0 if st.out0 else 0)
                    elif b == 0:
                        pe.wait_ge(in_free, item + 1)
                    if b == 1 and between:
                        between()
                    last = product(ps[:, bank + b, :c1 - c0], slot(2 * t + b), lambda a, k: h_in[:, a, k, c0:c1], KT,
                                   before=before if b == 0 else None)
                last.then_inc(in_ready, 1)

            def mod_sums(chunk, conds):
                pe.wait_ge(mod_step, 16 * chunk + 16)
                for c in range(conds):
                    for j in range(MOD_W // P):
                        last = mm(ps[:, MODB, 4 * c + j:4 * c + j + 1], mod_acc[:, c, j * P:(j + 1) * P], ones[:, 0:1],
                                  start=True, stop=True)
                last.then_inc(mod_sum, 1)

            def in_phase(n, st, ph):
                kind, c, g, count, item0 = ph
                per = 2 * st.nh
                tail = TAILS[n]

                def group(i, peeled):
                    for x in range(per):
                        first_use, two = peeled and c == 0 and x in (0, 2), len(tail.halves) == 2

                        def before(k):
                            if k == 4 and x == 0 and two and tail.stage:
                                stat(tail, "post", 1)
                            input_ready(tail, x // 2 if two else 0, k)

                        late = peeled and c == 0 and x == 1 and two and tail.stage
                        pair_item(st, x, item0 + per * i + x, (g + i) * NSLOT, pair_bank(st, x, peeled and c == 0),
                                  before=before if first_use else None,
                                  between=(lambda: stat(tail, "pre", 1)) if late else None)
                        if has_mods(st, ph) and x % 2 == 0 and not (peeled and x == 0):
                            if peeled and c == 1:
                                pe.wait_ge(ln_done, tail.end[1])
                            mod_sums(mod_chunk0(st, ph) + 2 * i + x // 2 - 1, mod_conds(st, c))

                start = 0
                if c == 0 or has_mods(st, ph):
                    group(0, True)
                    start = 1
                with pe.Fori(start, count) as i:
                    group(i, False)

            def out_item_products(st, h, q, x, item, unit, blocks, src, before=None):
                c0, c1 = st.halves[h]
                pe.wait_ge(w_lo, unit + 1)
                place = x % len(BANKS[st.nh])
                pe.wait_ge(out_free, 3 + item - BACK[st.nh][place] + 1)
                product(ps[:, BANKS[st.nh][place], :c1 - c0], slot(q), lambda a, k: src(a, k, c0, c1), blocks,
                        before=before).then_inc(out_ready, 1)

            def out_phase(n, st, ph):
                kind, c, g, count, item0 = ph
                nh = st.nh
                tail = TAILS[n + 1]
                final = ph == last_out(st)
                if st.kind == "ffn":
                    blocks, src = CHUNKS[c], lambda a, k, c0, c1: g_act[:, a, k, c0:c1]
                    done = g_total[0]
                    pe.wait_ge(g_free, 2 + done - 2)

                    def split_yet(k):
                        pe.wait_ge(g_free, 2 + done - blocks + min(k + 2, blocks))
                elif st.kind == "rg":
                    blocks, src = KT, lambda a, k, c0, c1: rg_m[a][:, k, c0:c1]
                    pe.wait_ge(sig_done, 4 * KT)
                    pe.wait_ge(y_copied, KT)
                else:
                    blocks, src = KT, lambda a, k, c0, c1: att_o[:, a, k, :]
                    pe.wait_ge(o_free, 1 + HEADS)

                def item(h, q, j, unit, before=None):
                    out_item_products(st, h, q, j, item0 + j, unit, blocks, src, before=before)

                def rg_first_items():
                    c0, c1 = HALVES[0]
                    for part in (range(KT - 1), range(KT - 1, KT)):
                        pe.wait_ge(m_lo, part[-1] + 1)
                        for j in range(3):
                            pe.wait_ge(w_lo, g * NSLOT + j + 1)
                            if not j and not part[0]:
                                pe.wait_ge(out_free, 3 + item0)
                            last = product(ps[:, out_bank(st, j), :c1 - c0], lambda a, k: w_slot[:, j, a, part[0] + k],
                                           lambda a, k: src(a, part[0] + k, c0, c1), len(part), start=part[0] == 0,
                                           stop=part[-1] == KT - 1)
                            if part[-1] == KT - 1:
                                last.then_inc(out_ready, 1)

                if final and nh == 2:
                    for j, (h, m) in enumerate(FINAL):
                        if st.kind == "ffn" and j == KT:
                            pe.wait_ge(g_free, 2 + done)
                        if st.kind == "rg" and j < 3:
                            if j == 0:
                                rg_first_items()
                            continue
                        item(h, m % 4, j, (g + (0, 1, 1, 2)[j // 4]) * NSLOT + m % 4)
                        if carries_mods(st) and j == 1:
                            mod_sums(st.mod0 - MOD_FIRST + 15, mod_conds(st, 2))
                        if j == KT:
                            if carries_mods(st):
                                pe.wait_ge(mod_done, mods_before(st) + 1)
                            stat(tail, "post", 0)
                        if j == KT + 3 and tail.pre:
                            direct_sums(tail, 0, KP)
                        if j == KT + 4 and tail.pre:
                            direct_sums(tail, KP, KT)
                    if not tail.pre:
                        stat(tail, "post", 1)
                elif final:
                    for m in range(KT):
                        item(0, m % 4, m, g * NSLOT + m, before=split_yet if st.kind == "ffn" and m == 0 else None)
                    stat(tail, "post", 0)
                    if tail.pre:
                        stat(tail, "pre", 0)
                else:
                    with pe.Fori(0, count) as i:
                        for x in range(4 * nh):
                            h, q = x // 4, x % 4
                            if st.kind == "ffn" and nh == 2 and x == 4:
                                pe.wait_ge(g_free, 2 + done)
                            out_item_products(st, h, q, x, item0 + 4 * nh * i + x, (g + i) * NSLOT + q, blocks, src,
                                              before=split_yet if nh == 1 and x == 0 else None)
                    if has_mods(st, ("in", c)):
                        mod_sums(mod_chunk0(st, ph) + 7, mod_conds(st, c))

            def gates(n, st, ph):
                kind, c, g, count, _ = ph

                def unit(what, number):
                    p = RG_UNITS.index((what, number))
                    pe.wait_ge(w_lo, rg_unit_ordinal(g, p) + 1)
                    return p % NSLOT

                def y_tile(m):
                    q = unit("y", m)
                    if m:
                        pe.wait_ge(y_copied, m)
                    for h, (c0, c1) in enumerate(HALVES):
                        last = product(ps[:, 6 + h, :c1 - c0], slot(q), lambda a, k: h_in[:, a, k, c0:c1], KT)
                    last.then_inc(y_ready, 1)

                pe.wait_ge(out_free, 3 + st.out0)
                pe.wait_ge(ln_done, TAILS[n].end[1])
                y_tile(0)
                pe.wait_ge(in_free, 2 + st.in0 + KT // 2 * st.nh)
                for m in range(KT):
                    q = unit("gate", m // 2)
                    pe.wait_ge(uc_lo, m + 1)
                    for d in range(2):
                        for k in range(2):
                            item = 4 * m + 2 * d + k
                            if item >= 3:
                                pe.wait_ge(sig_done, item - 2)
                            for h, (c0, c1) in enumerate(HALVES):
                                last = product(ps[:, 2 * (item % 3) + h, :c1 - c0],
                                               lambda a, b: w_slot[:, q, a, 4 * (m % 2) + 2 * d + k],
                                               lambda a, b: rg_split[m % 2][:, a, c0:c1], 1)
                            last.then_inc(gate_ready, 1)
                    if m + 1 < KT:
                        y_tile(m + 1)

            def latents(n, ph):
                kind, c, g, count, _ = ph
                tail = TAILS[n]
                items = [(q, h) for h in range(2) for q in range(3)] + [(3, None)] + [(q, None) for q in range(4)]
                sums = [0]

                def norm_sums(which):
                    src, _, cols, _ = latent_norms()[which]
                    if which:
                        pe.wait_ge(lat_ln, which)
                    for k in range(len(src)):
                        sums[0] += 1
                        pe.wait_ge(lat_sq, sums[0])
                        mm(ps[:, 6, :cols], ones[:], mla_sq[:, (sums[0] - 1) % 2, :cols], start=k == 0,
                           stop=k == len(src) - 1).then_inc(lat_sum, 1)

                for i, (q, h) in enumerate(items):
                    c0, c1 = HALVES[h] if h is not None else (CTX, TOK)
                    unit = g * NSLOT + q if i < 7 else (g + 1) * NSLOT + q
                    pe.wait_ge(w_lo, unit + 1)
                    wait_pos(pe, lat_read, i - 3)
                    product(ps[:, i % 4, :c1 - c0], slot(q), lambda a, k: h_in[:, a, k, c0:c1], KT,
                            before=(lambda k: input_ready(tail, h, k)) if i in (0, 3) else None).then_inc(lat_ready, 1)
                    if i == 0:
                        stat(tail, "post", 1)
                    if i == 2:
                        stat(tail, "pre", 1)
                    if i == 6:
                        norm_sums(0)
                    if i == 9:
                        norm_sums(1)
                norm_sums(2)

            def heads(ph):
                kind, c, g, count, _ = ph
                pe.wait_ge(lat_lo, 5)
                with pe.Fori(0, count) as i:
                    pe.wait_ge(s_exp, 8 * i + 2)
                    def project(n):
                        what, a, half = PROJ[n]
                        q = {"qr": 0, "q": 1 + a, "k": 1 + a, "v": 3}[what]
                        pe.wait_ge(w_lo, (g + i) * NSLOT + q + 1)
                        if PROJ_BANK[n] in PROJ_BANK[:n]:
                            pe.wait_ge(prj_free, len(PROJ) * i + PROJ_BANK.index(PROJ_BANK[n]) + 1)
                        if n == PROJ.index(("v", 0, 0)):
                            pe.wait_ge(o_free, 1 + 2 * i)
                            pe.wait_ge(t_free, 1 + 8 * i)
                        bank = PROJ_BANK[n]
                        if what == "qr":
                            pe.wait_ge(cq_lo, 4)
                        if what in ("qr", "q"):
                            last = product(ps[:, bank, :LAT], slot(q), lambda b, k: cq_n[:, b, k], QL // P)
                        elif what == "k":
                            c0, c1 = HALVES[half]
                            last = product(ps[:, bank, :c1 - c0], slot(q, QL // P), lambda b, k: ckv_n[:, b, k, c0:c1], KVL // P)
                        else:
                            last = product(ps[:, bank, :2 * VD], lambda b, k: ckv_n[:, b, k, a * P:(a + 1) * P],
                                           lambda b, k: w_slot[:, 3, b, 2 * k:2 * k + 2].rearrange("p k c -> p (k c)"),
                                           KVL // P)
                        last.then_inc(prj_ready, 1)

                    for n in range(FIRST_PROJ):
                        project(n)
                    pe.wait_ge(prj_free, len(PROJ) * i + QK_PROJ)
                    for what, u in PAIR_PE:
                        hd, cols = u // QT, slice((u % QT) * P, (u % QT + 1) * P)
                        if what == "P":
                            project(u)
                        elif what == "S":
                            pe.wait_ge(s_exp, 8 * i + u + 1)
                            for h, (c0, c1) in enumerate(HALVES):
                                bank = ps[:, 2 * (u % 2) + h, :c1 - c0]
                                product(bank, lambda a, k: q_head[hd][a][:, cols], lambda a, k: k_head[hd][:, a, c0:c1], 1,
                                        stop=False)
                                r0 = ROPE * hd
                                last = product(bank, lambda a, k: qr_pair[r0:r0 + ROPE, a, cols],
                                               lambda a, k: kr_n[r0:r0 + ROPE, a, c0:c1], 1, start=False)
                            last.then_inc(s_ready, 1)
                        elif what == "T":
                            pe.wait_ge(p_ready, 8 * i + u + 1)
                            if u == 0:
                                pe.wait_ge(prj_free, len(PROJ) * (i + 1))
                            if u in (1, QT + 1):
                                pe.wait_ge(o_free, 2 * i + 1 + (u > QT))
                            else:
                                pe.wait_ge(t_free, 1 + 8 * i + (u if u == QT else max(u - 1, 0)))
                            for t in range(CKT):
                                last = nc.tensor.transpose(ps[:, turn_bank("T", u) + t // 3, (t % 3) * P:(t % 3 + 1) * P],
                                                           p_soft[:, u % 2, t * P:(t + 1) * P], ident[:])
                            last.then_inc(t_ready, 1)
                        else:
                            pe.wait_ge(t_free, 1 + 8 * i + 4 * u + 4)
                            product(ps[:, turn_bank("V", u), :LAT], lambda a, k: v_pair[:, a, k, u * VD:(u + 1) * VD],
                                    lambda a, k: p_turned[:, a, k], CKT).then_inc(o_ready, 1)

            pe.wait_ge(cond_done, 1)
            pe.wait_ge(consts, 2)
            for c in range(MOD_FIRST):
                for k in range(KT):
                    if k in (0, KP):
                        pe.wait_ge(mod0_in[2 * c + k // KP], 16)
                    last = mm(ps[0:2, c, :MOD_W], cond[:, 2 * k:2 * k + 2], mod_first[c][:, k], start=k == 0, stop=k == KT - 1)
                last.then_inc(row_ready, 1)
                if c in (1, 2):
                    stat(TAILS[0], "pre", c - 1)
            for c in range(MOD_FIRST):
                pe.wait_ge(row_copied, c + 1)
                for j in range(MOD_W // P):
                    col = 2 * (4 * c + j)
                    last = mm(ps[:, 6, col:col + 2], mod_row[0:2, c, j * P:(j + 1) * P],
                              vecs[0:2, VEC["pick"]:VEC["pick"] + 2], start=True, stop=True)
            last.then_inc(mod_sum0, 1)
            g_total = [0]
            for n, st in enumerate(STAGES):
                for ph in phases(st):
                    kind = ph[0]
                    if kind == "in":
                        in_phase(n, st, ph)
                        if st.kind == "ffn":
                            g_total[0] += 2 * st.nh * ph[3]
                    elif kind == "out":
                        out_phase(n, st, ph)
                    elif kind == "gates":
                        gates(n, st, ph)
                    elif kind == "latent":
                        latents(n, ph)
                    else:
                        heads(ph)


def rope_tables():
    grid_w, base, quarter = 64, 10000.0, ROPE // 4
    inv_freq = np.float32(base) ** (-np.arange(quarter, dtype=np.float32) / np.float32(quarter))
    t = np.arange(LAT)
    pos = np.stack([t // grid_w, t % grid_w]).astype(np.float32)
    r = np.arange(P) % ROPE
    angle = pos[r // (2 * quarter)] * inv_freq[r % quarter][:, None]
    sign = np.where(r % (2 * quarter) < quarter, -1.0, 1.0)[:, None]
    return np.cos(angle).astype(np.float32), (np.sin(angle) * sign).astype(np.float32)


def kernel(**inputs):
    import numpy as _np
    import concourse.bacc as _bacc
    from concourse import mybir as _mybir
    from concourse.bass_utils import run_bass_kernel_spmd as _run

    a = {k: _np.asarray(v) for k, v in inputs.items()}

    def unit_blocks(w):
        r, c = w.shape
        return w.reshape(r // P, P, c // P, P).transpose(2, 1, 0, 3)

    def units_of(w, at, dst):
        u = unit_blocks(w)
        dst[at:at + u.shape[0], :, :u.shape[2]] = u

    units = _np.zeros((GROUPS * NSLOT, P, KT, P), _np.float32)
    def again(n):
        units[n:n + NSLOT] = units[n - KT:n - KT + NSLOT]

    for st in STAGES:
        n = st.group0 * NSLOT
        l, s = "l%d_" % st.layer, st.sub // 2
        if st.kind == "ffn":
            w_in, w_out = a[l + "ffn_w_in"][s], a[l + "ffn_w_out"][s]
            t0 = 0
            for tiles in CHUNKS:
                rows = slice(t0 * P, (t0 + tiles) * P)
                units[n:n + 2 * tiles:2] = unit_blocks(w_in[:, :DFF][:, rows])
                units[n + 1:n + 2 * tiles:2] = unit_blocks(w_in[:, DFF:][:, rows])
                n += 2 * tiles
                units_of(w_out[rows], n, units)
                n += KT
                t0 += tiles
            if st.nh == 2:
                again(n)
        elif st.kind == "rg":
            w_in = a[l + "rg_w_in"]
            units_of(w_in[:, D:], n, units)
            n += KT
            y_units = unit_blocks(w_in[:, :D])
            gw = a[l + "rg_gate_w"]
            gate_units = gw.transpose(2, 3, 0, 1, 4).reshape(NSLOT, 2, P, 4, P).transpose(0, 2, 1, 3, 4).reshape(
                NSLOT, P, KT, P)
            for what, number in RG_UNITS:
                units[n] = (y_units if what == "y" else gate_units)[number]
                n += 1
            units_of(a[l + "rg_w_out"], n, units)
            again(n + KT)
        else:
            w_a, w_qb, w_kvb = a[l + "mla_w_a"], a[l + "mla_w_qb"], a[l + "mla_w_kvb"]
            rope = w_a[:, QL + KVL:]
            swap = rope.reshape(D, 2, 2, ROPE // 4)[:, :, ::-1].reshape(D, ROPE)
            units_of(_np.concatenate([w_a[:, QL:QL + KVL], rope, rope, swap, swap, w_a[:, :QL]], 1), n, units)
            n += 2 * NSLOT
            wq = w_qb.reshape(QL, HEADS, QKD)
            wkv = w_kvb.reshape(KVL, HEADS, NOPE + VD)
            for p in range(HEADS // 2):
                units_of(wq[:, 2 * p:2 * p + 2, NOPE:].reshape(QL, 2 * ROPE), n, units)
                for h in range(2):
                    units[n + 1 + h, :, :4] = unit_blocks(wq[:, 2 * p + h, :NOPE])[0]
                    units[n + 1 + h, :, 4:6] = unit_blocks(wkv[:, 2 * p + h, :NOPE])[0]
                v = wkv[:, 2 * p:2 * p + 2, NOPE:].reshape(2, P, 2, VD)
                units[n + 3, :, :4] = v.transpose(1, 0, 2, 3).reshape(P, 4, VD)
                n += NSLOT
            units_of(a[l + "mla_w_o"], n, units)

    def mod_blocks(w):
        return w.reshape(KT, P, -1, MOD_W).transpose(2, 1, 0, 3)

    modw = _np.concatenate([mod_blocks(a["l0_mod_w"]), mod_blocks(a["l1_mod_w"])], 0)
    mod_start = _np.ascontiguousarray(modw[:MOD_FIRST])
    pieces = modw[MOD_FIRST:].reshape(-1, P, 4, 2, MOD_W).transpose(0, 2, 1, 3, 4).reshape(-1, P, 2, MOD_W)

    def cols(v):
        return _np.asarray(v).reshape(-1, P).T

    cond = _np.stack([cols(a["c"]), cols(a["c_ctx"])], 2).reshape(P, 2 * KT)
    vecs = _np.concatenate([cond, cols(a["l0_norm_g"]), cols(a["l1_norm_g"]), cols(a["l0_mod_b"]), cols(a["l1_mod_b"]),
                            cols(a["l0_rg_conv_w"]), cols(a["l0_rg_conv_b"]), cols(a["l0_rg_gate_b"]),
                            cols(a["l0_rg_lambda"]), cols(a["l1_mla_q_norm"]), cols(a["l1_mla_kv_norm"]),
                            _np.eye(P, 2, dtype=_np.float32)], 1)
    tokens = _np.concatenate([a["ctx"][0], a["x"][0]], 0)
    x_t = tokens.T.reshape(KT, P, TOK).transpose(1, 0, 2)
    cos, sin = rope_tables()

    nc = _bacc.Bacc("TRN2", target_bir_lowering=False, num_devices=1, dynamic_dma_scratch_size=1024)
    arrays = {}

    def dram(name, value):
        arrays[name] = _np.ascontiguousarray(value)
        return nc.dram_tensor(name, arrays[name].shape, _mybir.dt.float32, kind="ExternalInput").ap()

    out_tok = TOK if STAGES[-1].nh == 2 else LAT
    out_d = nc.dram_tensor("out_t", (KT, P, out_tok), _mybir.dt.float32, kind="ExternalOutput").ap()
    io = (dram("units", units), dram("mod_pieces", pieces), dram("mod_start", mod_start), dram("x_t", x_t),
          dram("vecs_in", vecs), [dram("cos_in", cos), dram("sin_in", sin), dram("ident_in", _np.eye(P, dtype=_np.float32))],
          out_d)
    build(nc, io)
    got = _run(nc, [arrays], core_ids=[0]).results[0]["out_t"]
    return _np.ascontiguousarray(got.reshape(D, out_tok).T[None])
```
